# Optimizing a Trainium2 kernel written in Bass

```python
import jax, jax.numpy as jnp
from jax import lax
import numpy as np
import math

D_MODEL = 1024
BATCH = 1
SEQ = 256
DEPTH = 2

CHUNK = 64
PLE_DIM = 256
N_A = DEPTH // 2
N_B = DEPTH - N_A
POOL_WINDOWS = (2, 4, 8, 16)
N_POOL_GROUPS = len(POOL_WINDOWS)
POOL_GROUP_DIM = D_MODEL // N_POOL_GROUPS
POOL_WMAX = max(POOL_WINDOWS)
SB_HEADS = 16
SB_HEAD_DIM = D_MODEL // SB_HEADS
SB_SCALE = SB_HEAD_DIM ** -0.5
Q_BLOCK = 128
EPS = 1e-6


def rms_norm(x, g):
    xf = x.astype(jnp.float32)
    y = xf * lax.rsqrt(jnp.mean(xf * xf, axis=-1, keepdims=True) + EPS)
    return (y * g.astype(jnp.float32)).astype(x.dtype)

def pool_mixer(h, w_in, w_group, scale, w_out):
    B, S, _ = h.shape
    u, z = jnp.split(h @ w_in, 2, axis=-1)
    u = u.reshape(B, S, N_POOL_GROUPS, POOL_GROUP_DIM)
    uf = u.astype(jnp.float32)
    cs = jnp.cumsum(uf, axis=1)
    cs_ext = jnp.pad(cs, ((0, 0), (POOL_WMAX, 0), (0, 0), (0, 0)))
    pos1 = jnp.arange(1, S + 1)
    means = []
    for g, w in enumerate(POOL_WINDOWS):
        lo = cs_ext[:, POOL_WMAX - w: POOL_WMAX - w + S, g]
        cnt = jnp.minimum(pos1, w).astype(jnp.float32)[None, :, None]
        means.append((cs[:, :, g] - lo) / cnt)
    pooled = (jnp.stack(means, axis=2) - uf).astype(h.dtype)
    mixed = jnp.einsum('bsgc,gcd->bsgd', pooled, w_group).reshape(B, S, D_MODEL) * scale
    return (mixed * jax.nn.silu(z)) @ w_out

def split_heads(t):
    B, S, _ = t.shape
    return t.reshape(B, S, SB_HEADS, SB_HEAD_DIM).transpose(0, 2, 1, 3)

def stick_breaking_attention(q, k, v):
    S = q.shape[2]
    outs = []
    for blk in range(S // Q_BLOCK):
        t0 = blk * Q_BLOCK
        L = t0 + Q_BLOCK
        logits = jnp.einsum('bhtd,bhsd->bhts', q[:, :, t0:L], k[:, :, :L]).astype(jnp.float32) * SB_SCALE
        t_idx = t0 + jnp.arange(Q_BLOCK)[:, None]
        s_idx = jnp.arange(L)[None, :]
        mask = s_idx < t_idx
        log_keep = jnp.where(mask, jax.nn.log_sigmoid(-logits), 0.0)
        later = lax.cumsum(log_keep, axis=log_keep.ndim - 1, reverse=True) - log_keep
        log_a = jax.nn.log_sigmoid(logits) + later
        a = jnp.where(mask, jnp.exp(log_a), 0.0)
        outs.append(jnp.einsum('bhts,bhsd->bhtd', a.astype(v.dtype), v[:, :, :L]))
    return jnp.concatenate(outs, axis=2)

def first_inputs(seed: int = 0) -> dict:
    key = jax.random.key(seed)
    ks = jax.random.split(key, 20)
    D, C = D_MODEL, POOL_GROUP_DIM
    f32 = jnp.float32

    def nrm(k, shape, fan_in, gain=1.0):
        return jax.random.normal(k, shape, f32) * (gain * fan_in ** -0.5)

    def gain(k, shape):
        return 1.0 + 0.05 * jax.random.normal(k, shape, f32)

    return {
        "x": jax.random.normal(ks[0], (BATCH, SEQ, D), f32),
        "p": jax.random.normal(ks[1], (DEPTH, BATCH, SEQ, PLE_DIM), f32),
        "a_norm": gain(ks[2], (N_A, D)),
        "a_w_in": nrm(ks[3], (N_A, D, 2 * D), D),
        "a_w_group": nrm(ks[4], (N_A, N_POOL_GROUPS, C, C), C),
        "a_scale": gain(ks[5], (N_A, D)),
        "a_w_out": nrm(ks[6], (N_A, D, D), D, 0.5),
        "kv_norm": gain(ks[7], (D,)),
        "w_kv": nrm(ks[8], (D, 2 * D), D),
        "k_norm": gain(ks[9], (SB_HEAD_DIM,)),
        "b_norm": gain(ks[10], (N_B, D)),
        "b_w_in": nrm(ks[11], (N_B, D, 2 * D), D),
        "b_q_norm": gain(ks[12], (N_B, SB_HEAD_DIM)),
        "b_w_out": nrm(ks[13], (N_B, D, D), D, 0.5),
        "ple_w": nrm(ks[14], (DEPTH, PLE_DIM, D), PLE_DIM, 0.5),
        "ple_gate_w": nrm(ks[15], (DEPTH, D, D), D),
    }

def first_block(x, p, a_norm, a_w_in, a_w_group, a_scale, a_w_out, kv_norm, w_kv, k_norm,
              b_norm, b_w_in, b_q_norm, b_w_out, ple_w, ple_gate_w):
    B, S, _ = x.shape
    k_sh = v_sh = None
    for i in range(DEPTH):
        if i < N_A:
            h = rms_norm(x, a_norm[i])
            x = x + pool_mixer(h, a_w_in[i], a_w_group[i], a_scale[i], a_w_out[i])
        else:
            j = i - N_A
            if j == 0:
                kv_in = rms_norm(x, kv_norm)
                k_all, v_all = jnp.split(kv_in @ w_kv, 2, axis=-1)
                k_sh = rms_norm(split_heads(k_all), k_norm)
                v_sh = split_heads(v_all)
            h = rms_norm(x, b_norm[j])
            q, z = jnp.split(h @ b_w_in[j], 2, axis=-1)
            q = rms_norm(split_heads(q), b_q_norm[j])
            o = stick_breaking_attention(q, k_sh, v_sh)
            o = o.transpose(0, 2, 1, 3).reshape(B, S, D_MODEL)
            x = x + (o * jax.nn.silu(z)) @ b_w_out[j]
        x = x + (p[i] @ ple_w[i]) * jax.nn.sigmoid(x @ ple_gate_w[i])
    return x


MLA_HEADS = 8
MLA_NOPE = 64
MLA_ROPE = 32
MLA_V = 64
MLA_QK = MLA_NOPE + MLA_ROPE
MLA_Q_RANK = 256
MLA_KV_RANK = 128
ROPE_THETA = 10000.0
MOBA_HEADS = 8
MOBA_HEAD_DIM = 64
MOBA_W = MOBA_HEADS * MOBA_HEAD_DIM
MOBA_BLOCK = 256
MOBA_TOPK = 3
MOBA_Q_CHUNK = 16
S5_GROUP = 16
S5_GROUPS = D_MODEL // S5_GROUP
S5_STATE = 64
S5_CHUNK = 128
DT_MIN = 1e-3
DT_MAX = 1e-1
D_FF = 4 * D_MODEL

N_EVEN = (DEPTH + 1) // 2
N_ODD = DEPTH // 2
IN_SIZES = [MLA_Q_RANK, MLA_KV_RANK, MLA_ROPE, MOBA_W, MOBA_W, MOBA_W]
IN_COLS = sum(IN_SIZES)
IN_SPLITS = [int(v) for v in np.cumsum(IN_SIZES)[:-1]]
MIX_WIDTH = MLA_HEADS * MLA_V + MOBA_W


def rms_norm_2(x, g):
    xf = x.astype(jnp.float32)
    y = xf * lax.rsqrt(jnp.mean(xf * xf, axis=-1, keepdims=True) + EPS)
    return (y * g.astype(jnp.float32)).astype(x.dtype)

def apply_rope(x, pos):
    half = x.shape[-1] // 2
    inv = ROPE_THETA ** (-jnp.arange(half, dtype=jnp.float32) / half)
    ang = pos.astype(jnp.float32)[:, None] * inv[None, :]
    cos = jnp.cos(ang).astype(x.dtype)
    sin = jnp.sin(ang).astype(x.dtype)
    x1, x2 = x[..., :half], x[..., half:]
    return jnp.concatenate([x1 * cos - x2 * sin, x1 * sin + x2 * cos], axis=-1)

def causal_attention_blocks(q, k, v):
    S = q.shape[2]
    outs = []
    for i in range(S // Q_BLOCK):
        lo, hi = i * Q_BLOCK, (i + 1) * Q_BLOCK
        s = jnp.einsum('bhqd,bhkd->bhqk', q[:, :, lo:hi], k[:, :, :hi]).astype(jnp.float32)
        mask = jnp.arange(hi)[None, :] <= jnp.arange(lo, hi)[:, None]
        p = jax.nn.softmax(jnp.where(mask, s, -jnp.inf), axis=-1).astype(v.dtype)
        outs.append(jnp.einsum('bhqk,bhkd->bhqd', p, v[:, :, :hi]))
    return jnp.concatenate(outs, axis=2)

def moba_attention(q, k, v):
    B, H, S, d = q.shape
    nb = -(-S // MOBA_BLOCK)
    pad = nb * MOBA_BLOCK - S
    kp = jnp.pad(k, ((0, 0), (0, 0), (0, pad), (0, 0)))
    vp = jnp.pad(v, ((0, 0), (0, 0), (0, pad), (0, 0)))
    k_blocks = kp.reshape(B, H, nb, MOBA_BLOCK, d)
    kv_blocks = jnp.concatenate([k_blocks, vp.reshape(B, H, nb, MOBA_BLOCK, d)], axis=-1)
    k_mean = jnp.mean(k_blocks.astype(jnp.float32), axis=3).astype(k.dtype)
    n_sel = min(MOBA_TOPK, nb - 1)
    b_idx = jnp.arange(B)[:, None, None, None]
    h_idx = jnp.arange(H)[None, :, None, None]
    blk_pos = jnp.arange(MOBA_BLOCK)

    def chunk(c):
        t0 = c * MOBA_Q_CHUNK
        qc = lax.dynamic_slice_in_dim(q, t0, MOBA_Q_CHUNK, axis=2)
        t = t0 + jnp.arange(MOBA_Q_CHUNK)
        cur = t0 // MOBA_BLOCK
        kv_own = lax.dynamic_index_in_dim(kv_blocks, cur, axis=2, keepdims=False)
        s_own = jnp.einsum('bhqd,bhld->bhql', qc, kv_own[..., :d]).astype(jnp.float32)
        s_own = jnp.where(cur * MOBA_BLOCK + blk_pos[None, :] <= t[:, None], s_own, -jnp.inf)
        if n_sel == 0:
            p = jax.nn.softmax(s_own, axis=-1).astype(v.dtype)
            return jnp.einsum('bhql,bhld->bhqd', p, kv_own[..., d:])
        gate = jnp.einsum('bhqd,bhnd->bhqn', qc, k_mean).astype(jnp.float32)
        gate = jnp.where(jnp.arange(nb) < cur, gate, -jnp.inf)
        _, sel = lax.top_k(gate, n_sel)
        sel_ok = jnp.arange(n_sel) < cur
        kv_sel = kv_blocks[b_idx, h_idx, sel]
        s_sel = jnp.einsum('bhqd,bhqnld->bhqnl', qc, kv_sel[..., :d]).astype(jnp.float32)
        s_sel = jnp.where(sel_ok[:, None], s_sel, -jnp.inf)
        s_sel = s_sel.reshape(B, H, MOBA_Q_CHUNK, n_sel * MOBA_BLOCK)
        p = jax.nn.softmax(jnp.concatenate([s_sel, s_own], axis=-1), axis=-1).astype(v.dtype)
        p_sel = p[..., :n_sel * MOBA_BLOCK].reshape(B, H, MOBA_Q_CHUNK, n_sel, MOBA_BLOCK)
        p_own = p[..., n_sel * MOBA_BLOCK:]
        return (jnp.einsum('bhqnl,bhqnld->bhqd', p_sel, kv_sel[..., d:])
                + jnp.einsum('bhql,bhld->bhqd', p_own, kv_own[..., d:]))

    outs = lax.map(chunk, jnp.arange(S // MOBA_Q_CHUNK))
    return outs.transpose(1, 2, 0, 3, 4).reshape(B, H, S, d)

def attn_mixer(h, w_in, g_cq, w_uq, g_ckv, w_ukv, g_qn_mla, g_kn_mla, g_qn_moba, g_kn_moba, w_o):
    B, S, _ = h.shape
    pos = jnp.arange(S)
    c_q, c_kv, k_r, q_b, k_b, v_b = jnp.split(h @ w_in, IN_SPLITS, axis=-1)
    q = (rms_norm_2(c_q, g_cq) @ w_uq).reshape(B, S, MLA_HEADS, MLA_QK).transpose(0, 2, 1, 3)
    kv = (rms_norm_2(c_kv, g_ckv) @ w_ukv).reshape(B, S, MLA_HEADS, MLA_NOPE + MLA_V).transpose(0, 2, 1, 3)
    k_nope, v = kv[..., :MLA_NOPE], kv[..., MLA_NOPE:]
    q = jnp.concatenate([q[..., :MLA_NOPE], apply_rope(q[..., MLA_NOPE:], pos)], axis=-1)
    k_rope = jnp.broadcast_to(apply_rope(k_r, pos)[:, None], (B, MLA_HEADS, S, MLA_ROPE))
    k = jnp.concatenate([k_nope, k_rope], axis=-1)
    q = rms_norm_2(q, g_qn_mla) * (MLA_QK ** -0.5)
    k = rms_norm_2(k, g_kn_mla)
    o_mla = causal_attention_blocks(q, k, v)
    def heads(t):
        return t.reshape(B, S, MOBA_HEADS, MOBA_HEAD_DIM).transpose(0, 2, 1, 3)
    qm = rms_norm_2(heads(q_b), g_qn_moba) * (MOBA_HEAD_DIM ** -0.5)
    km = rms_norm_2(heads(k_b), g_kn_moba)
    o_moba = moba_attention(qm, km, heads(v_b))
    o = jnp.concatenate([o_mla.transpose(0, 2, 1, 3).reshape(B, S, MLA_HEADS * MLA_V),
                         o_moba.transpose(0, 2, 1, 3).reshape(B, S, MOBA_W)], axis=-1)
    return o @ w_o

def s5_mixer(h, lam_re, lam_im, log_dt, b_re, b_im, c_re, c_im, d_skip, w_glu):
    B, S, D = h.shape
    f32 = jnp.float32
    u = h.astype(f32)
    lam = lax.complex(lam_re.astype(f32), lam_im.astype(f32))
    dt = jnp.exp(log_dt.astype(f32))[:, None]
    a_bar = jnp.exp(lam * dt)
    b_bar = ((a_bar - 1.0) / lam)[..., None] * lax.complex(b_re.astype(f32), b_im.astype(f32))
    cmat = lax.complex(c_re.astype(f32), c_im.astype(f32))
    nc = S // S5_CHUNK
    u_chunks = u.reshape(B, nc, S5_CHUNK, S5_GROUPS, S5_GROUP).transpose(1, 2, 0, 3, 4)
    steps = jnp.arange(1, S5_CHUNK + 1, dtype=f32)
    a_pow = jnp.exp(lam[None] * dt[None] * steps[:, None, None])
    a_el = jnp.broadcast_to(a_bar, (S5_CHUNK, 1, S5_GROUPS, S5_STATE))

    def combine(e1, e2):
        a1, b1 = e1
        a2, b2 = e2
        return a1 * a2, a2 * b1 + b2

    def step(state, uc):
        bu = jnp.einsum('gpi,lbgi->lbgp', b_bar, uc.astype(jnp.complex64))
        _, hs = lax.associative_scan(combine, (a_el, bu), axis=0)
        hs = hs + a_pow[:, None] * state[None]
        y = jnp.einsum('gop,lbgp->lbgo', cmat, hs).real
        return hs[-1], y

    state0 = jnp.zeros((B, S5_GROUPS, S5_STATE), jnp.complex64)
    _, ys = lax.scan(step, state0, u_chunks)
    y = ys.transpose(2, 0, 1, 3, 4).reshape(B, S, D) + d_skip.astype(f32) * u
    g = jax.nn.gelu(y).astype(h.dtype)
    val, gate = jnp.split(g @ w_glu, 2, axis=-1)
    return val * jax.nn.sigmoid(gate)

def sq_relu_mlp(h, w1, w2):
    return jnp.square(jax.nn.relu(h @ w1)) @ w2

def second_inputs(seed: int = 0) -> dict:
    key = jax.random.key(seed)
    ks = iter(jax.random.split(key, 32))
    f32 = jnp.float32

    def nrm(shape, scale):
        return jax.random.normal(next(ks), shape, f32) * scale

    def gain(shape):
        return 1.0 + 0.02 * jax.random.normal(next(ks), shape, f32)

    n_idx = jnp.arange(S5_STATE, dtype=f32)
    return {
        "x": nrm((BATCH, SEQ, D_MODEL), 1.0),
        "mix_norm_g": gain((DEPTH, D_MODEL)),
        "ffn_norm_g": gain((DEPTH, D_MODEL)),
        "w_in": nrm((N_EVEN, D_MODEL, IN_COLS), D_MODEL ** -0.5),
        "g_cq": gain((N_EVEN, MLA_Q_RANK)),
        "w_uq": nrm((N_EVEN, MLA_Q_RANK, MLA_HEADS * MLA_QK), MLA_Q_RANK ** -0.5),
        "g_ckv": gain((N_EVEN, MLA_KV_RANK)),
        "w_ukv": nrm((N_EVEN, MLA_KV_RANK, MLA_HEADS * (MLA_NOPE + MLA_V)), MLA_KV_RANK ** -0.5),
        "g_qn_mla": gain((N_EVEN, MLA_QK)),
        "g_kn_mla": gain((N_EVEN, MLA_QK)),
        "g_qn_moba": gain((N_EVEN, MOBA_HEAD_DIM)),
        "g_kn_moba": gain((N_EVEN, MOBA_HEAD_DIM)),
        "w_o": nrm((N_EVEN, MIX_WIDTH, D_MODEL), MIX_WIDTH ** -0.5),
        "lam_re": -0.5 + nrm((N_ODD, S5_GROUPS, S5_STATE), 0.01),
        "lam_im": math.pi * n_idx + nrm((N_ODD, S5_GROUPS, S5_STATE), 0.01),
        "log_dt": jax.random.uniform(next(ks), (N_ODD, S5_GROUPS), f32, math.log(DT_MIN), math.log(DT_MAX)),
        "b_re": nrm((N_ODD, S5_GROUPS, S5_STATE, S5_GROUP), (2 * S5_GROUP) ** -0.5),
        "b_im": nrm((N_ODD, S5_GROUPS, S5_STATE, S5_GROUP), (2 * S5_GROUP) ** -0.5),
        "c_re": nrm((N_ODD, S5_GROUPS, S5_GROUP, S5_STATE), (2 * S5_STATE) ** -0.5),
        "c_im": nrm((N_ODD, S5_GROUPS, S5_GROUP, S5_STATE), (2 * S5_STATE) ** -0.5),
        "d_skip": nrm((N_ODD, D_MODEL), 1.0),
        "w_glu": nrm((N_ODD, D_MODEL, 2 * D_MODEL), D_MODEL ** -0.5),
        "w_ff1": nrm((DEPTH, D_MODEL, D_FF), D_MODEL ** -0.5),
        "w_ff2": nrm((DEPTH, D_FF, D_MODEL), D_FF ** -0.5),
    }

def second_block(x, mix_norm_g, ffn_norm_g, w_in, g_cq, w_uq, g_ckv, w_ukv, g_qn_mla, g_kn_mla,
              g_qn_moba, g_kn_moba, w_o, lam_re, lam_im, log_dt, b_re, b_im, c_re, c_im,
              d_skip, w_glu, w_ff1, w_ff2):
    for layer in range(DEPTH):
        h = rms_norm_2(x, mix_norm_g[layer])
        i = layer // 2
        if layer % 2 == 0:
            x = x + attn_mixer(h, w_in[i], g_cq[i], w_uq[i], g_ckv[i], w_ukv[i], g_qn_mla[i],
                               g_kn_mla[i], g_qn_moba[i], g_kn_moba[i], w_o[i])
        else:
            x = x + s5_mixer(h, lam_re[i], lam_im[i], log_dt[i], b_re[i], b_im[i], c_re[i],
                             c_im[i], d_skip[i], w_glu[i]).astype(x.dtype)
        x = x + sq_relu_mlp(rms_norm_2(x, ffn_norm_g[layer]), w_ff1[layer], w_ff2[layer])
    return x


def setup_inputs(seed=0):
    out = dict(first_inputs(seed))
    for name, value in second_inputs(seed + 1).items():
        if name != "x":
            out[name + "_2"] = value
    return out


def reference(
    x, p, a_norm, a_w_in, a_w_group, a_scale, a_w_out, kv_norm, w_kv, k_norm, b_norm, b_w_in,
    b_q_norm, b_w_out, ple_w, ple_gate_w, mix_norm_g_2, ffn_norm_g_2, w_in_2, g_cq_2, w_uq_2,
    g_ckv_2, w_ukv_2, g_qn_mla_2, g_kn_mla_2, g_qn_moba_2, g_kn_moba_2, w_o_2, lam_re_2,
    lam_im_2, log_dt_2, b_re_2, b_im_2, c_re_2, c_im_2, d_skip_2, w_glu_2, w_ff1_2, w_ff2_2,
):
    x = first_block(
        x, p, a_norm, a_w_in, a_w_group, a_scale, a_w_out, kv_norm, w_kv, k_norm, b_norm,
        b_w_in, b_q_norm, b_w_out, ple_w, ple_gate_w,
    )
    return second_block(
        x, mix_norm_g_2, ffn_norm_g_2, w_in_2, g_cq_2, w_uq_2, g_ckv_2, w_ukv_2, g_qn_mla_2,
        g_kn_mla_2, g_qn_moba_2, g_kn_moba_2, w_o_2, lam_re_2, lam_im_2, log_dt_2, b_re_2,
        b_im_2, c_re_2, c_im_2, d_skip_2, w_glu_2, w_ff1_2, w_ff2_2,
    )


_drawn_inputs = setup_inputs


def setup_inputs(seed=0):
    import zlib

    import numpy as np

    out = dict(_drawn_inputs(seed))
    spreads = {}
    factors = {'a_norm': 2.715,
     'a_scale': 3.822,
     'kv_norm': 5.144,
     'k_norm': 8.0,
     'b_norm': 5.034,
     'b_q_norm': 8.0,
     'mix_norm_g_2': 6.69,
     'g_cq_2': 8.0,
     'g_ckv_2': 8.0,
     'g_qn_mla_2': 8.0,
     'g_kn_mla_2': 8.0,
     'g_qn_moba_2': 8.0,
     'g_kn_moba_2': 8.0,
     'lam_re_2': 64.0,
     'lam_im_2': 34.816,
     'log_dt_2': 39.88,
     'b_re_2': 46.808,
     'b_im_2': 50.288,
     'c_re_2': 48.664,
     'c_im_2': 51.8,
     'ffn_norm_g_2': 8.0}
    for name, (base, spread) in spreads.items():
        noise = np.random.default_rng([zlib.crc32(name.encode()), seed]).standard_normal(out[name].shape)
        drawn = base * np.exp(spread * noise) if base else spread * noise
        out[name] = __import__('jax').numpy.asarray(drawn.astype(out[name].dtype))
    for name, factor in factors.items():
        out[name] = (out[name] * factor).astype(out[name].dtype)
    return out
```

```python
from contextlib import ExitStack

import concourse.bass as bass
from concourse import mybir

F32 = mybir.dt.float32
BF16 = mybir.dt.bfloat16
ALU = mybir.AluOpType
ACT = mybir.ActivationFunctionType
AX_X = mybir.AxisListType.X

P = 128
S, D = 256, 1024
NT = S // P
KC = D // P
EPS = 1e-6
WINDOWS = (2, 4, 8, 16)
RING = 5
BLK = 4096
NH = 16
HD = 64
MH, MQK, MNOPE, MROPE = 8, 96, 64, 32
G, GI, GP = 64, 16, 64
L = 8
NC = S // L
FB = 8
BIG = -1.0e30

VEC_ROWS = {"a_norm": 8, "a_scale": 8, "kv_norm": 8, "b_norm": 8, "mix0": 8, "ffn0": 8, "mix1": 8, "ffn1": 8,
            "d_skip": 8, "g_cq": 2, "g_ckv": 1, "k_norm": 1, "q_norm": 1, "qn_mla": 1, "kn_mla": 1,
            "qn_moba": 1, "kn_moba": 1}
VEC_AT = {}
for _n, _k in VEC_ROWS.items():
    VEC_AT[_n] = sum(VEC_ROWS[m] for m in VEC_AT)
NVEC = sum(VEC_ROWS.values())

CONST_COLS = {"ident": 128, "tneg": 128, "swap": 128, "bmask": 128, "mask_st": 128, "mask_ts": 128, "cos": 32,
              "sin": 32, "sgn": 2}
CONST_AT = {}
for _n, _k in CONST_COLS.items():
    CONST_AT[_n] = sum(CONST_COLS[m] for m in CONST_AT)
NCONST = sum(CONST_COLS.values())
NPOOL = 4 * 384


def constants():
    import numpy as np
    i = np.arange(P)
    c = np.zeros((P, NCONST), np.float32)

    def put(name, a):
        c[:, CONST_AT[name]:CONST_AT[name] + CONST_COLS[name]] = a

    put("ident", np.eye(P))
    put("tneg", -(i[:, None] >= i[None, :]).astype(np.float32))
    put("swap", np.roll(np.eye(P), 64, axis=1))
    put("bmask", (i[:, None] // GI == i[None, :] // GI))
    put("mask_st", np.where(i[:, None] >= i[None, :], BIG, 0))
    put("mask_ts", np.where(i[None, :] > i[:, None], BIG, 0))
    half = MROPE // 2
    inv = (np.float32(10000.0) ** (-np.arange(half, dtype=np.float32) / np.float32(half))).astype(np.float32)
    ang = (np.arange(S, dtype=np.float32)[:, None] * inv[None, :]).astype(np.float32)
    put("cos", np.cos(ang).reshape(NT, P, half).transpose(1, 0, 2).reshape(P, 32))
    put("sin", np.sin(ang).reshape(NT, P, half).transpose(1, 0, 2).reshape(P, 32))
    put("sgn", np.where(i[:, None] < 64, [[1.0, -1.0]], [[-1.0, 1.0]]))
    pool = np.zeros((P, 4, 384), np.float32)
    t = np.arange(S)
    for g, w in enumerate(WINDOWS):
        m = ((t[:, None] <= t[None, :]) & (t[:, None] > t[None, :] - w)) / np.minimum(t[None, :] + 1, w)
        m = m - np.eye(S)
        pool[:, g, 0:256] = m[0:P]
        pool[:, g, 256:384] = m[P:, P:]
    return c, pool.reshape(P, NPOOL)


class Units:

    def __init__(self):
        self.at, self.bank, self.before, self.by, self.count = {}, [], [], [], []
        self.last, self.turn, self.banks = {}, 0, list(range(8))

    def add(self, name, freed_by, bank=None):
        if bank is None:
            bank = self.banks[self.turn % len(self.banks)]
            self.turn += 1
        q = len(self.bank)
        assert name not in self.at, name
        self.at[name] = q
        self.bank.append(bank)
        self.before.append(self.last.get(bank))
        self.by.append(freed_by)
        self.count.append(self.by.count(freed_by))
        self.last[bank] = q

    def done(self, name):
        return self.at[name] + 1

    def emptied(self, name):
        return self.count[self.at[name]]


def gemm(u, stage, blocks, freed_by):
    for nb in range(blocks):
        for t in range(NT):
            u.add((stage, nb, t), freed_by)


def turned(u, stage, n=4):
    for k in range(n):
        u.add(("T", stage, k), "av"[(k + 1) % 2])


def plan():
    u = Units()
    u.add("vec", "v")
    u.add(("pT", 0), "a")
    u.add(("pT", 1), "a")
    turned(u, "a")
    gemm(u, "u", 2, "a")
    gemm(u, "za", 2, "a")
    for g in range(4):
        u.add(("pool", g), "a")
    gemm(u, "mixed", 2, "v")
    turned(u, "mixed")
    gemm(u, "a_out", 2, "v")
    gemm(u, "ple0", 2, "a")
    turned(u, "x0")
    gemm(u, "gate0", 2, "a")
    turned(u, "b")
    gemm(u, "k", 2, "a")
    gemm(u, "v", 2, "a")
    turned(u, "k")
    gemm(u, "q", 2, "a")
    gemm(u, "zb", 2, "a")
    turned(u, "q")
    for i in range(NH + 3):
        if i < NH:
            u.add(("logits", i), "", bank=i % 5)
        if 2 <= i < NH + 2:
            u.add(("loga", i - 2), "a", bank=(i - 2) % 5)
        if i >= 3 and (i - 3) % 4 == 3:
            u.add(("stick_out", (i - 3) // 4), "v", bank=5 + (i - 3) // 4 % 3)
    turned(u, "o1")
    gemm(u, "b_out", 2, "v")
    gemm(u, "ple1", 2, "a")
    turned(u, "x1")
    gemm(u, "gate1", 2, "a")
    turned(u, "mix0")
    gemm(u, "wc", 1, "a")
    gemm(u, "wq", 1, "a")
    u.add(("T", "c", 0), "v")
    u.add(("T", "c", 1), "v")
    gemm(u, "uq", 2, "a")
    gemm(u, "ukv", 2, "a")
    gemm(u, "wk", 1, "a")
    gemm(u, "wv", 1, "a")
    for kind in ("moba", "mla"):
        turned(u, "q" + kind, 2 if kind == "moba" else 4)
        turned(u, "k" + kind, 2 if kind == "moba" else 4)
        for i in range(MH + 3):
            if i < MH:
                u.add(("scores", kind, i), "a", bank=i % 4)
            if 2 <= i < MH + 2:
                u.add(("probsT", kind, i - 2), "v", bank=4 + i % 2)
            if i >= 3 and (i - 3) % 4 == 3:
                u.add(("soft_out", kind, (i - 3) // 4), "v", bank=6 + (i - 3) // 4)
    turned(u, "o2")
    gemm(u, "w_o", 2, "v")
    mlp_plan(u, 0)
    turned(u, "mix1")
    u.add("gain_gi", "v")
    for b in range(4):
        u.add(("ug", b), "v")
    for b in range(4):
        u.add(("inject", b), "a")
    for b in range(4):
        u.add(("injectx", b), "a")
    for b in range(4):
        u.add(("fir", b), "v")
    for b in range(4):
        u.add(("state_out", b), "a")
    for b in range(4):
        u.add(("state_outT", b), "v")
    for h in range(2):
        gemm(u, ("val", h), 1, "v")
        gemm(u, ("gate", h), 1, "a")
    mlp_plan(u, 1)
    return u


def mlp_plan(u, layer):
    turned(u, ("ffn", layer))
    u.banks, u.turn = [4, 5, 6, 7], 0
    for i in range(FB + 2):
        if i < FB:
            gemm(u, ("f1", layer, i), 1, "v")
        if 1 <= i <= FB:
            for k in range(2):
                u.add(("fT", layer, i - 1, k), "a")
        if layer == 0:
            if i == 1:
                for k in range(3):
                    u.add(("powT", k), "a")
                for k in range(8):
                    u.add(("bcT", k), "v")
            if i >= 2:
                u.add(("wT", i - 2, 0), "a")
                u.add(("wT", i - 2, 1), "a")
                u.add(("taps", i - 2), "v")
    for k in range(4):
        u.add(("acc", layer, k), "v", bank=k)
    u.banks, u.turn = list(range(8)), 4


def loads(w):
    def cols(a, c0, c1):
        return a[:, c0:c1].rearrange("(k p) n -> p k n", p=P)

    out = []
    a_in, a_out, w_kv, b_in, b_out = w["a_w_in"][0], w["a_w_out"][0], w["w_kv"], w["b_w_in"][0], w["b_w_out"][0]

    def add(name, parts, reader):
        out.append((name, parts, reader))

    def two(name, a, base, unit):
        for nb in range(2):
            add((name, nb), [(0, cols(a, base + 512 * nb, base + 512 * nb + 512))], (unit, nb, 1))

    two("u", a_in, 0, "u")
    two("za", a_in, D, "za")
    add("w_group", [(0, w["a_w_group"][0].rearrange("g (k p) n -> p (g k) n", p=P))], ("mixed", 1, 1))
    two("a_out", a_out, 0, "a_out")
    add("ple0", [(0, cols(w["ple_w"][0], 0, D))], ("ple0", 1, 1))
    two("gate0", w["ple_gate_w"][0], 0, "gate0")
    two("k", w_kv, 0, "k")
    two("v", w_kv, D, "v")
    two("q", b_in, 0, "q")
    two("zb", b_in, D, "zb")
    two("b_out", b_out, 0, "b_out")
    add("ple1", [(0, cols(w["ple_w"][1], 0, D))], ("ple1", 1, 1))
    two("gate1", w["ple_gate_w"][1], 0, "gate1")
    w_in = w["w_in_2"][0]
    add("wc", [(0, cols(w_in, 0, 416))], ("wc", 0, 1))
    add("wq", [(0, cols(w_in, 416, 928))], ("wq", 0, 1))
    add("lowrank", [(0, cols(w["w_uq_2"][0], 0, 768)), (1536, cols(w["w_ukv_2"][0], 0, 1024))], ("ukv", 1, 1))
    add("wk", [(0, cols(w_in, 928, 1440))], ("wk", 0, 1))
    add("wv", [(0, cols(w_in, 1440, 1952))], ("wv", 0, 1))
    two("w_o", w["w_o_2"][0], 0, "w_o")
    mlp_loads(w, add, cols, 0)
    for name, reader in (("inject", ("inject", 3)), ("taps", ("fir", 3)), ("readout", ("state_out", 3))):
        for half in range(2):
            add((name, half), [(0, w["scratch_" + name][:, half * BLK:half * BLK + BLK])], (reader[0], 2 * half + 1))
    for h in range(2):
        for name, base in (("val", 0), ("gate", D)):
            add((name, h), [(0, cols(w["w_glu_2"][0], base + 512 * h, base + 512 * h + 512))], ((name, h), 0, 1))
    mlp_loads(w, add, cols, 1)
    return out


def mlp_loads(w, add, cols, layer):
    w1, w2 = w["w_ff1_2"][layer], w["w_ff2_2"][layer]
    for i in range(FB + 2):
        if i < FB:
            add(("f1", layer, i), [(0, cols(w1, 512 * i, 512 * i + 512))], (("f1", layer, i), 0, 1))
        if layer == 0 and i == 1:
            add("rawB", [(1024 * n, w[b][0].rearrange("g p i -> g (p i)")) for n, b in
                         enumerate(("b_re_2", "b_im_2", "b_re_2"))], ("bcT", 3))
            add("rawC", [(GP * n, w[c][0]) for n, c in enumerate(("c_re_2", "c_im_2", "c_re_2"))], ("bcT", 7))
        if i >= 2:
            add(("f2", layer, i - 2), [(0, w2[512 * (i - 2):512 * (i - 2) + 512, :].rearrange("(k p) n -> p k n", p=P))],
                ("f2", (FB - 1) * layer + i - 2) if i - 2 < FB - 1 else ("acc", layer, 3))


def program(nc, w, out):
    import numpy as np
    u = plan()
    blocks = loads(w)
    slot = {name: n % RING for n, (name, _, _) in enumerate(blocks)}
    landed = {}
    for n, (name, parts, _) in enumerate(blocks):
        before = landed[blocks[n - RING][0]] if n >= RING else 0
        landed[name] = before + 16 * len(parts)
    done = u.done

    with ExitStack() as ctx:
        def sb(name, shape, dt=F32):
            return ctx.enter_context(nc.sbuf_tensor(name, shape, dt))

        def sem(name):
            return ctx.enter_context(nc.semaphore(name))

        ps = [ctx.enter_context(nc.psum_tensor(f"bank{i}", [P, 512], F32)) for i in range(8)]

        x = sb("x", [P, NT, D])
        h = sb("h", [P, NT, D])
        hT = sb("hT", [P, KC, S])
        hT2 = sb("hT2", [P, KC, S])
        work = sb("work", [P, 12288])
        aux = sb("aux", [P, 6144])
        ring = sb("ring", [P, RING, BLK])
        junk = sb("junk", [P, D])
        sig = sb("sig", [P, 2, 512])
        pT = sb("pT", [P, 2, 2, S])
        vrows = sb("vrows", [NVEC, P])
        vcols = sb("vcols", [P, NVEC])
        cst = sb("cst", [P, NCONST])
        bf = sb("bf", [P, 3, P], BF16)
        allneg = sb("allneg", [P, P])
        half_neg = sb("half_neg", [P, 32])
        ssq = sb("ssq", [P, 6, NT])
        ms = sb("ms", [P, 6, NT])
        rstd = sb("rstd", [P, 6, NT])
        ssh = sb("ssh", [P, 32])
        msh = sb("msh", [P, 32])
        rsh = sb("rsh", [P, 32])
        lowss = sb("lowss", [P, 4])
        lowms = sb("lowms", [P, 4])
        lowr = sb("lowr", [P, 4])
        nmax = sb("nmax", [P, 2, MH, NT])
        den = sb("den", [P, 2, MH, NT])
        rden = sb("rden", [P, 2, MH, NT])
        a8 = sb("a8", [P, 3, G])
        gain_rows = sb("gain_rows", [G, 2, P])
        gain_gi = sb("gain_gi", [P, G])
        log_dt = sb("log_dt", [G, 2])

        block_landed = [sem(f"block_landed{i}") for i in range(RING)]
        (pe_done, act_emptied, dve_emptied, x_landed, tables_landed, p_landed, pools_landed, vecs_landed,
         masks_ready, gains_ready, x_updated, ssq_ready, ms_ready, rstd_ready, headms_ready, headr_ready,
         heads_normed, logs_ready, sp_ready, lowms_ready, lowr_ready, max_ready, f2_done, halves_ready,
         dt_ready, zr_ready, exp_ready, angle_ready, sin_ready, lam_landed, powers_ready, pads_zeroed,
         inputs_scaled, injects_made, readouts_made, pads_filled, w_stored, v_stored, t_stored, h_normed,
         regrouped_a, regrouped_b, gain_rows_ready, gain_landed, states_ready, gelu_ready, act_step, dve_step, pool_step,
         out_stored) = (
            sem(n) for n in (
                "pe_done", "act_emptied", "dve_emptied", "x_landed", "tables_landed", "p_landed",
                "pools_landed", "vecs_landed", "masks_ready", "gains_ready", "x_updated",
                "ssq_ready", "ms_ready", "rstd_ready", "headms_ready", "headr_ready",
                "heads_normed", "logs_ready", "sp_ready", "lowms_ready", "lowr_ready", "max_ready",
                "f2_done", "halves_ready", "dt_ready", "zr_ready", "exp_ready", "angle_ready",
                "sin_ready", "lam_landed", "powers_ready", "pads_zeroed", "inputs_scaled",
                "injects_made", "readouts_made", "pads_filled", "w_stored", "v_stored", "t_stored",
                "h_normed", "regrouped_a", "regrouped_b", "gain_rows_ready", "gain_landed", "states_ready",
                "gelu_ready", "act_step", "dve_step", "pool_step", "out_stored"))

        chunked = [sem("chunked_a"), sem("chunked_b")]

        def const(name):
            return cst[:, CONST_AT[name]:CONST_AT[name] + CONST_COLS[name]]

        def gain(name, c=0, rows=P):
            return vcols[0:rows, VEC_AT[name] + c:VEC_AT[name] + c + 1]

        def weights(name, k, n, at=0):
            return ring[:, slot[name], at:at + k * n].rearrange("p (k n) -> p k n", k=k)

        def tok(at, n=D):
            return work[:, at:at + NT * n].rearrange("p (t n) -> p t n", t=NT)

        def bank(name):
            return ps[u.bank[u.at[name]]]

        ident, tneg = const("ident"), const("tneg")
        q_tok, k_tok, v_tok, z_tok = (tok(2048 * n) for n in range(4))
        u_tok = q_tok
        p_tok = work[:, 8192:9216].rearrange("p (l t n) -> p l t n", l=2, t=NT)
        pl_tok = aux[:, 0:2048].rearrange("p (t n) -> p t n", t=NT)
        pools = aux[:, 2048:2048 + NPOOL].rearrange("p (g n) -> p g n", g=4)
        qT = work[:, 8192:10240].rearrange("p (c s) -> p c s", c=KC)
        kT = work[:, 10240:12288].rearrange("p (c s) -> p c s", c=KC)
        squares = aux[:, 0:2048]
        logs, sps, sticks = (aux[:, 2048 + 1152 * n:3200 + 1152 * n].rearrange("p (b n) -> p b n", b=3)
                             for n in range(3))
        qm, km = tok(0, MH * MQK), tok(1536, MH * MQK)
        vm, qb, kb, vb = (tok(3072 + 1024 * n, 512) for n in range(4))
        cbuf = tok(7168, 416)
        cT = hT2[:, 0:3, :]
        turned_qk = {"moba": (hT2[:, 0:4, :], hT2[:, 4:8, :]), "mla": (qT, kT)}
        ropes = aux[:, 2048:3072].rearrange("p (n t h c) -> p n t h c", n=4, t=NT, h=MH)
        probs = aux[:, 3200:4352].rearrange("p (b n) -> p b n", b=3)
        probsT = aux[:, 4352:5504].rearrange("p (b n) -> p b n", b=3)
        hid = aux[:, 0:2048].rearrange("p (b t n) -> p b t n", b=2, t=NT)
        hidT = aux[:, 2048:4096].rearrange("p (b c s) -> p b c s", b=2, c=4)
        inject_T = aux[:, 4096:5120]
        taps = aux[:, 5120:6144]
        inject = work[:, 0:1024].rearrange("p (g j i) -> p g j i", g=8, j=L)
        readout = work[:, 1024:2176].rearrange("p (g k o) -> p g k o", g=8, k=L + 1)
        t1, t2 = work[:, 2176:3328], work[:, 3328:4480]
        Bs, Bx, Cs, Cx = (work[:, 4480 + 1024 * n:5504 + 1024 * n].rearrange("p (i g) -> p i g", i=GI)
                          for n in range(4))
        powT = work[:, 8576:9856].rearrange("p (q g) -> p q g", q=20)
        pads = work[:, 9856:10880]
        t3 = work[:, 10880:12032]
        lam = work[0:G, 10880:12288].rearrange("p (n c) -> p n c", c=GP)
        pw = work[0:G, 0:2560].rearrange("p (q r c) -> p q r c", q=20, r=2)
        powers = work[0:G, 3328:4352].rearrange("p (r k c) -> p r k c", r=2, k=L)
        prods = work[0:G, 4480:5504].rearrange("p (n k c) -> p n k c", n=4, k=4)
        xc = [v.rearrange("p (j n) -> p j n", j=L) for v in (work[0:NC, 8192:12288], aux[0:NC, 0:4096])]
        xg = work[0:NC, 0:8192].rearrange("p (g j i) -> p g j i", g=G, j=L)
        ug = aux[:, 4096:6144].rearrange("p (g c) -> p g c", g=G)
        states = work[:, 0:33 * 128].rearrange("p (r c g) -> p r c g", r=2, c=NC + 1)
        steps = work[:, 4224:4480].rearrange("p (n r g) -> p n r g", n=2, r=2)
        yc = work[:, 4480:6528].rearrange("p (f j n) -> p f j n", f=2, j=L)
        ybuf = work[:, 10240:12288].rearrange("p (c s) -> p c s", c=KC)

        block = ctx.enter_context(nc.Block())

        @block.sync
        def _(sp):
            stores = {"inject": w_stored, "readout": v_stored, "taps": t_stored}
            for n, (name, parts, _) in enumerate(blocks):
                if n >= RING:
                    reader = blocks[n - RING][2]
                    if reader[0] == "f2":
                        sp.wait_ge(f2_done, reader[1] + 1)
                    else:
                        sp.wait_ge(pe_done, done(reader))
                if name[0] in stores:
                    sp.wait_ge(stores[name[0]], 16 * 8)
                for at, src in parts:
                    rows, cols = src.shape[0], src.shape[1] * (src.shape[2] if len(src.shape) > 2 else 1)
                    dst = ring[0:rows, slot[name], at:at + cols]
                    if name == "rawC":
                        dst = ring[0:rows, slot[name], 0:3072].rearrange("p (o r c) -> p r o c", o=GI, r=3)[:, at // GP]
                    elif len(src.shape) > 2:
                        dst = dst.rearrange("p (k n) -> p k n", k=src.shape[1])
                    sp.dma_start(dst, src).then_inc(block_landed[slot[name]], 16)
            sp.wait_ge(dve_emptied, u.emptied(("acc", 1, 3)))
            sp.dma_start(out.rearrange("b (t p) n -> p (b t) n", p=P), x[:, :, :]).then_inc(out_stored, 16)
            sp.wait_ge(out_stored, 16)

        @block.tensor
        def _(pe):

            def begin(name):
                before = u.before[u.at[name]]
                if before is not None and u.by[before] == "a":
                    pe.wait_ge(act_emptied, u.count[before])
                elif before is not None:
                    pe.wait_ge(dve_emptied, u.count[before])
                return bank(name)

            def emptied(name):
                if u.by[u.at[name]] == "a":
                    pe.wait_ge(act_emptied, u.emptied(name))
                else:
                    pe.wait_ge(dve_emptied, u.emptied(name))

            def weights_here(name):
                pe.wait_ge(block_landed[slot[name]], landed[name])

            def turn(stage, src, units=range(4), width=P, chunks=8, ready=None):
                for k in units:
                    b = begin(("T", stage, k))
                    if ready:
                        ready(k)
                    for cc in range(2):
                        c = 2 * k + cc
                        if c < chunks:
                            for t in range(NT):
                                last = pe.transpose(b[0:width, cc * S + t * P:cc * S + t * P + P],
                                                    src[:, t, c * width:(c + 1) * width], ident)
                    last.then_inc(pe_done, 1)

            def product(stage, nb, name, stationary, k_chunks, width=512, turned_by=None, at=0):
                weights_here(name)
                wv = weights(name, k_chunks, width if at is None else width, 0) if at == 0 else at
                for t in range(NT):
                    b = begin((stage, nb, t))
                    for k in range(k_chunks):
                        if turned_by and t == 0 and k % 2 == 0:
                            emptied(("T", turned_by, k // 2))
                        last = pe.matmul(b[:, 0:width], stationary[:, k, t * P:(t + 1) * P], wv[:, k, :],
                                         start=(k == 0), stop=(k == k_chunks - 1))
                    last.then_inc(pe_done, 1)

            def x_has(stage):
                return lambda k: emptied((stage, k // 2, 1))

            def x_gated(before):
                return lambda k: pe.wait_ge(x_updated, before + (2 if k < 2 else 4))

            pe.wait_ge(tables_landed, 16)
            pe.wait_ge(vecs_landed, 16)
            b = begin("vec")
            pe.transpose(b[:, 0:NVEC], vrows[:, :], ident[0:NVEC, 0:NVEC]).then_inc(pe_done, 1)
            pe.wait_ge(p_landed, 32)
            for l in range(2):
                b = begin(("pT", l))
                for cc in range(2):
                    for t in range(NT):
                        last = pe.transpose(b[:, cc * S + t * P:cc * S + t * P + P],
                                            p_tok[:, l, t, cc * P:(cc + 1) * P], ident)
                last.then_inc(pe_done, 1)

            pe.wait_ge(x_landed, 16)
            turn("a", x)
            for stage in ("u", "za"):
                for nb in range(2):
                    product(stage, nb, (stage, nb), hT, KC, turned_by="a")
            pe.wait_ge(pools_landed, 16)
            for g in range(4):
                b = begin(("pool", g))
                emptied(("u", g // 2, 1))
                for cc in range(2):
                    c = 2 * g + cc
                    pe.matmul(b[:, cc * S:(cc + 1) * S], u_tok[:, 0, c * P:(c + 1) * P], pools[:, g, 0:S],
                              start=(cc == 0), stop=False, skip_group_check=True)
                    last = pe.matmul(b[:, cc * S + P:(cc + 1) * S], u_tok[:, 1, c * P:(c + 1) * P],
                                     pools[:, g, S:S + P], start=False, stop=True, skip_group_check=True)
                last.then_inc(pe_done, 1)
            weights_here("w_group")
            wg = ring[:, slot["w_group"], 0:2048].rearrange("p (g k n) -> p g k n", g=4, k=2)
            for nb in range(2):
                for t in range(NT):
                    b = begin(("mixed", nb, t))
                    for g in (2 * nb, 2 * nb + 1):
                        emptied(("pool", g))
                        for k in range(2):
                            last = pe.matmul(b[:, (g % 2) * S:(g % 2) * S + S], hT2[:, 2 * g + k, t * P:(t + 1) * P],
                                             wg[:, g, k, :], start=(k == 0), stop=(k == 1))
                    last.then_inc(pe_done, 1)
            turn("mixed", h, ready=lambda k: emptied(("mixed", k // 2, 1)))
            for nb in range(2):
                product("a_out", nb, ("a_out", nb), hT, KC, turned_by="mixed")

            def ple(l, before):
                name = f"ple{l}"
                weights_here(name)
                wp = weights(name, 2, D)
                for nb in range(2):
                    for t in range(NT):
                        b = begin((name, nb, t))
                        emptied(("pT", l))
                        for k in range(2):
                            last = pe.matmul(b[:, :], pT[:, l, k, t * P:(t + 1) * P],
                                             wp[:, k, nb * 512:(nb + 1) * 512], start=(k == 0), stop=(k == 1))
                        last.then_inc(pe_done, 1)
                turn(f"x{l}", x, ready=x_has(before))
                for nb in range(2):
                    product(f"gate{l}", nb, (f"gate{l}", nb), hT, KC, turned_by=f"x{l}")

            ple(0, "a_out")

            turn("b", x, ready=x_gated(0))
            for stage in ("k", "v"):
                for nb in range(2):
                    product(stage, nb, (stage, nb), hT, KC, turned_by="b")
            turn("k", k_tok, ready=lambda k: pe.wait_ge(heads_normed, 1))
            for stage in ("q", "zb"):
                for nb in range(2):
                    product(stage, nb, (stage, nb), hT2, KC, turned_by="b")
            turn("q", q_tok, ready=lambda k: pe.wait_ge(heads_normed, 2))
            pe.wait_ge(masks_ready, 4)
            for i in range(NH + 3):
                if i < NH:
                    b = begin(("logits", i))
                    c, p0 = i // 2, HD * (i % 2)
                    if i % 2 == 0:
                        emptied(("T", "q", c // 2))
                        emptied(("T", "k", c // 2))
                    pe.matmul(b[:, 0:S], kT[p0:p0 + HD, c, 0:P], qT[p0:p0 + HD, c, :], start=True, stop=False,
                              skip_group_check=True)
                    pe.matmul(b[:, S:S + P], kT[p0:p0 + HD, c, P:S], qT[p0:p0 + HD, c, P:S], start=False,
                              stop=False, skip_group_check=True)
                    pe.matmul(b[:, 0:P], bf[:, 0, :], bf[:, 1, :], start=False, stop=False, skip_group_check=True)
                    pe.matmul(b[:, S:S + P], bf[:, 0, :], bf[:, 1, :], start=False, stop=False,
                              skip_group_check=True).then_inc(pe_done, 1)
                if 2 <= i < NH + 2:
                    n = i - 2
                    b = bank(("loga", n))
                    pe.wait_ge(sp_ready, n + 1)
                    pe.matmul(b[:, 0:S], tneg, sps[:, n % 3, 0:S], start=False, stop=False, skip_group_check=True)
                    pe.matmul(b[:, P:S], allneg[:, :], sps[:, n % 3, S:S + P], start=False, stop=False,
                              skip_group_check=True)
                    pe.matmul(b[:, S:S + P], tneg, sps[:, n % 3, S:S + P], start=False, stop=True,
                              skip_group_check=True).then_inc(pe_done, 1)
                if i >= 3:
                    n = i - 3
                    b = begin(("stick_out", n // 4)) if n % 4 == 0 else bank(("stick_out", n // 4))
                    o = b[:, (n % 4) * P:(n % 4) * P + P]
                    emptied(("loga", n))
                    a = sticks[:, n % 3, :]
                    vh = v_tok[:, :, n * HD:(n + 1) * HD]
                    pe.matmul(o[:, 0:HD], a[:, 0:P], vh[:, 0, :], start=True, stop=True)
                    pe.matmul(o[:, HD:P], a[:, P:S], vh[:, 0, :], start=True, stop=False)
                    last = pe.matmul(o[:, HD:P], a[:, S:S + P], vh[:, 1, :], start=False, stop=True)
                    if n % 4 == 3:
                        last.then_inc(pe_done, 1)
            turn("o1", h, ready=lambda k: emptied(("stick_out", k)))
            for nb in range(2):
                product("b_out", nb, ("b_out", nb), hT, KC, turned_by="o1")
            ple(1, "b_out")

            turn("mix0", x, ready=x_gated(4))
            product("wc", 0, "wc", hT, KC, width=416, turned_by="mix0")
            product("wq", 0, "wq", hT, KC, turned_by="mix0")
            turn("c", cbuf, units=range(2), chunks=3, ready=lambda k: emptied(("wc", 0, 1)))
            for nb in range(2):
                product("uq", nb, "lowrank", cT, 2, width=384, turned_by="c",
                        at=weights("lowrank", 2, 768)[:, :, nb * 384:(nb + 1) * 384])
            for nb in range(2):
                weights_here("lowrank")
                wkv = ring[:, slot["lowrank"], 1536 + 512 * nb:2048 + 512 * nb]
                for t in range(NT):
                    b = begin(("ukv", nb, t))
                    emptied(("T", "c", 1))
                    pe.matmul(b[:, :], cT[:, 2, t * P:(t + 1) * P], wkv, start=True, stop=True).then_inc(pe_done, 1)
            product("wk", 0, "wk", hT, KC, turned_by="mix0")
            product("wv", 0, "wv", hT, KC, turned_by="mix0")
            for kind in ("moba", "mla"):
                moba = kind == "moba"
                tq, tk = turned_qk[kind]
                v_all = vb if moba else vm
                for which, src, normed in (("q", qb if moba else qm, 3 if moba else 4),
                                           ("k", kb if moba else km, 6 if moba else 5)):
                    turn(which + kind, src, units=range(2 if moba else 4), width=P if moba else MQK,
                         ready=lambda k: pe.wait_ge(heads_normed, normed))
                for i in range(MH + 3):
                    if i < MH:
                        b = begin(("scores", kind, i))
                        c, rows = (i // 2, slice(HD * (i % 2), HD * (i % 2) + HD)) if moba else (i, slice(0, MQK))
                        emptied(("T", "q" + kind, c // 2))
                        emptied(("T", "k" + kind, c // 2))
                        pe.matmul(b[:, 0:P], tq[rows, c, 0:P], tk[rows, c, 0:P], start=True, stop=False,
                                  skip_group_check=True)
                        pe.matmul(b[:, P:P + S], tq[rows, c, P:S], tk[rows, c, :], start=False, stop=False,
                                  skip_group_check=True)
                        pe.matmul(b[:, 0:P], bf[:, 0, :], bf[:, 2, :], start=False, stop=False,
                                  skip_group_check=True)
                        pe.matmul(b[:, S:S + P], bf[:, 0, :], bf[:, 2, :], start=False, stop=True,
                                  skip_group_check=True).then_inc(pe_done, 1)
                    if 2 <= i < MH + 2:
                        n = i - 2
                        b = begin(("probsT", kind, n))
                        emptied(("scores", kind, n))
                        for k in range(3):
                            last = pe.transpose(b[:, k * P:(k + 1) * P], probs[:, n % 3, k * P:(k + 1) * P], ident)
                        last.then_inc(pe_done, 1)
                    if i >= 3:
                        n = i - 3
                        name = ("soft_out", kind, n // 4)
                        b = begin(name) if n % 4 == 0 else bank(name)
                        o = b[:, (n % 4) * P:(n % 4) * P + P]
                        emptied(("probsT", kind, n))
                        a = probsT[:, n % 3, :]
                        vh = v_all[:, :, n * HD:(n + 1) * HD]
                        pe.matmul(o[:, 0:HD], a[:, 0:P], vh[:, 0, :], start=True, stop=True)
                        pe.matmul(o[:, HD:P], a[:, P:S], vh[:, 0, :], start=True, stop=False)
                        last = pe.matmul(o[:, HD:P], a[:, S:S + P], vh[:, 1, :], start=False, stop=True)
                        if n % 4 == 3:
                            last.then_inc(pe_done, 1)
            turn("o2", h, ready=lambda k: emptied(("soft_out", "mla" if k < 2 else "moba", k % 2)))
            for nb in range(2):
                product("w_o", nb, ("w_o", nb), hT, KC, turned_by="o2")

            def mlp(layer, ready):
                turn(("ffn", layer), x, ready=ready)
                acc = [ps[k] for k in range(4)]
                for i in range(FB + 2):
                    if i < FB:
                        product(("f1", layer, i), 0, ("f1", layer, i), hT, KC, turned_by=("ffn", layer))
                    if 1 <= i <= FB:
                        n = i - 1
                        for k in range(2):
                            b = begin(("fT", layer, n, k))
                            emptied((("f1", layer, n), 0, 1))
                            for cc in range(2):
                                for t in range(NT):
                                    c = 2 * k + cc
                                    last = pe.transpose(b[:, cc * S + t * P:cc * S + t * P + P],
                                                        hid[:, n % 2, t, c * P:(c + 1) * P], ident)
                            last.then_inc(pe_done, 1)
                    if layer == 0 and i == 1:
                        s5_coefficients()
                    if layer == 0 and i >= 2:
                        s5_chunk(i - 2)
                    if i >= 2:
                        n = i - 2
                        weights_here(("f2", layer, n))
                        w2 = weights(("f2", layer, n), 4, D)
                        for t in range(NT):
                            for nb in range(2):
                                if n == 0:
                                    begin(("acc", layer, 2 * t + nb))
                                for k in range(4):
                                    emptied(("fT", layer, n, k // 2))
                                    last = pe.matmul(acc[2 * t + nb][:, :], hidT[:, n % 2, k, t * P:(t + 1) * P],
                                                     w2[:, k, nb * 512:(nb + 1) * 512],
                                                     start=(n == 0 and k == 0), stop=(n == FB - 1 and k == 3))
                                if n == FB - 1:
                                    last.then_inc(pe_done, 1)
                        if n < FB - 1:
                            last.then_inc(f2_done, 1)

            def s5_coefficients():
                pe.wait_ge(powers_ready, 1)
                for k in range(3):
                    b = begin(("powT", k))
                    for q in range(8 * k, min(8 * k + 8, 20)):
                        last = pe.transpose(b[:, (q % 8) * G:(q % 8) * G + G],
                                            pw[:, q, :, :].rearrange("p r c -> p (r c)"), ident[0:G, 0:G])
                    last.then_inc(pe_done, 1)
                for k in range(8):
                    name = "rawB" if k < 4 else "rawC"
                    weights_here(name)
                    swapped = k // 2 % 2
                    raw = ring[0:G, slot[name], 0:3072]
                    b = begin(("bcT", k))
                    for i in range(8):
                        n = 8 * (k % 2) + i
                        v = raw.rearrange("p (rc i) -> p i rc", i=GI) if k < 4 else \
                            raw.rearrange("p (o rc) -> p o rc", o=GI)
                        last = pe.transpose(b[:, i * G:(i + 1) * G], v[:, n, GP * swapped:GP * swapped + P],
                                            ident[0:G, 0:G])
                    last.then_inc(pe_done, 1)

            def s5_chunk(f):
                pe.wait_ge(injects_made, f + 1)
                for k in range(2):
                    b = begin(("wT", f, k))
                    for g in range(4):
                        last = pe.transpose(b[:, g * P:(g + 1) * P],
                                            inject[:, 4 * k + g, :, :].rearrange("p j i -> p (j i)"), ident)
                    last.then_inc(pe_done, 1)
                pe.wait_ge(pads_filled, f + 1)
                pe.wait_ge(readouts_made, f + 1)
                b = begin(("taps", f))
                for g in range(8):
                    last = pe.matmul(b[:, 0:P], pads[:, g * P:(g + 1) * P],
                                     readout[:, g, 0:L, :].rearrange("p k o -> p (k o)"),
                                     start=(g == 0), stop=(g == 7))
                last.then_inc(pe_done, 1)

            mlp(0, x_has("w_o"))

            turn("mix1", h, ready=lambda k: pe.wait_ge(h_normed, 2))
            b = begin("gain_gi")
            pe.wait_ge(gain_rows_ready, 1)
            pe.transpose(b[:, 0:G], gain_rows[:, 1, :], ident[0:G, 0:G]).then_inc(pe_done, 1)
            for n in range(4):
                pe.wait_ge(regrouped_a if n < 2 else regrouped_b, 1)
                b = begin(("ug", n))
                for g in range(16):
                    f = 16 * n + g
                    last = pe.transpose(b[:, g * NC:(g + 1) * NC], xg[:, f].rearrange("p j i -> p (j i)"),
                                        ident[0:NC, 0:NC])
                last.then_inc(pe_done, 1)
            for n in range(4):
                b = begin(("inject", n))
                emptied(("ug", n))
                weights_here(("inject", n // 2))
                wi = weights(("inject", n // 2), 32, P)
                for g in range(16):
                    f = 16 * n + g
                    last = pe.matmul(b[:, g * NC:(g + 1) * NC], wi[:, f % 32, :], ug[:, f, :], start=True, stop=True)
                last.then_inc(pe_done, 1)
            for n in range(4):
                b = begin(("injectx", n))
                emptied(("inject", 3))
                pe.matmul(b[:, :], const("swap"),
                          states[:, 0, 1 + 8 * n:9 + 8 * n, :].rearrange("p c g -> p (c g)"),
                          start=True, stop=True).then_inc(pe_done, 1)
            for n in range(4):
                b = begin(("fir", n))
                emptied(("T", "mix1", n))
                weights_here(("taps", n // 2))
                wt = weights(("taps", n // 2), 32, P)
                for fl in range(2):
                    f = 2 * n + fl
                    src = hT[:, f, :].rearrange("p (c j) -> p c j", j=L)
                    dst = b[:, fl * S:(fl + 1) * S].rearrange("p (c j) -> p c j", j=L)
                    for k in range(L):
                        last = pe.matmul(dst[:, :, k:L], wt[:, (f % 4) * 8 + k, :], src[:, :, 0:L - k],
                                         start=(k == 0), stop=(k == L - 1), skip_group_check=True)
                last.then_inc(pe_done, 1)
            pe.wait_ge(states_ready, 1)
            for n in range(4):
                b = begin(("state_out", n))
                half, part = n // 2, n % 2
                weights_here(("readout", half))
                wr = weights(("readout", half), 32, P)
                for q in range(4):
                    for g in range(4):
                        f = 8 * q + 4 * part + g
                        last = pe.matmul(b[32 * q:32 * q + 32, g * P:(g + 1) * P], states[:, 0, 0:NC, 32 * half + f],
                                         wr[:, f, :], start=True, stop=True)
                last.then_inc(pe_done, 1)
            for n in range(4):
                b = begin(("state_outT", n))
                emptied(("state_out", 2 * (n // 2) + 1))
                for jj in range(4):
                    last = pe.transpose(b[:, jj * P:(jj + 1) * P], yc[:, n // 2, 4 * (n % 2) + jj, :], ident)
                last.then_inc(pe_done, 1)
            pe.wait_ge(gelu_ready, 4)
            for hh in range(2):
                for name in ("val", "gate"):
                    product((name, hh), 0, (name, hh), hT2, KC)
            mlp(1, x_gated(8))

        @block.scalar
        def _(act):
            steps_done = [0]

            def link(ins):
                steps_done[0] += 1
                ins.then_inc(act_step, 1)
                act.wait_ge(act_step, steps_done[0])

            def filled(name):
                act.wait_ge(pe_done, done(name))
                return bank(name)

            def copy_out(name, dst, src=None, scale=1.0, func=ACT.Copy):
                b = filled(name)
                act.activation(dst, b[:, :] if src is None else src, func, scale=scale).then_inc(act_emptied, 1)

            def turned_out(stage, pairs, units=(1, 3), width=P):
                for k in units:
                    b = filled(("T", stage, k))
                    for n, (dst, name, one) in enumerate(pairs):
                        if name is None:
                            ins = act.activation(dst[0:width, 2 * k:2 * k + 2, :].rearrange("p c s -> p (c s)"),
                                                 b[0:width, :], ACT.Copy)
                            continue
                        for cc in range(2):
                            c = 2 * k + cc
                            ins = act.activation(dst[0:width, c, :], b[0:width, cc * S:cc * S + S], ACT.Copy,
                                                 scale=gain(name, 0 if one else c, width))
                    ins.then_inc(act_emptied, 1)

            def squares_of_x(m):
                for t in range(NT):
                    act.wait_ge(ssq_ready, 2 * m + t)
                    act.activation(junk[:, :], x[:, t, :], ACT.Square, accum_out=ssq[:, m, t:t + 1]).then_inc(ssq_ready, 1)

            def root(m):
                act.wait_ge(rstd_ready, m + 1)

            def tokens_out(stage, nb, dst, m=None, func=ACT.Copy, width=512):
                for t in range(NT):
                    copy_out((stage, nb, t), dst[:, t, nb * width:(nb + 1) * width], bank((stage, nb, t))[:, 0:width],
                             1.0 if m is None else rstd[:, m, t:t + 1], func)

            act.dma_start(x[:, :, :], w["x"].rearrange("b (t p) n -> p (b t) n", p=P)).then_inc(x_landed, 16)
            act.dma_start(cst[:, :], w["tables"]).then_inc(tables_landed, 16)
            act.dma_start(vrows[:, :], w["vecs"]).then_inc(vecs_landed, 16)
            for l in range(2):
                act.dma_start(p_tok[:, l], w["p"][l, 0].rearrange("(t p) n -> p t n", p=P)).then_inc(p_landed, 16)
            act.dma_start(aux[:, 2048:2048 + NPOOL], w["pools"]).then_inc(pools_landed, 16)
            act.wait_ge(x_landed, 16)
            squares_of_x(0)
            act.wait_ge(gains_ready, 3)
            for l in range(2):
                copy_out(("pT", l), pT[:, l, :, :].rearrange("p c s -> p (c s)"))
            turned_out("a", [(hT, "a_norm", False)])
            root(0)
            for nb in range(2):
                tokens_out("u", nb, u_tok, 0)
            for nb in range(2):
                tokens_out("za", nb, z_tok, 0, ACT.Silu)
            for g in range(4):
                copy_out(("pool", g), hT2[:, 2 * g:2 * g + 2, :].rearrange("p c s -> p (c s)"))
            turned_out("mixed", [(hT, "a_scale", False)])
            for nb in range(2):
                tokens_out("ple0", nb, pl_tok)
            turned_out("x0", [(hT, None, False)])

            sigs = [0]

            def gate(name):
                b = filled(name)
                n = sigs[0]
                sigs[0] += 1
                if n >= 2:
                    act.wait_ge(x_updated, n - 1)
                act.activation(sig[:, n % 2, :], b[:, :], ACT.Sigmoid).then_inc(act_emptied, 1)

            for nb in range(2):
                for t in range(NT):
                    gate(("gate0", nb, t))
            turned_out("b", [(hT, "kv_norm", False), (hT2, "b_norm", False)])
            act.wait_ge(x_updated, 4)
            squares_of_x(1)
            root(1)
            for nb in range(2):
                tokens_out("k", nb, k_tok, 1)
            for nb in range(2):
                tokens_out("v", nb, v_tok, 1)
            turned_out("k", [(kT, "k_norm", True)])
            for nb in range(2):
                tokens_out("q", nb, q_tok, 1)
            for nb in range(2):
                tokens_out("zb", nb, z_tok, 1, ACT.Silu)
            turned_out("q", [(qT, "q_norm", True)])
            for i in range(NH + 3):
                if i < NH:
                    b = filled(("logits", i))
                    if i >= 3:
                        act.wait_ge(sp_ready, i - 2)
                    link(act.activation(logs[:, i % 3, :], b[:, 0:384], ACT.Abs))
                    link(act.activation(logs[:, i % 3, :], logs[:, i % 3, :], ACT.Exp, scale=-1.0))
                    act.activation(logs[:, i % 3, :], logs[:, i % 3, :], ACT.Ln, bias=1.0).then_inc(logs_ready, 1)
                if 2 <= i < NH + 2:
                    n = i - 2
                    b = filled(("loga", n))
                    act.activation(sticks[:, n % 3, :], b[:, 0:384], ACT.Exp).then_inc(act_emptied, 1)
            turned_out("o1", [(hT, None, False)])
            for nb in range(2):
                tokens_out("ple1", nb, pl_tok)
            turned_out("x1", [(hT, None, False)])
            for nb in range(2):
                for t in range(NT):
                    gate(("gate1", nb, t))
            turned_out("mix0", [(hT, "mix0", False)])
            act.wait_ge(x_updated, 8)
            squares_of_x(2)
            root(2)
            tokens_out("wc", 0, cbuf, 2, width=416)
            tokens_out("wq", 0, qb, 2)
            act.wait_ge(lowr_ready, 1)
            for nb in range(2):
                for t in range(NT):
                    copy_out(("uq", nb, t), qm[:, t, nb * 384:(nb + 1) * 384], bank(("uq", nb, t))[:, 0:384],
                             lowr[:, t:t + 1])
            for nb in range(2):
                for t in range(NT):
                    b = filled(("ukv", nb, t))
                    v = b[:, :].rearrange("p (h n) -> p h n", h=4)
                    kv = km[:, t, :].rearrange("p (h n) -> p h n", h=MH)
                    act.activation(kv[:, 4 * nb:4 * nb + 4, 0:MNOPE], v[:, :, 0:MNOPE], ACT.Copy, scale=lowr[:, 2 + t:3 + t])
                    act.activation(vm[:, t, 256 * nb:256 * nb + 256].rearrange("p (h n) -> p h n", h=4), v[:, :, MNOPE:P],
                                   ACT.Copy, scale=lowr[:, 2 + t:3 + t]).then_inc(act_emptied, 1)
            tokens_out("wk", 0, kb, 2)
            tokens_out("wv", 0, vb, 2)
            for n, kind in enumerate(("moba", "mla")):
                moba = kind == "moba"
                tq, tk = turned_qk[kind]
                for which, dst, name in (("q", tq, "qn_" + kind), ("k", tk, "kn_" + kind)):
                    turned_out(which + kind, [(dst, name, True)], units=(1,) if moba else (1, 3),
                               width=P if moba else MQK)
                for i in range(MH):
                    b = filled(("scores", kind, i))
                    act.wait_ge(max_ready, MH * n + i + 1)
                    if i >= 3:
                        act.wait_ge(pe_done, done(("probsT", kind, i - 3)))
                    act.activation(probs[:, i % 3, 0:P], b[:, 0:P], ACT.Exp, bias=nmax[:, n, i, 0:1],
                                   accum_out=den[:, n, i, 0:1])
                    act.activation(probs[:, i % 3, P:384], b[:, P:384], ACT.Exp, bias=nmax[:, n, i, 1:2],
                                   accum_out=den[:, n, i, 1:2]).then_inc(act_emptied, 1)
            turned_out("o2", [(hT, None, False)])

            def mlp(layer, m):
                turned_out(("ffn", layer), [(hT, f"ffn{layer}", False)])
                squares_of_x(m)
                if layer == 0:
                    act.wait_ge(lam_landed, 48)
                    act.activation(log_dt[:, 1:2], log_dt[:, 0:1], ACT.Exp).then_inc(dt_ready, 1)
                    act.wait_ge(zr_ready, 1)
                    act.activation(lam[:, 5, :], lam[:, 3, :], ACT.Exp).then_inc(exp_ready, 1)
                    act.wait_ge(angle_ready, 1)
                    act.activation(lam[:, 8:10, :], lam[:, 6:8, :], ACT.Sin).then_inc(sin_ready, 1)
                for i in range(FB + 2):
                    if 1 <= i <= FB:
                        n = i - 1
                        if n >= 2:
                            act.wait_ge(f2_done, (FB - 1) * layer + n - 1)
                        for k in range(2):
                            copy_out(("fT", layer, n, k), hidT[:, n % 2, 2 * k:2 * k + 2, :].rearrange("p c s -> p (c s)"),
                                     func=ACT.Square)
                    if layer == 0 and i == 1:
                        for k in range(3):
                            q = min(8, 20 - 8 * k)
                            copy_out(("powT", k), powT[:, 8 * k:8 * k + q, :].rearrange("p q g -> p (q g)"),
                                     bank(("powT", k))[:, 0:q * G])
                    if layer == 0 and i >= 2:
                        f = i - 2
                        if f:
                            act.wait_ge(w_stored, 16 * f)
                        for k in range(2):
                            copy_out(("wT", f, k), inject_T[:, 512 * k:512 * k + 512])

            mlp(0, 3)
            act.wait_ge(dve_emptied, u.emptied(("acc", 0, 3)))
            squares_of_x(4)
            act.wait_ge(h_normed, 2)
            act.wait_ge(v_stored, 16 * 8)
            for t in range(NT):
                for half in range(2):
                    act.dma_start(xc[half][16 * t:16 * t + 16, :, :],
                                  h[:, t, 512 * half:512 * half + 512]).then_inc(chunked[half], 16)
            turned_out("mix1", [(hT, "mix1", False)])
            act.wait_ge(chunked[1], 32)
            act.activation(xg[:, 32:64].rearrange("p g j i -> p j g i"),
                           xc[1].rearrange("p j (g i) -> p j g i", i=GI), ACT.Copy).then_inc(regrouped_b, 1)
            for n in range(4):
                b = filled(("inject", n))
                act.activation(states[:, 0, 1:NC + 1, 16 * n:16 * n + 16], b[:, :].rearrange("p (g c) -> p c g", g=16),
                               ACT.Copy).then_inc(act_emptied, 1)
            for n in range(4):
                copy_out(("injectx", n), states[:, 1, 1 + 8 * n:9 + 8 * n, :].rearrange("p c g -> p (c g)"))
            for n in range(4):
                b = filled(("state_out", n))
                dst = yc[:, n // 2, :, 64 * (n % 2):64 * (n % 2) + 64].rearrange("p j (g o) -> p j g o", g=4)
                act.activation(dst, b[:, :].rearrange("p (g j o) -> p j g o", g=4, j=L), ACT.Copy).then_inc(act_emptied, 1)
            for n in range(4):
                act.wait_ge(dve_emptied, u.emptied(("state_outT", 2 * (n // 2) + 1)))
                act.activation(hT2[:, 2 * n:2 * n + 2, :], ybuf[:, 2 * n:2 * n + 2, :], ACT.Gelu_apprx_tanh)\
                    .then_inc(gelu_ready, 1)
            for hh in range(2):
                for t in range(NT):
                    gate((("gate", hh), 0, t))
            mlp(1, 5)

        @block.vector
        def _(dve):
            steps_done = [0]

            def link(ins):
                steps_done[0] += 1
                ins.then_inc(dve_step, 1)
                dve.wait_ge(dve_step, steps_done[0])

            def filled(name):
                dve.wait_ge(pe_done, done(name))
                return bank(name)

            def emptied(name):
                dve.wait_ge(act_emptied, u.emptied(name))

            def turned_out(stage, pairs, units=(0, 2), width=P, chunks=8):
                for k in units:
                    b = filled(("T", stage, k))
                    for n, (dst, name, one) in enumerate(pairs):
                        if name is None:
                            ins = dve.tensor_copy(dst[0:width, 2 * k:2 * k + 2, :].rearrange("p c s -> p (c s)"),
                                                  b[0:width, :])
                            continue
                        for cc in range(min(2, chunks - 2 * k)):
                            c = 2 * k + cc
                            ins = dve.tensor_scalar(dst[0:width, c, :], b[0:width, cc * S:cc * S + S],
                                                    gain(name, 0 if one else c, width), None, ALU.mult)
                    ins.then_inc(dve_emptied, 1)

            def means(m):
                dve.wait_ge(ssq_ready, 2 * m + 2)
                dve.tensor_scalar(ms[:, m, :], ssq[:, m, :], 1.0 / D, EPS, ALU.mult, ALU.add).then_inc(ms_ready, 1)

            def add_to_x(stage, nb_at, nb, t):
                b = filled((stage, nb, t))
                xs = x[:, t, nb_at * 512:(nb_at + 1) * 512]
                dve.tensor_tensor(xs, xs, b[:, :], ALU.add).then_inc(dve_emptied, 1)

            dve.memset(allneg[:, :], -1.0).then_inc(masks_ready, 1)
            dve.wait_ge(tables_landed, 16)
            dve.tensor_copy(bf[:, 0, :], ident).then_inc(masks_ready, 1)
            dve.tensor_copy(bf[:, 1, :], const("mask_st")).then_inc(masks_ready, 1)
            dve.tensor_copy(bf[:, 2, :], const("mask_ts")).then_inc(masks_ready, 1)
            b = filled("vec")
            dve.tensor_copy(vcols[:, :], b[:, 0:NVEC]).then_inc(dve_emptied, 1)
            dve.wait_ge(dve_emptied, 1)
            for name, scale in (("q_norm", HD ** -0.5), ("qn_moba", HD ** -0.5), ("qn_mla", MQK ** -0.5)):
                dve.tensor_scalar(gain(name), gain(name), scale, None, ALU.mult).then_inc(gains_ready, 1)
            dve.wait_ge(gains_ready, 3)
            means(0)
            turned_out("a", [(hT, "a_norm", False)])
            for nb in range(2):
                for t in range(NT):
                    b = filled(("mixed", nb, t))
                    emptied(("za", nb, t))
                    dve.tensor_tensor(h[:, t, nb * 512:(nb + 1) * 512], b[:, :], z_tok[:, t, nb * 512:(nb + 1) * 512],
                                      ALU.mult).then_inc(dve_emptied, 1)
            turned_out("mixed", [(hT, "a_scale", False)])
            for nb in range(2):
                for t in range(NT):
                    add_to_x("a_out", nb, nb, t)

            gates = [0]

            def gate_in(name, t, nb, other, free):
                n = gates[0]
                gates[0] += 1
                emptied(name)
                s = sig[:, n % 2, :]
                ins = dve.tensor_tensor(s, s, other, ALU.mult)
                if free:
                    ins.then_inc(dve_emptied, 1)
                    dve.wait_ge(dve_emptied, u.emptied(free))
                else:
                    link(ins)
                xs = x[:, t, nb * 512:(nb + 1) * 512]
                dve.tensor_tensor(xs, xs, s, ALU.add).then_inc(x_updated, 1)

            turned_out("x0", [(hT, None, False)])
            for nb in range(2):
                for t in range(NT):
                    gate_in(("gate0", nb, t), t, nb, pl_tok[:, t, nb * 512:(nb + 1) * 512], None)
            turned_out("b", [(hT, "kv_norm", False), (hT2, "b_norm", False)])
            means(1)

            def norm_heads(buf, n, width):
                sq = squares[:, 0:n * width].rearrange("p (n c) -> p n c", n=n)
                k = headnorms[0] = headnorms[0] + 1
                link(dve.tensor_tensor(sq, buf, buf, ALU.mult))
                link(dve.tensor_reduce(ssh[:, 0:n], sq, AX_X, ALU.add))
                dve.tensor_scalar(msh[:, 0:n], ssh[:, 0:n], 1.0 / width, EPS, ALU.mult, ALU.add).then_inc(headms_ready, 1)
                dve.wait_ge(headr_ready, k)
                dve.tensor_tensor(buf, buf, rsh[:, 0:n].unsqueeze(2).broadcast_to([P, n, width]), ALU.mult)\
                    .then_inc(heads_normed, 1)

            headnorms = [0]
            emptied(("k", 1, 1))
            norm_heads(work[:, 2048:4096].rearrange("p (n c) -> p n c", c=HD), NT * NH, HD)
            turned_out("k", [(kT, "k_norm", True)])
            emptied(("q", 1, 1))
            norm_heads(work[:, 0:2048].rearrange("p (n c) -> p n c", c=HD), NT * NH, HD)
            turned_out("q", [(qT, "q_norm", True)])
            emptied(("zb", 1, 1))
            for i in range(NH + 3):
                if i < NH:
                    b = bank(("logits", i))
                    dve.wait_ge(logs_ready, i + 1)
                    dve.scalar_tensor_tensor(out=sps[:, i % 3, :], in0=b[:, 0:384], scalar=0.0, in1=logs[:, i % 3, :],
                                             op0=ALU.max, op1=ALU.add).then_inc(sp_ready, 1)
                if i >= 3 and (i - 3) % 4 == 3:
                    k = (i - 3) // 4
                    b = filled(("stick_out", k))
                    hv, zv = (a[:, :, 256 * k:256 * k + 256].rearrange("p t (n d) -> p n t d", d=HD) for a in (h, z_tok))
                    dve.tensor_tensor(hv, b[:, :].rearrange("p (n t d) -> p n t d", n=4, t=NT), zv, ALU.mult)\
                        .then_inc(dve_emptied, 1)
            turned_out("o1", [(hT, None, False)])
            for nb in range(2):
                for t in range(NT):
                    add_to_x("b_out", nb, nb, t)
            turned_out("x1", [(hT, None, False)])
            for nb in range(2):
                for t in range(NT):
                    gate_in(("gate1", nb, t), t, nb, pl_tok[:, t, nb * 512:(nb + 1) * 512], None)

            turned_out("mix0", [(hT, "mix0", False)])
            means(2)
            emptied(("wc", 0, 1))
            sq = squares[:, 0:768].rearrange("p (t n) -> p t n", t=NT)
            link(dve.tensor_tensor(sq, cbuf[:, :, 0:384], cbuf[:, :, 0:384], ALU.mult))
            link(dve.tensor_reduce(lowss[:, 0:2], sq[:, :, 0:256], AX_X, ALU.add))
            link(dve.tensor_reduce(lowss[:, 2:4], sq[:, :, 256:384], AX_X, ALU.add))
            dve.tensor_scalar(lowms[:, 0:2], lowss[:, 0:2], 1.0 / 256, EPS, ALU.mult, ALU.add).then_inc(lowms_ready, 1)
            dve.tensor_scalar(lowms[:, 2:4], lowss[:, 2:4], 1.0 / 128, EPS, ALU.mult, ALU.add).then_inc(lowms_ready, 1)
            turned_out("c", [(cT, "g_cq", False)], units=(0, 1), chunks=3)
            emptied(("wq", 0, 1))
            norm_heads(work[:, 4096:5120].rearrange("p (n c) -> p n c", c=HD), NT * MH, HD)

            def rotate(a1, a2, out1, out2, n, spread):
                cs, sn = (const(name).rearrange("p (t c) -> p t c", t=NT) for name in ("cos", "sin"))
                part = [ropes[:, k, :, 0:n, :] for k in range(4)]
                if n > 1:
                    cs, sn = (a.unsqueeze(2).broadcast_to([P, NT, n, 16]) for a in (cs, sn))
                else:
                    part = [a[:, :, 0, :] for a in part]
                for o, a, c in zip(part, (a1, a2, a1, a2), (cs, sn, sn, cs)):
                    ins = dve.tensor_tensor(o, a, c, ALU.mult)
                link(ins)
                if spread:
                    part = [a.unsqueeze(2).broadcast_to([P, NT, MH, 16]) for a in part]
                dve.tensor_tensor(out1, part[0], part[1], ALU.subtract)
                link(dve.tensor_tensor(out2, part[2], part[3], ALU.add))

            emptied(("uq", 1, 1))
            qh = qm.rearrange("p t (h c) -> p t h c", h=MH)
            rotate(qh[:, :, :, 64:80], qh[:, :, :, 80:96], qh[:, :, :, 64:80], qh[:, :, :, 80:96], MH, False)
            norm_heads(work[:, 0:1536].rearrange("p (n c) -> p n c", c=MQK), NT * MH, MQK)
            emptied(("ukv", 1, 1))
            kh = km.rearrange("p t (h c) -> p t h c", h=MH)
            rotate(cbuf[:, :, 384:400], cbuf[:, :, 400:416], kh[:, :, :, 64:80], kh[:, :, :, 80:96], 1, True)
            norm_heads(work[:, 1536:3072].rearrange("p (n c) -> p n c", c=MQK), NT * MH, MQK)
            emptied(("wk", 0, 1))
            norm_heads(work[:, 5120:6144].rearrange("p (n c) -> p n c", c=HD), NT * MH, HD)
            for n, kind in enumerate(("moba", "mla")):
                moba = kind == "moba"
                tq, tk = turned_qk[kind]
                for which, dst, name in (("q", tq, "qn_" + kind), ("k", tk, "kn_" + kind)):
                    turned_out(which + kind, [(dst, name, True)], units=(0,) if moba else (0, 2),
                               width=P if moba else MQK)
                for i in range(MH + 3):
                    if i < MH:
                        b = filled(("scores", kind, i))
                        dve.tensor_reduce(nmax[:, n, i, 0:1], b[:, 0:P], AX_X, ALU.max, negate=True)
                        dve.tensor_reduce(nmax[:, n, i, 1:2], b[:, P:384], AX_X, ALU.max, negate=True)\
                            .then_inc(max_ready, 1)
                    if 2 <= i < MH + 2:
                        b = filled(("probsT", kind, i - 2))
                        dve.tensor_copy(probsT[:, (i - 2) % 3, :], b[:, 0:384]).then_inc(dve_emptied, 1)
                    if i >= 3 and (i - 3) % 4 == 3:
                        k = (i - 3) // 4
                        b = filled(("soft_out", kind, k))
                        emptied(("scores", kind, 4 * k + 3))
                        link(dve.reciprocal(rden[:, n, 4 * k:4 * k + 4, :], den[:, n, 4 * k:4 * k + 4, :]))
                        at = (512 if moba else 0) + 256 * k
                        dve.tensor_tensor(h[:, :, at:at + 256].rearrange("p t (n d) -> p n t d", d=HD),
                                          b[:, :].rearrange("p (n t d) -> p n t d", n=4, t=NT),
                                          rden[:, n, 4 * k:4 * k + 4, :].unsqueeze(3).broadcast_to([P, 4, NT, HD]),
                                          ALU.mult).then_inc(dve_emptied, 1)
            turned_out("o2", [(hT, None, False)])
            for nb in range(2):
                for t in range(NT):
                    add_to_x("w_o", nb, nb, t)

            def s5_powers():
                tau = 2 * np.pi
                c1 = 6.28125
                c2 = float(np.float32(np.round((tau - c1) * 2 ** 20) / 2 ** 20))
                c3 = float(np.float32(tau - c1 - c2))
                magic = 12582912.0
                lr, li = lam[:, 0, :], lam[:, 1, :]
                dve.wait_ge(dt_ready, 1)
                dve.wait_ge(lam_landed, 48)
                dt = log_dt[:, 1:2]
                dve.tensor_scalar(lam[:, 3, :], lr, dt, None, ALU.mult).then_inc(zr_ready, 1)
                link(dve.tensor_scalar(lam[:, 4, :], li, dt, 0.5, ALU.mult, ALU.mult))
                link(dve.tensor_scalar(lam[:, 10, :], lam[:, 4, :], 0.5 * np.pi, None, ALU.add))
                for a, o in ((lam[:, 4, :], lam[:, 6, :]), (lam[:, 10, :], lam[:, 7, :])):
                    turns = lam[:, 11, :]
                    link(dve.tensor_scalar(turns, a, 1 / tau, magic, ALU.mult, ALU.add))
                    link(dve.tensor_scalar(turns, turns, magic, None, ALU.subtract))
                    link(dve.scalar_tensor_tensor(out=o, in0=turns, scalar=-c1, in1=a, op0=ALU.mult, op1=ALU.add))
                    link(dve.scalar_tensor_tensor(out=o, in0=turns, scalar=-c2, in1=o, op0=ALU.mult, op1=ALU.add))
                    link(dve.scalar_tensor_tensor(out=o, in0=turns, scalar=-c3, in1=o, op0=ALU.mult, op1=ALU.add))
                    ins = dve.tensor_scalar(o, o, 3.1415925, -3.1415925, ALU.min, ALU.max)
                    link(ins)
                dve.tensor_copy(lam[:, 12, :], lam[:, 4, :]).then_inc(angle_ready, 1)
                dve.wait_ge(sin_ready, 1)
                dve.wait_ge(exp_ready, 1)
                e, sn, co = lam[:, 5, :], lam[:, 8, :], lam[:, 9, :]
                s2, es, es2, e1, cosv = (lam[:, n, :] for n in (12, 13, 14, 15, 16))
                link(dve.tensor_tensor(s2, sn, sn, ALU.mult))
                dve.tensor_tensor(es, e, sn, ALU.mult)
                dve.tensor_tensor(es2, e, s2, ALU.mult)
                dve.tensor_scalar(e1, e, -1.0, None, ALU.add)
                link(dve.tensor_scalar(cosv, s2, -2.0, 1.0, ALU.mult, ALU.add))
                re, im = powers[:, 0], powers[:, 1]
                dve.tensor_tensor(re[:, 0, :], e, cosv, ALU.mult)
                dve.scalar_tensor_tensor(out=im[:, 0, :], in0=es, scalar=2.0, in1=co, op0=ALU.mult, op1=ALU.mult)
                num = lam[:, 17, :]
                link(dve.scalar_tensor_tensor(out=num, in0=es2, scalar=-2.0, in1=e1, op0=ALU.mult, op1=ALU.add))
                a, b2, c, d, e2 = (lam[:, n, :] for n in (18, 19, 20, 21, 3))
                dve.tensor_tensor(a, lr, lr, ALU.mult)
                dve.tensor_tensor(b2, li, li, ALU.mult)
                dve.tensor_tensor(c, num, lr, ALU.mult)
                dve.tensor_tensor(d, im[:, 0, :], li, ALU.mult)
                link(dve.tensor_tensor(e2, im[:, 0, :], lr, ALU.mult))
                dve.tensor_tensor(lam[:, 4, :], num, li, ALU.mult)
                dve.tensor_tensor(a, a, b2, ALU.add)
                link(dve.tensor_tensor(c, c, d, ALU.add))
                link(dve.reciprocal(b2, a))
                link(dve.tensor_tensor(e2, e2, lam[:, 4, :], ALU.subtract))
                dve.tensor_tensor(pw[:, 18, 0, :], c, b2, ALU.mult)
                dve.tensor_tensor(pw[:, 18, 1, :], c, b2, ALU.mult)
                dve.tensor_tensor(pw[:, 19, 1, :], e2, b2, ALU.mult)
                for m in (1, 2, 4):
                    ar, ai = re[:, 0:m, :], im[:, 0:m, :]
                    br, bi = (v[:, m - 1:m, :].broadcast_to([G, m, GP]) for v in (re, im))
                    for n, (p1, p2) in enumerate(((ar, br), (ai, bi), (ar, bi), (ai, br))):
                        ins = dve.tensor_tensor(prods[:, n, 0:m, :], p1, p2, ALU.mult)
                    link(ins)
                    dve.tensor_tensor(re[:, m:2 * m, :], prods[:, 0, 0:m, :], prods[:, 1, 0:m, :], ALU.subtract)
                    link(dve.tensor_tensor(im[:, m:2 * m, :], prods[:, 2, 0:m, :], prods[:, 3, 0:m, :], ALU.add))
                dve.tensor_scalar(pw[:, 19, 0, :], pw[:, 19, 1, :], -1.0, None, ALU.mult)
                dve.memset(pw[:, 0, :, :], 1.0)
                dve.memset(pw[:, 9, :, :], 0.0)
                dve.tensor_copy(pw[:, 1:9, 0, :], re)
                dve.tensor_copy(pw[:, 1:9, 1, :], re)
                dve.tensor_scalar(pw[:, 10:18, 0, :], im, -1.0, None, ALU.mult)
                dve.tensor_copy(pw[:, 10:18, 1, :], im).then_inc(powers_ready, 1)

            def s5_inputs():
                sgn = const("sgn")[:, 0:1]
                for k in range(8):
                    b = filled(("bcT", k))
                    dst = (Bs, Bx, Cs, Cx)[k // 2][:, 8 * (k % 2):8 * (k % 2) + 8, :].rearrange("p i g -> p (i g)")
                    if k < 4:
                        dve.tensor_copy(dst, b[:, :]).then_inc(dve_emptied, 1)
                    else:
                        dve.tensor_scalar(dst, b[:, :], sgn, None, ALU.mult).then_inc(dve_emptied, 1)
                emptied(("powT", 2))
                dve.wait_ge(dve_emptied, u.emptied(("bcT", 7)))
                fr, fi = (powT[:, q, :].unsqueeze(1).broadcast_to([P, GI, G]) for q in (18, 19))
                m1, m2, m3 = (v[:, 0:1024].rearrange("p (i g) -> p i g", i=GI) for v in (t1, t2, work[:, 0:1024]))
                dve.tensor_tensor(m1, Bs, fr, ALU.mult)
                dve.tensor_tensor(m2, Bx, fi, ALU.mult)
                link(dve.tensor_tensor(m3, Bs, fi, ALU.mult))
                link(dve.tensor_tensor(Bs, m1, m2, ALU.add))
                link(dve.tensor_tensor(m1, Bx, fr, ALU.mult))
                dve.tensor_tensor(Bx, m1, m3, ALU.subtract).then_inc(inputs_scaled, 1)
                dve.wait_ge(inputs_scaled, 1)
                dve.tensor_copy(a8[:, 0, :], powT[:, 8, :])
                dve.tensor_copy(a8[:, 1, :], powT[:, 17, :])
                dve.tensor_scalar(a8[:, 2, :], powT[:, 17, :], -1.0, None, ALU.mult)

            def s5_inject(f):
                if f:
                    dve.wait_ge(pe_done, done(("taps", f - 1)))
                gs = slice(8 * f, 8 * f + 8)
                ar, ai = (powT[:, q:q + 8, gs][:, ::-1, :].rearrange("p q g -> p g q").unsqueeze(3)
                          .broadcast_to([P, 8, L, GI]) for q in (0, 9))
                bs, bx = (v[:, :, gs].rearrange("p i g -> p g i").unsqueeze(2).broadcast_to([P, 8, L, GI])
                          for v in (Bs, Bx))
                m1, m2 = (v[:, 0:1024].rearrange("p (g j i) -> p g j i", g=8, j=L) for v in (t1, t2))
                dve.tensor_tensor(m1, ar, bs, ALU.mult)
                link(dve.tensor_tensor(m2, ai, bx, ALU.mult))
                dve.tensor_tensor(inject, m1, m2, ALU.add).then_inc(injects_made, 1)
                dve.wait_ge(pads_zeroed, 1)
                diagonal = work[:, 9856:9856 + 8 * 144].rearrange("p (g n) -> p g n", n=144)[:, :, 0:GI]
                dve.tensor_copy(diagonal, Bs[:, :, gs].rearrange("p i g -> p g i")).then_inc(pads_filled, 1)

            def s5_taps(f):
                b = filled(("taps", f))
                if f:
                    dve.wait_ge(t_stored, 16 * f)
                dve.tensor_tensor(taps.rearrange("p (k g o) -> p k g o", k=L, g=8),
                                  b[:, 0:P].rearrange("p (k o) -> p k o", k=L).unsqueeze(2).broadcast_to([P, L, 8, GI]),
                                  const("bmask").rearrange("p (g o) -> p g o", g=8).unsqueeze(1)
                                  .broadcast_to([P, L, 8, GI]), ALU.mult).then_inc(dve_emptied, 1)

            def mlp(layer, m):
                turned_out(("ffn", layer), [(hT, f"ffn{layer}", False)])
                means(m)
                for i in range(FB + 2):
                    if i < FB:
                        for t in range(NT):
                            b = filled((("f1", layer, i), 0, t))
                            dve.wait_ge(rstd_ready, m + 1)
                            dve.tensor_scalar(hid[:, i % 2, t, :], b[:, :], rstd[:, m, t:t + 1], 0.0, ALU.mult, ALU.max)\
                                .then_inc(dve_emptied, 1)
                    if layer == 0:
                        if i == 0:
                            s5_powers()
                        if i == 1:
                            s5_inputs()
                        if i >= 2:
                            s5_taps(i - 2)
                        if 1 <= i <= FB:
                            s5_inject(i - 1)
                for t in range(NT):
                    for nb in range(2):
                        b = filled(("acc", layer, 2 * t + nb))
                        xs = x[:, t, nb * 512:(nb + 1) * 512]
                        dve.tensor_tensor(xs, xs, b[:, :], ALU.add).then_inc(dve_emptied, 1)

            mlp(0, 3)

            means(4)
            dve.wait_ge(gain_landed, 16)
            dve.tensor_copy(gain_rows[:, 1, :].rearrange("p (j i) -> p j i", j=L),
                            gain_rows[:, 0, 0:GI].unsqueeze(1).broadcast_to([G, L, GI])).then_inc(gain_rows_ready, 1)
            dve.wait_ge(rstd_ready, 5)
            for t in range(NT):
                dve.tensor_scalar(h[:, t, :], x[:, t, :], rstd[:, 4, t:t + 1], None, ALU.mult).then_inc(h_normed, 1)
            turned_out("mix1", [(hT, "mix1", False)])
            dve.wait_ge(chunked[0], 32)
            dve.tensor_copy(xg[:, 0:32].rearrange("p g j i -> p j g i"),
                            xc[0].rearrange("p j (g i) -> p j g i", i=GI)).then_inc(regrouped_a, 1)
            b = filled("gain_gi")
            dve.tensor_copy(gain_gi[:, :], b[:, 0:G]).then_inc(dve_emptied, 1)
            dve.wait_ge(dve_emptied, u.emptied("gain_gi"))
            dve.wait_ge(w_stored, 16 * 8)
            dve.wait_ge(t_stored, 16 * 8)
            for n in range(4):
                b = filled(("ug", n))
                dve.tensor_tensor(ug[:, 16 * n:16 * n + 16, :], b[:, :].rearrange("p (g c) -> p g c", g=16),
                                  gain_gi[:, 16 * n:16 * n + 16].unsqueeze(2).broadcast_to([P, 16, NC]),
                                  ALU.mult).then_inc(dve_emptied, 1)
            link(dve.memset(states[:, :, 0, :], 0.0))
            emptied(("injectx", 3))
            ar = a8[:, 0:1, :].broadcast_to([P, 2, G])
            for c in range(2, NC):
                before, now = states[:, :, c - 1, :], states[:, :, c, :]
                dve.tensor_tensor(steps[:, 0], ar, before, ALU.mult)
                link(dve.tensor_tensor(steps[:, 1], a8[:, 1:3, :], before[:, ::-1, :], ALU.mult))
                link(dve.tensor_tensor(steps[:, 0], steps[:, 0], steps[:, 1], ALU.add))
                ins = dve.tensor_tensor(now, now, steps[:, 0], ALU.add)
                if c < NC - 1:
                    link(ins)
            ins.then_inc(states_ready, 1)
            for n in range(4):
                b = filled(("fir", n))
                for fl in range(2):
                    f = 2 * n + fl
                    ins = dve.scalar_tensor_tensor(out=ybuf[:, f, :], in0=hT[:, f, :], scalar=gain("d_skip", f),
                                                   in1=b[:, fl * S:(fl + 1) * S], op0=ALU.mult, op1=ALU.add)
                ins.then_inc(dve_emptied, 1)
            for n in range(4):
                b = filled(("state_outT", n))
                dve.wait_ge(dve_emptied, u.emptied(("fir", 2 * (n // 2) + 1)))
                yv = ybuf[:, 4 * (n // 2):4 * (n // 2) + 4, :].rearrange("p c s -> p (c s)")\
                    .rearrange("p (n j) -> p n j", j=L)[:, :, 4 * (n % 2):4 * (n % 2) + 4]
                dve.tensor_tensor(yv, yv, b[:, :].rearrange("p (j n) -> p n j", j=4), ALU.add).then_inc(dve_emptied, 1)
            for hh in range(2):
                for t in range(NT):
                    gate_in((("gate", hh), 0, t), t, hh, bank((("val", hh), 0, t))[:, :], (("val", hh), 0, t))
            mlp(1, 5)

        @block.gpsimd
        def _(pool):
            pool.memset(half_neg[:, :], -0.5).then_inc(halves_ready, 1)
            pool.dma_start(gain_rows[:, 0, 0:GI], w["mix_norm_g_2"][1].rearrange("(g i) -> g i", i=GI))\
                .then_inc(gain_landed, 16)
            pool.wait_ge(halves_ready, 1)

            def root(m):
                pool.wait_ge(ms_ready, m + 1)
                pool.tensor_tensor(rstd[:, m, :], ms[:, m, :], half_neg[:, 0:NT], ALU.pow).then_inc(rstd_ready, 1)

            def head_root(k, n):
                pool.wait_ge(headms_ready, k)
                pool.tensor_tensor(rsh[:, 0:n], msh[:, 0:n], half_neg[:, 0:n], ALU.pow).then_inc(headr_ready, 1)

            root(0)
            root(1)
            head_root(1, NT * NH)
            head_root(2, NT * NH)
            root(2)
            pool.wait_ge(lowms_ready, 2)
            pool.tensor_tensor(lowr[:, :], lowms[:, :], half_neg[:, 0:4], ALU.pow).then_inc(lowr_ready, 1)
            for k in range(3, 7):
                head_root(k, NT * MH)
            root(3)
            pool.wait_ge(pe_done, done(("soft_out", "mla", 1)))
            pool.dma_start(lam[:, 0, :], w["lam_re_2"][0]).then_inc(lam_landed, 16)
            pool.dma_start(lam[:, 1, :], w["lam_im_2"][0]).then_inc(lam_landed, 16)
            pool.dma_start(log_dt[:, 0:1], w["log_dt_2"][0].rearrange("(g a) -> g a", a=1)).then_inc(lam_landed, 16)
            pool.memset(pads, 0.0).then_inc(pads_zeroed, 1)
            pool.wait_ge(inputs_scaled, 1)
            stored = 0
            for f in range(8):
                gs = slice(8 * f, 8 * f + 8)
                if f:
                    pool.wait_ge(pe_done, done(("taps", f - 1)))
                    pool.wait_ge(v_stored, 16 * f)
                ar, ai = (powT[:, q:q + 9, gs].rearrange("p q g -> p g q").unsqueeze(3)
                          .broadcast_to([P, 8, L + 1, GI]) for q in (0, 9))
                cs, cx = (v[:, :, gs].rearrange("p i g -> p g i").unsqueeze(2).broadcast_to([P, 8, L + 1, GI])
                          for v in (Cs, Cx))
                tmp = t3.rearrange("p (g k o) -> p g k o", g=8, k=L + 1)
                pool.tensor_tensor(readout, ar, cs, ALU.mult).then_inc(pool_step, 1)
                pool.tensor_tensor(tmp, ai, cx, ALU.mult).then_inc(pool_step, 1)
                pool.wait_ge(pool_step, 2 * f + 2)
                pool.tensor_tensor(readout, readout, tmp, ALU.add).then_inc(readouts_made, 1)
                pool.wait_ge(readouts_made, f + 1)
                pool.dma_start(w["scratch_readout"][:, 1024 * f:1024 * f + 1024].rearrange("p (g n) -> p g n", g=8),
                               readout[:, :, 1:L + 1, :].rearrange("p g k o -> p g (k o)")).then_inc(v_stored, 16)
                pool.wait_ge(act_emptied, u.emptied(("wT", f, 1)))
                pool.dma_start(w["scratch_inject"][:, 1024 * f:1024 * f + 1024], inject_T).then_inc(w_stored, 16)
                pool.wait_ge(dve_emptied, u.emptied(("taps", f)))
                pool.dma_start(w["scratch_taps"][:, 1024 * f:1024 * f + 1024], taps).then_inc(t_stored, 16)
            root(4)
            root(5)


_INS = ["x", "p", "a_w_in", "a_w_group", "a_w_out", "w_kv", "b_w_in", "b_w_out", "ple_w", "ple_gate_w", "mix_norm_g_2",
        "w_in_2", "w_uq_2", "w_ukv_2", "w_o_2", "lam_re_2", "lam_im_2", "log_dt_2", "b_re_2", "b_im_2", "c_re_2",
        "c_im_2", "w_glu_2", "w_ff1_2", "w_ff2_2"]


def kernel(**inputs):
    import numpy as np
    import concourse.bacc as bacc
    from concourse.bass_utils import run_bass_kernel_spmd

    vecs = np.zeros((NVEC, P), np.float32)
    for name, v in (("a_norm", inputs["a_norm"][0]), ("a_scale", inputs["a_scale"][0]), ("kv_norm", inputs["kv_norm"]),
                    ("b_norm", inputs["b_norm"][0]), ("mix0", inputs["mix_norm_g_2"][0]),
                    ("mix1", inputs["mix_norm_g_2"][1]), ("ffn0", inputs["ffn_norm_g_2"][0]),
                    ("ffn1", inputs["ffn_norm_g_2"][1]), ("d_skip", inputs["d_skip_2"][0]),
                    ("g_cq", inputs["g_cq_2"][0]), ("g_ckv", inputs["g_ckv_2"][0]), ("k_norm", inputs["k_norm"]),
                    ("q_norm", inputs["b_q_norm"][0]), ("qn_mla", inputs["g_qn_mla_2"][0]),
                    ("kn_mla", inputs["g_kn_mla_2"][0]), ("qn_moba", inputs["g_qn_moba_2"][0]),
                    ("kn_moba", inputs["g_kn_moba_2"][0])):
        v = np.asarray(v)
        if v.size == HD:
            v = np.concatenate([v, v])
        if v.size % P:
            v = np.concatenate([v, np.zeros(-v.size % P, np.float32)])
        vecs[VEC_AT[name]:VEC_AT[name] + VEC_ROWS[name]] = v.reshape(-1, P)
    tables, pools = constants()

    nc = bacc.Bacc("TRN2", target_bir_lowering=False, num_devices=1)
    arrays, w = {}, {}
    given = {name: np.ascontiguousarray(inputs[name]) for name in _INS}
    for name, a in {**given, "vecs": vecs, "tables": tables, "pools": pools}.items():
        arrays[f"in_{name}"] = a
        w[name] = nc.dram_tensor(f"in_{name}", a.shape, mybir.dt.from_np(a.dtype), kind="ExternalInput").ap()
    for name in ("inject", "readout", "taps"):
        w["scratch_" + name] = nc.dram_tensor("scratch_" + name, (P, 2 * BLK), F32, kind="Internal").ap()
    out = nc.dram_tensor("out_0", (1, S, D), F32, kind="ExternalOutput").ap()
    program(nc, w, out)
    r = run_bass_kernel_spmd(nc, [arrays], core_ids=[0])
    return r.results[0]["out_0"]
```

```python
from contextlib import ExitStack

import concourse.bass as bass
from concourse import mybir

F32 = mybir.dt.float32
BF16 = mybir.dt.bfloat16
F32R = mybir.dt.float32r
ALU = mybir.AluOpType
ACT = mybir.ActivationFunctionType
AX_X = mybir.AxisListType.X

P = 128
S, D = 256, 1024
NT = S // P
KC = D // P
EPS = 1e-6
WINDOWS = (2, 4, 8, 16)
RING = 2
PARTS = 3
BLK = 4096
NH = 16
HD = 64
MH, MQK, MNOPE, MROPE = 8, 96, 64, 32
G, GI, GP = 64, 16, 64
L = 8
NC = S // L
FB = 8
BIG = -1.0e30
SPLIT = ("u", "za", "a_out", "gate0", "k", "v", "q", "zb", "b_out", "gate1", "wc", "wq", "wk", "wv", "w_o",
         "val", "gate", "f1", "f2")

VEC_ROWS = {"a_norm": 8, "a_scale": 8, "kv_norm": 8, "b_norm": 8, "mix0": 8, "ffn0": 8, "mix1": 8, "ffn1": 8,
            "d_skip": 8, "g_cq": 2, "g_ckv": 1, "k_norm": 1, "q_norm": 1, "qn_mla": 1, "kn_mla": 1,
            "qn_moba": 1, "kn_moba": 1}
VEC_AT = {}
for _n, _k in VEC_ROWS.items():
    VEC_AT[_n] = sum(VEC_ROWS[m] for m in VEC_AT)
NVEC = sum(VEC_ROWS.values())

CONST_COLS = {"ident": 128, "tneg": 128, "swap": 128, "bmask": 128, "mask_st": 128, "mask_ts": 128, "cos": 32,
              "sin": 32, "sgn": 2}
CONST_AT = {}
for _n, _k in CONST_COLS.items():
    CONST_AT[_n] = sum(CONST_COLS[m] for m in CONST_AT)
NCONST = sum(CONST_COLS.values())
NPOOL = 4 * 384


def constants():
    import numpy as np
    i = np.arange(P)
    c = np.zeros((P, NCONST), np.float32)

    def put(name, a):
        c[:, CONST_AT[name]:CONST_AT[name] + CONST_COLS[name]] = a

    put("ident", np.eye(P))
    put("tneg", -(i[:, None] >= i[None, :]).astype(np.float32))
    put("swap", np.roll(np.eye(P), 64, axis=1))
    put("bmask", (i[:, None] // GI == i[None, :] // GI))
    put("mask_st", np.where(i[:, None] >= i[None, :], BIG, 0))
    put("mask_ts", np.where(i[None, :] > i[:, None], BIG, 0))
    half = MROPE // 2
    inv = (np.float32(10000.0) ** (-np.arange(half, dtype=np.float32) / np.float32(half))).astype(np.float32)
    ang = (np.arange(S, dtype=np.float32)[:, None] * inv[None, :]).astype(np.float32)
    put("cos", np.cos(ang).reshape(NT, P, half).transpose(1, 0, 2).reshape(P, 32))
    put("sin", np.sin(ang).reshape(NT, P, half).transpose(1, 0, 2).reshape(P, 32))
    put("sgn", np.where(i[:, None] < 64, [[1.0, -1.0]], [[-1.0, 1.0]]))
    pool = np.zeros((P, 4, 384), np.float32)
    t = np.arange(S)
    for g, w in enumerate(WINDOWS):
        m = ((t[:, None] <= t[None, :]) & (t[:, None] > t[None, :] - w)) / np.minimum(t[None, :] + 1, w)
        m = m - np.eye(S)
        pool[:, g, 0:256] = m[0:P]
        pool[:, g, 256:384] = m[P:, P:]
    return c, pool.reshape(P, NPOOL)


class Units:

    def __init__(self):
        self.at, self.bank, self.before, self.by, self.count = {}, [], [], [], []
        self.last, self.turn, self.banks, self.high = {}, 0, list(range(8)), {}

    def add(self, name, freed_by, bank=None):
        if freed_by == "av":
            self.high[name] = len(self.high) + 1
            freed_by = "v"
        if bank is None:
            bank = self.banks[self.turn % len(self.banks)]
            self.turn += 1
        q = len(self.bank)
        assert name not in self.at, name
        self.at[name] = q
        self.bank.append(bank)
        self.before.append(self.last.get(bank))
        self.by.append(freed_by)
        self.count.append(self.by.count(freed_by))
        self.last[bank] = q

    def done(self, name):
        return self.at[name] + 1

    def emptied(self, name):
        return self.count[self.at[name]]


def gemm(u, stage, blocks, freed_by):
    for nb in range(blocks):
        for t in range(NT):
            u.add((stage, nb, t), freed_by)


def turned(u, stage, n=4):
    for k in range(n):
        u.add(("T", stage, k), "va"[k % 2])


def turned_in_two(u, stage):
    for k in range(4):
        u.add(("T", stage, k), "av")


def plan():
    u = Units()
    u.add("vec", "v")
    u.add(("pT", 0), "a")
    u.add(("pT", 1), "a")
    turned_in_two(u, "a")
    gemm(u, "u", 2, "a")
    gemm(u, "za", 2, "a")
    for g in range(4):
        u.add(("pool", g), "a")
    gemm(u, "mixed", 2, "v")
    turned_in_two(u, "mixed")
    gemm(u, "a_out", 2, "v")
    turned_in_two(u, "x0")
    gemm(u, "ple0", 2, "a")
    gemm(u, "gate0", 2, "a")
    turned_in_two(u, "kv")
    gemm(u, "k", 2, "a")
    gemm(u, "v", 2, "a")
    turned_in_two(u, "qz")
    turned(u, "k")
    gemm(u, "q", 2, "a")
    for t in range(NT):
        u.add(("zb", 0, t), "a")
    turned(u, "q")
    for t in range(NT):
        u.add(("zb", 1, t), "a")
    for i in range(NH + 3):
        if i < NH:
            u.add(("logits", i), "", bank=i % 5)
        if 2 <= i < NH + 2:
            u.add(("loga", i - 2), "a", bank=(i - 2) % 5)
        if i >= 3 and (i - 3) % 4 == 3:
            u.add(("stick_out", (i - 3) // 4), "v", bank=5 + (i - 3) // 4 % 3)
    turned_in_two(u, "o1")
    gemm(u, "b_out", 2, "v")
    turned_in_two(u, "x1")
    gemm(u, "ple1", 2, "a")
    gemm(u, "gate1", 2, "a")
    turned_in_two(u, "mix0")
    gemm(u, "wc", 1, "a")
    gemm(u, "wq", 1, "a")
    gemm(u, "wk", 1, "a")
    u.add(("T", "c", 0), "v")
    u.add(("T", "c", 1), "v")
    gemm(u, "wv", 1, "a")
    turned(u, "qmoba", 2)
    turned(u, "kmoba", 2)
    gemm(u, "uq", 2, "a")
    gemm(u, "ukv", 2, "a")
    for kind in ("moba", "mla"):
        if kind == "mla":
            turned(u, "qmla")
            turned(u, "kmla")
        for i in range(MH + 3):
            if i < MH:
                u.add(("scores", kind, i), "a", bank=i % 4)
            if 2 <= i < MH + 2:
                u.add(("probsT", kind, i - 2), "v", bank=4 + i % 2)
            if i >= 3 and (i - 3) % 4 == 3:
                u.add(("soft_out", kind, (i - 3) // 4), "v", bank=6 + (i - 3) // 4)
    turned_in_two(u, "o2")
    gemm(u, "w_o", 2, "v")
    mlp_plan(u, 0)
    u.add("gain_gi", "v")
    for b in range(4):
        u.add(("ug", b), "v")
    turned(u, "mix1")
    for b in range(4):
        u.add(("inject", b), "a")
    for b in range(4):
        u.add(("injectx", b), "a")
    for b in range(4):
        u.add(("fir", b), "v")
    for b in range(4):
        u.add(("state_out", b), "a")
    for b in range(4):
        u.add(("state_outT", b), "v")
    for h in range(2):
        gemm(u, ("val", h), 1, "v")
        gemm(u, ("gate", h), 1, "a")
    mlp_plan(u, 1)
    return u


def mlp_plan(u, layer):
    turned_in_two(u, ("ffn", layer))
    u.banks, u.turn = [4, 5, 6, 7], 0

    def s5_chunk(f):
        u.add(("wT", f, 0), "a")
        u.add(("wT", f, 1), "a")
        u.add(("taps", f), "v")

    for i in range(FB + 1):
        if i:
            for k in range(2):
                u.add(("fT", layer, i - 1, k), "av")
        if i < FB:
            gemm(u, ("f1", layer, i), 1, "v")
        if layer == 0 and i == 2:
            for k in range(3):
                u.add(("powT", k), "a")
            for name in ("bcT", "bcX"):
                for k in range(4):
                    u.add((name, k), "v")
        if layer == 0 and i >= 3:
            s5_chunk(i - 3)
    for k in range(4):
        u.add(("acc", layer, k), "v", bank=k)
    if layer == 0:
        s5_chunk(FB - 2)
        s5_chunk(FB - 1)
    u.banks, u.turn = list(range(8)), 4


def loads(w):
    def cols(a, c0, c1):
        return a[:, c0:c1].rearrange("(k p) n -> p k n", p=P)

    out = []
    a_in, a_out, w_kv, b_in, b_out = w["a_w_in"][0], w["a_w_out"][0], w["w_kv"], w["b_w_in"][0], w["b_w_out"][0]

    def add(name, parts, reader):
        out.append((name, parts, reader))

    def two(name, a, base, unit):
        for nb in range(2):
            add((name, nb), [(0, cols(a, base + 512 * nb, base + 512 * nb + 512))], (unit, nb, 1))

    two("u", a_in, 0, "u")
    two("za", a_in, D, "za")
    add("w_group", [(0, w["a_w_group"][0].rearrange("g (k p) n -> p (g k) n", p=P))], ("mixed", 1, 1))
    two("a_out", a_out, 0, "a_out")
    add("ple0", [(0, cols(w["ple_w"][0], 0, D))], ("ple0", 1, 1))
    two("gate0", w["ple_gate_w"][0], 0, "gate0")
    two("k", w_kv, 0, "k")
    two("v", w_kv, D, "v")
    two("q", b_in, 0, "q")
    two("zb", b_in, D, "zb")
    two("b_out", b_out, 0, "b_out")
    add("ple1", [(0, cols(w["ple_w"][1], 0, D))], ("ple1", 1, 1))
    two("gate1", w["ple_gate_w"][1], 0, "gate1")
    w_in = w["w_in_2"][0]
    add("wc", [(0, cols(w_in, 0, 416))], ("wc", 0, 1))
    add("wq", [(0, cols(w_in, 416, 928))], ("wq", 0, 1))
    add("wk", [(0, cols(w_in, 928, 1440))], ("wk", 0, 1))
    add("wv", [(0, cols(w_in, 1440, 1952))], ("wv", 0, 1))
    add("lowrank", [(0, cols(w["w_uq_2"][0], 0, 768)), (1536, cols(w["w_ukv_2"][0], 0, 1024))], ("ukv", 1, 1))
    two("w_o", w["w_o_2"][0], 0, "w_o")
    mlp_loads(w, add, cols, 0)
    def glu(name, h):
        base = 512 * h + (D if name == "gate" else 0)
        add((name, h), [(0, cols(w["w_glu_2"][0], base, base + 512))], ((name, h), 0, 1))

    for name, reader in (("inject", "inject"), ("taps", "fir"), ("readout", "state_out")):
        if name == "readout":
            glu("val", 0)
        for half in range(2):
            add((name, half), [(0, w["scratch_" + name][:, half * BLK:half * BLK + BLK])], (reader, 2 * half + 1))
    for name, h in (("gate", 0), ("val", 1), ("gate", 1)):
        glu(name, h)
    mlp_loads(w, add, cols, 1)
    return out


def mlp_loads(w, add, cols, layer):
    w1, w2 = w["w_ff1_2"][layer], w["w_ff2_2"][layer]
    for i in range(FB + 1):
        if layer == 0 and i == 2:
            add("rawBC", [(0, w["b_re_2"][0].rearrange("g p i -> g (p i)")),
                          (1024, w["b_im_2"][0].rearrange("g p i -> g (p i)")),
                          (2048, w["c_re_2"][0]), (2048 + GP, w["c_im_2"][0])], ("bcT", 3))
        if i < FB:
            add(("f1", layer, i), [(0, cols(w1, 512 * i, 512 * i + 512))], (("f1", layer, i), 0, 1))
        if i:
            add(("f2", layer, i - 1), [(0, w2[512 * (i - 1):512 * (i - 1) + 512, :].rearrange("(k p) n -> p k n", p=P))],
                ("f2", (FB - 1) * layer + i - 1) if i - 1 < FB - 1 else ("acc", layer, 3))


def program(nc, w, out):
    import numpy as np
    u = plan()
    blocks = loads(w)
    slot = {name: n % RING for n, (name, _, _) in enumerate(blocks)}
    landed = {}
    for n, (name, parts, _) in enumerate(blocks):
        before = landed[blocks[n - RING][0]] if n >= RING else 0
        landed[name] = before + 16 * len(parts)
    done = u.done
    split_names = [name for name, _, _ in blocks if name[0] in SPLIT or name in SPLIT]
    order = {name: n for n, name in enumerate(split_names)}
    reader_of = {name: reader for name, _, reader in blocks}
    size = {name: 8 * 416 if name == "wc" else BLK for name in split_names}

    with ExitStack() as ctx:
        def sb(name, shape, dt=F32):
            return ctx.enter_context(nc.sbuf_tensor(name, shape, dt))

        def sem(name):
            return ctx.enter_context(nc.semaphore(name))

        ps = [ctx.enter_context(nc.psum_tensor(f"bank{i}", [P, 512], F32)) for i in range(8)]

        x = sb("x", [P, NT, D])
        h = sb("h", [P, NT, D])
        hT_hi = sb("hT_hi", [P, KC, S], F32R)
        hT_lo = sb("hT_lo", [P, KC, S], F32R)
        hidT_hi = sb("hidT_hi", [P, 4, S], F32R)
        hidT_lo = sb("hidT_lo", [P, 4, S], F32R)
        work = sb("work", [P, 12288])
        aux = sb("aux", [P, 5504])
        ring = sb("ring", [P, RING, BLK])
        whi = sb("whi", [P, PARTS, BLK // 2], F32R)
        wlo = sb("wlo", [P, PARTS, BLK // 2], F32R)
        sig = sb("sig", [P, 2, 512])
        pT = sb("pT", [P, 2, 2, S])
        vrows = sb("vrows", [NVEC, P])
        vcols = sb("vcols", [P, NVEC])
        cst = sb("cst", [P, NCONST])
        bf = sb("bf", [P, 3, P], BF16)
        allneg = sb("allneg", [P, P])
        inv = sb("inv", [P, 2, NT])
        half_neg = sb("half_neg", [P, 32])
        ssq = sb("ssq", [P, 6, NT])
        ms = sb("ms", [P, 6, NT])
        rstd = sb("rstd", [P, 6, NT])
        ssh = sb("ssh", [P, 32])
        msh = sb("msh", [P, 32])
        rsh = sb("rsh", [P, 32])
        lowss = sb("lowss", [P, 4])
        lowms = sb("lowms", [P, 4])
        lowr = sb("lowr", [P, 4])
        nmax = sb("nmax", [P, 2, MH, NT])
        den = sb("den", [P, 2, MH, NT])
        rden = sb("rden", [P, 2, MH, NT])
        a8 = sb("a8", [P, 3, G])
        gain_rows = sb("gain_rows", [G, 2, P])
        gain_gi = sb("gain_gi", [P, G])
        log_dt = sb("log_dt", [G, 2])

        block_landed = [sem(f"block_landed{i}") for i in range(RING)]
        (pe_done, act_emptied, dve_emptied, x_landed, tables_landed, p_landed, pools_landed, vecs_landed,
         masks_ready, gains_ready, x_updated, ssq_ready, ms_ready, rstd_ready, headms_ready, headr_ready,
         heads_normed, logs_ready, sp_ready, lowms_ready, lowr_ready, max_ready, f2_done, halves_ready,
         dt_ready, zr_ready, exp_ready, angle_ready, sin_ready, lam_landed, powers_ready, pads_zeroed,
         inputs_scaled, injects_made, readouts_made, pads_filled, w_stored, v_stored, t_stored, h_normed,
         regrouped_a, regrouped_b, gain_rows_ready, gain_landed, states_ready, gelu_ready, act_step, dve_step, pool_step,
         out_stored) = (
            sem(n) for n in (
                "pe_done", "act_emptied", "dve_emptied", "x_landed", "tables_landed", "p_landed",
                "pools_landed", "vecs_landed", "masks_ready", "gains_ready", "x_updated",
                "ssq_ready", "ms_ready", "rstd_ready", "headms_ready", "headr_ready",
                "heads_normed", "logs_ready", "sp_ready", "lowms_ready", "lowr_ready", "max_ready",
                "f2_done", "halves_ready", "dt_ready", "zr_ready", "exp_ready", "angle_ready",
                "sin_ready", "lam_landed", "powers_ready", "pads_zeroed", "inputs_scaled",
                "injects_made", "readouts_made", "pads_filled", "w_stored", "v_stored", "t_stored",
                "h_normed", "regrouped_a", "regrouped_b", "gain_rows_ready", "gain_landed", "states_ready",
                "gelu_ready", "act_step", "dve_step", "pool_step", "out_stored"))

        chunked = [sem("chunked_a"), sem("chunked_b")]
        high_made, low_made, high_turned, inv_ready, gelu_high, relu_ready, first_used = (
            sem(n) for n in ("high_made", "low_made", "high_turned", "inv_ready", "gelu_high", "relu_ready",
                             "first_used"))

        def half_of(g):
            name = split_names[g // 2]
            n = size[name] // 2
            return name, slice(n * (g % 2), n * (g % 2) + n), (slice(None), g % PARTS, slice(0, n))

        def const(name):
            return cst[:, CONST_AT[name]:CONST_AT[name] + CONST_COLS[name]]

        def gain(name, c=0, rows=P):
            return vcols[0:rows, VEC_AT[name] + c:VEC_AT[name] + c + 1]

        def weights(name, k, n, at=0):
            return ring[:, slot[name], at:at + k * n].rearrange("p (k n) -> p k n", k=k)

        def tok(at, n=D):
            return work[:, at:at + NT * n].rearrange("p (t n) -> p t n", t=NT)

        def bank(name):
            return ps[u.bank[u.at[name]]]

        ident, tneg = const("ident"), const("tneg")
        q_tok, k_tok, v_tok, z_tok = (tok(2048 * n) for n in range(4))
        u_tok = q_tok
        p_tok = work[:, 8192:9216].rearrange("p (l t n) -> p l t n", l=2, t=NT)
        pl_tok = aux[:, 0:2048].rearrange("p (t n) -> p t n", t=NT)
        pools = aux[:, 2048:2048 + NPOOL].rearrange("p (g n) -> p g n", g=4)
        qT = work[:, 8192:10240].rearrange("p (c s) -> p c s", c=KC)
        kT = work[:, 10240:12288].rearrange("p (c s) -> p c s", c=KC)
        squares = aux[:, 0:2048]
        logs, sps, sticks = (aux[:, 2048 + 1152 * n:3200 + 1152 * n].rearrange("p (b n) -> p b n", b=3)
                             for n in range(3))
        qm, km = tok(0, MH * MQK), tok(1536, MH * MQK)
        vm, qb, kb, vb = (tok(3072 + 1024 * n, 512) for n in range(4))
        cbuf = tok(7168, 416)
        pooledT = work[:, 2048:4096].rearrange("p (c s) -> p c s", c=KC)
        cT = aux[:, 3200:3968].rearrange("p (c s) -> p c s", c=3)
        turned_qk = {"moba": (sig[:, :, :].rearrange("p b (c s) -> p (b c) s", s=S),
                              pT[:, :, :, :].rearrange("p l c s -> p (l c) s")), "mla": (qT, kT)}
        ropes = aux[:, 2048:3072].rearrange("p (n t h c) -> p n t h c", n=4, t=NT, h=MH)
        probs = aux[:, 3200:4352].rearrange("p (b n) -> p b n", b=3)
        probsT = aux[:, 4352:5504].rearrange("p (b n) -> p b n", b=3)
        hid = aux[:, 0:1024].rearrange("p (t n) -> p t n", t=NT)
        inject_T = aux[:, 2048:3072]
        taps = aux[:, 3072:4096]
        inject = work[:, 0:1024].rearrange("p (g j i) -> p g j i", g=8, j=L)
        readout = work[:, 1024:2176].rearrange("p (g k o) -> p g k o", g=8, k=L + 1)
        t1, t2 = work[:, 2176:3328], work[:, 3328:4480]
        Bs, Bx, Cs, Cx = (work[:, 4480 + 1024 * n:5504 + 1024 * n].rearrange("p (i g) -> p i g", i=GI)
                          for n in range(4))
        powT = work[:, 8576:9856].rearrange("p (q g) -> p q g", q=20)
        pads = work[:, 9856:10880]
        t3 = work[:, 10880:12032]
        lam = work[0:G, 10880:12288].rearrange("p (n c) -> p n c", c=GP)
        pw = work[0:G, 0:2560].rearrange("p (q r c) -> p q r c", q=20, r=2)
        powers = work[0:G, 3328:4352].rearrange("p (r k c) -> p r k c", r=2, k=L)
        prods = work[0:G, 4480:5504].rearrange("p (n k c) -> p n k c", n=4, k=4)
        xc = [v.rearrange("p (j n) -> p j n", j=L) for v in (work[0:NC, 8192:12288], aux[0:NC, 0:4096])]
        xg = work[0:NC, 0:8192].rearrange("p (g j i) -> p g j i", g=G, j=L)
        uT = aux[:, 0:2048].rearrange("p (c s) -> p c s", c=KC)
        ug = work[:, 8192:10240].rearrange("p (g c) -> p g c", g=G)
        states = work[:, 0:33 * 128].rearrange("p (r c g) -> p r c g", r=2, c=NC + 1)
        steps = work[:, 4224:4480].rearrange("p (n r g) -> p n r g", n=2, r=2)
        yc = work[:, 4480:6528].rearrange("p (f j n) -> p f j n", f=2, j=L)
        ybuf = work[:, 10240:12288].rearrange("p (c s) -> p c s", c=KC)

        block = ctx.enter_context(nc.Block())

        @block.sync
        def _(sp):
            stores = {"inject": w_stored, "readout": v_stored, "taps": t_stored}
            for n, (name, parts, _) in enumerate(blocks):
                if n >= RING:
                    before, _, reader = blocks[n - RING]
                    if before in order:
                        sp.wait_ge(low_made, 2 * order[before] + 2)
                    else:
                        sp.wait_ge(pe_done, done(reader))
                if name[0] in stores:
                    sp.wait_ge(stores[name[0]], 16 * 4 * (name[1] + 1))
                for at, src in parts:
                    rows, cols = src.shape[0], src.shape[1] * (src.shape[2] if len(src.shape) > 2 else 1)
                    dst = ring[0:rows, slot[name], at:at + cols]
                    if name == "rawBC" and at >= 2048:
                        dst = ring[0:rows, slot[name], 2048:4096].rearrange("p (o r c) -> p r o c", o=GI, r=2)[:, (at - 2048) // GP]
                    elif len(src.shape) > 2:
                        dst = dst.rearrange("p (k n) -> p k n", k=src.shape[1])
                    sp.dma_start(dst, src).then_inc(block_landed[slot[name]], 16)
            sp.wait_ge(dve_emptied, u.emptied(("acc", 1, 3)))
            sp.dma_start(out.rearrange("b (t p) n -> p (b t) n", p=P), x[:, :, :]).then_inc(out_stored, 16)
            sp.wait_ge(out_stored, 16)

        @block.tensor
        def _(pe):

            def begin(name):
                before = u.before[u.at[name]]
                if before is not None and u.by[before] == "a":
                    pe.wait_ge(act_emptied, u.count[before])
                elif before is not None:
                    pe.wait_ge(dve_emptied, u.count[before])
                return bank(name)

            def emptied(name):
                if u.by[u.at[name]] == "a":
                    pe.wait_ge(act_emptied, u.emptied(name))
                else:
                    pe.wait_ge(dve_emptied, u.emptied(name))

            def weights_here(name):
                pe.wait_ge(block_landed[slot[name]], landed[name])

            def turn(stage, src, units=range(4), width=P, chunks=8, ready=None):
                for k in units:
                    b = begin(("T", stage, k))
                    if ready:
                        ready(k)
                    for cc in range(2):
                        c = 2 * k + cc
                        if c < chunks:
                            for t in range(NT):
                                last = pe.transpose(b[0:width, cc * S + t * P:cc * S + t * P + P],
                                                    src[:, t, c * width:(c + 1) * width], ident)
                    last.then_inc(pe_done, 1)

            def three(bank_cols, parts, at, w_high, w_low, first, last):
                high, low = parts
                pe.matmul(bank_cols, high[:, at[0], at[1]], w_high, start=first, stop=False)
                pe.matmul(bank_cols, high[:, at[0], at[1]], w_low, start=False, stop=False)
                return pe.matmul(bank_cols, low[:, at[0], at[1]], w_high, start=False, stop=last)

            def part_views(g, k, width):
                _, _, at = half_of(g)
                return (v[at].rearrange("p (k n) -> p k n", n=width) for v in (whi, wlo))

            def product(stage, nb, name, width=512, turned_by=None):
                banks = [begin((stage, nb, t)) for t in range(NT)]
                for half in range(2):
                    g = 2 * order[name] + half
                    w_high, w_low = part_views(g, 4, width)
                    pe.wait_ge(low_made, g + 1)
                    for t in range(NT):
                        for kk in range(4):
                            k = 4 * half + kk
                            if turned_by and nb == 0 and t == 0 and k % 2 == 0:
                                emptied(("T", turned_by, k // 2))
                            last = three(banks[t][:, 0:width], (hT_hi, hT_lo), (k, slice(t * P, t * P + P)),
                                         w_high[:, kk, :], w_low[:, kk, :], k == 0, k == KC - 1)
                        if half:
                            last.then_inc(pe_done, 1)
                    if half == 0:
                        last.then_inc(first_used, 1)

            def x_has(stage):
                return lambda k: emptied((stage, k // 2, 1))

            def x_gated(before):
                return lambda k: pe.wait_ge(x_updated, before + (2 if k < 2 else 4))

            pe.wait_ge(tables_landed, 16)
            pe.wait_ge(vecs_landed, 16)
            b = begin("vec")
            pe.transpose(b[:, 0:NVEC], vrows[:, :], ident[0:NVEC, 0:NVEC]).then_inc(pe_done, 1)
            pe.wait_ge(p_landed, 32)
            for l in range(2):
                b = begin(("pT", l))
                for cc in range(2):
                    for t in range(NT):
                        last = pe.transpose(b[:, cc * S + t * P:cc * S + t * P + P],
                                            p_tok[:, l, t, cc * P:(cc + 1) * P], ident)
                last.then_inc(pe_done, 1)

            pe.wait_ge(x_landed, 16)
            turn("a", x)
            for stage in ("u", "za"):
                for nb in range(2):
                    product(stage, nb, (stage, nb), turned_by="a" if stage == "u" else None)
            pe.wait_ge(pools_landed, 16)
            for g in range(4):
                b = begin(("pool", g))
                emptied(("u", g // 2, 1))
                for cc in range(2):
                    c = 2 * g + cc
                    pe.matmul(b[:, cc * S:(cc + 1) * S], u_tok[:, 0, c * P:(c + 1) * P], pools[:, g, 0:S],
                              start=(cc == 0), stop=False, skip_group_check=True)
                    last = pe.matmul(b[:, cc * S + P:(cc + 1) * S], u_tok[:, 1, c * P:(c + 1) * P],
                                     pools[:, g, S:S + P], start=False, stop=True, skip_group_check=True)
                last.then_inc(pe_done, 1)
            weights_here("w_group")
            wg = ring[:, slot["w_group"], 0:2048].rearrange("p (g k n) -> p g k n", g=4, k=2)
            for nb in range(2):
                for t in range(NT):
                    b = begin(("mixed", nb, t))
                    for g in (2 * nb, 2 * nb + 1):
                        emptied(("pool", g))
                        for k in range(2):
                            last = pe.matmul(b[:, (g % 2) * S:(g % 2) * S + S], pooledT[:, 2 * g + k, t * P:(t + 1) * P],
                                             wg[:, g, k, :], start=(k == 0), stop=(k == 1))
                    last.then_inc(pe_done, 1)
            turn("mixed", h, ready=lambda k: emptied(("mixed", k // 2, 1)))
            for nb in range(2):
                product("a_out", nb, ("a_out", nb), turned_by="mixed")

            def ple(l, before):
                name = f"ple{l}"
                turn(f"x{l}", x, ready=x_has(before))
                weights_here(name)
                wp = weights(name, 2, D)
                emptied(("pT", l))
                for nb in range(2):
                    for t in range(NT):
                        b = begin((name, nb, t))
                        for k in range(2):
                            last = pe.matmul(b[:, :], pT[:, l, k, t * P:(t + 1) * P],
                                             wp[:, k, nb * 512:(nb + 1) * 512], start=(k == 0), stop=(k == 1))
                        last.then_inc(pe_done, 1)
                for nb in range(2):
                    product(f"gate{l}", nb, (f"gate{l}", nb), turned_by=f"x{l}")

            ple(0, "a_out")

            turn("kv", x, ready=x_gated(0))
            for stage in ("k", "v"):
                for nb in range(2):
                    product(stage, nb, (stage, nb), turned_by="kv" if stage == "k" else None)
            turn("qz", x)
            turn("k", k_tok, ready=lambda k: pe.wait_ge(heads_normed, 1))
            for nb in range(2):
                product("q", nb, ("q", nb), turned_by="qz")
            product("zb", 0, ("zb", 0))
            turn("q", q_tok, ready=lambda k: pe.wait_ge(heads_normed, 2))
            product("zb", 1, ("zb", 1))
            pe.wait_ge(masks_ready, 4)
            for i in range(NH + 3):
                if i < NH:
                    b = begin(("logits", i))
                    c, p0 = i // 2, HD * (i % 2)
                    if i % 2 == 0:
                        emptied(("T", "q", c // 2))
                        emptied(("T", "k", c // 2))
                    pe.matmul(b[:, 0:S], kT[p0:p0 + HD, c, 0:P], qT[p0:p0 + HD, c, :], start=True, stop=False,
                              skip_group_check=True)
                    pe.matmul(b[:, S:S + P], kT[p0:p0 + HD, c, P:S], qT[p0:p0 + HD, c, P:S], start=False,
                              stop=False, skip_group_check=True)
                    pe.matmul(b[:, 0:P], bf[:, 0, :], bf[:, 1, :], start=False, stop=False, skip_group_check=True)
                    pe.matmul(b[:, S:S + P], bf[:, 0, :], bf[:, 1, :], start=False, stop=False,
                              skip_group_check=True).then_inc(pe_done, 1)
                if 2 <= i < NH + 2:
                    n = i - 2
                    b = bank(("loga", n))
                    pe.wait_ge(sp_ready, n + 1)
                    pe.matmul(b[:, 0:S], tneg, sps[:, n % 3, 0:S], start=False, stop=False, skip_group_check=True)
                    pe.matmul(b[:, P:S], allneg[:, :], sps[:, n % 3, S:S + P], start=False, stop=False,
                              skip_group_check=True)
                    pe.matmul(b[:, S:S + P], tneg, sps[:, n % 3, S:S + P], start=False, stop=True,
                              skip_group_check=True).then_inc(pe_done, 1)
                if i >= 3:
                    n = i - 3
                    b = begin(("stick_out", n // 4)) if n % 4 == 0 else bank(("stick_out", n // 4))
                    o = b[:, (n % 4) * P:(n % 4) * P + P]
                    emptied(("loga", n))
                    a = sticks[:, n % 3, :]
                    vh = v_tok[:, :, n * HD:(n + 1) * HD]
                    pe.matmul(o[:, 0:HD], a[:, 0:P], vh[:, 0, :], start=True, stop=True)
                    pe.matmul(o[:, HD:P], a[:, P:S], vh[:, 0, :], start=True, stop=False)
                    last = pe.matmul(o[:, HD:P], a[:, S:S + P], vh[:, 1, :], start=False, stop=True)
                    if n % 4 == 3:
                        last.then_inc(pe_done, 1)
            turn("o1", h, ready=lambda k: emptied(("stick_out", k)))
            for nb in range(2):
                product("b_out", nb, ("b_out", nb), turned_by="o1")
            ple(1, "b_out")

            turn("mix0", x, ready=x_gated(4))
            product("wc", 0, "wc", width=416, turned_by="mix0")
            product("wq", 0, "wq")
            product("wk", 0, "wk")
            turn("c", cbuf, units=range(2), chunks=3, ready=lambda k: emptied(("wc", 0, 1)))
            product("wv", 0, "wv")
            turn("qmoba", qb, units=range(2), ready=lambda k: pe.wait_ge(heads_normed, 3))
            turn("kmoba", kb, units=range(2), ready=lambda k: pe.wait_ge(heads_normed, 4))
            weights_here("lowrank")
            wuq = weights("lowrank", 2, 768)
            for nb in range(2):
                for t in range(NT):
                    b = begin(("uq", nb, t))
                    for k in range(2):
                        emptied(("T", "c", 0))
                        last = pe.matmul(b[:, 0:384], cT[:, k, t * P:(t + 1) * P], wuq[:, k, nb * 384:(nb + 1) * 384],
                                         start=(k == 0), stop=(k == 1))
                    last.then_inc(pe_done, 1)
            for nb in range(2):
                weights_here("lowrank")
                wkv = ring[:, slot["lowrank"], 1536 + 512 * nb:2048 + 512 * nb]
                for t in range(NT):
                    b = begin(("ukv", nb, t))
                    emptied(("T", "c", 1))
                    pe.matmul(b[:, :], cT[:, 2, t * P:(t + 1) * P], wkv, start=True, stop=True).then_inc(pe_done, 1)
            for kind in ("moba", "mla"):
                moba = kind == "moba"
                tq, tk = turned_qk[kind]
                v_all = vb if moba else vm
                if not moba:
                    turn("qmla", qm, width=MQK, ready=lambda k: pe.wait_ge(heads_normed, 5))
                    turn("kmla", km, width=MQK, ready=lambda k: pe.wait_ge(heads_normed, 6))
                for i in range(MH + 3):
                    if i < MH:
                        b = begin(("scores", kind, i))
                        c, rows = (i // 2, slice(HD * (i % 2), HD * (i % 2) + HD)) if moba else (i, slice(0, MQK))
                        emptied(("T", "q" + kind, c // 2))
                        emptied(("T", "k" + kind, c // 2))
                        pe.matmul(b[:, 0:P], tq[rows, c, 0:P], tk[rows, c, 0:P], start=True, stop=False,
                                  skip_group_check=True)
                        pe.matmul(b[:, P:P + S], tq[rows, c, P:S], tk[rows, c, :], start=False, stop=False,
                                  skip_group_check=True)
                        pe.matmul(b[:, 0:P], bf[:, 0, :], bf[:, 2, :], start=False, stop=False,
                                  skip_group_check=True)
                        pe.matmul(b[:, S:S + P], bf[:, 0, :], bf[:, 2, :], start=False, stop=True,
                                  skip_group_check=True).then_inc(pe_done, 1)
                    if 2 <= i < MH + 2:
                        n = i - 2
                        b = begin(("probsT", kind, n))
                        emptied(("scores", kind, n))
                        for k in range(3):
                            last = pe.transpose(b[:, k * P:(k + 1) * P], probs[:, n % 3, k * P:(k + 1) * P], ident)
                        last.then_inc(pe_done, 1)
                    if i >= 3:
                        n = i - 3
                        name = ("soft_out", kind, n // 4)
                        b = begin(name) if n % 4 == 0 else bank(name)
                        o = b[:, (n % 4) * P:(n % 4) * P + P]
                        emptied(("probsT", kind, n))
                        a = probsT[:, n % 3, :]
                        vh = v_all[:, :, n * HD:(n + 1) * HD]
                        pe.matmul(o[:, 0:HD], a[:, 0:P], vh[:, 0, :], start=True, stop=True)
                        pe.matmul(o[:, HD:P], a[:, P:S], vh[:, 0, :], start=True, stop=False)
                        last = pe.matmul(o[:, HD:P], a[:, S:S + P], vh[:, 1, :], start=False, stop=True)
                        if n % 4 == 3:
                            last.then_inc(pe_done, 1)
            turn("o2", h, ready=lambda k: emptied(("soft_out", "mla" if k < 2 else "moba", k % 2)))
            for nb in range(2):
                product("w_o", nb, ("w_o", nb), turned_by="o2")

            def mlp(layer, ready):
                turn(("ffn", layer), x, ready=ready)
                acc = [ps[k] for k in range(4)]
                for i in range(FB + 1):
                    n = i - 1
                    if i:
                        for k in range(2):
                            b = begin(("fT", layer, n, k))
                            emptied((("f1", layer, n), 0, 1))
                            for cc in range(2):
                                for t in range(NT):
                                    c = 2 * k + cc
                                    last = pe.transpose(b[:, cc * S + t * P:cc * S + t * P + P],
                                                        hid[:, t, c * P:(c + 1) * P], ident)
                            last.then_inc(pe_done, 1)
                    if i < FB:
                        product(("f1", layer, i), 0, ("f1", layer, i), turned_by=("ffn", layer) if i == 0 else None)
                    if layer == 0 and i == 2:
                        s5_coefficients()
                    if layer == 0 and i >= 3:
                        s5_chunk(i - 3)
                    if i:
                        for half in range(2):
                            g = 2 * order[("f2", layer, n)] + half
                            w_high, w_low = part_views(g, 2, D)
                            pe.wait_ge(low_made, g + 1)
                            emptied(("fT", layer, n, half))
                            for t in range(NT):
                                for nb in range(2):
                                    if n == 0 and half == 0:
                                        begin(("acc", layer, 2 * t + nb))
                                    for kk in range(2):
                                        cols = slice(nb * 512, nb * 512 + 512)
                                        last = three(acc[2 * t + nb][:, :], (hidT_hi, hidT_lo),
                                                     (2 * half + kk, slice(t * P, t * P + P)), w_high[:, kk, cols],
                                                     w_low[:, kk, cols], n == 0 and half == 0 and kk == 0,
                                                     n == FB - 1 and half == 1 and kk == 1)
                                    if n == FB - 1 and half == 1:
                                        last.then_inc(pe_done, 1)
                            if half == 0:
                                last.then_inc(first_used, 1)
                            elif n < FB - 1:
                                last.then_inc(f2_done, 1)
                if layer == 0:
                    s5_chunk(FB - 2)
                    s5_chunk(FB - 1)

            def s5_coefficients():
                pe.wait_ge(powers_ready, 1)
                for k in range(3):
                    b = begin(("powT", k))
                    for q in range(8 * k, min(8 * k + 8, 20)):
                        last = pe.transpose(b[:, (q % 8) * G:(q % 8) * G + G],
                                            pw[:, q, :, :].rearrange("p r c -> p (r c)"), ident[0:G, 0:G])
                    last.then_inc(pe_done, 1)
                weights_here("rawBC")
                raw = ring[0:G, slot["rawBC"], :]
                for k in range(4):
                    b = begin(("bcT", k))
                    v = raw[:, 0:2048].rearrange("p (rc i) -> p i rc", i=GI) if k < 2 else \
                        raw[:, 2048:4096].rearrange("p (o rc) -> p o rc", o=GI)
                    for i in range(8):
                        last = pe.transpose(b[:, i * G:(i + 1) * G], v[:, 8 * (k % 2) + i, :], ident[0:G, 0:G])
                    last.then_inc(pe_done, 1)
                for k in range(4):
                    b = begin(("bcX", k))
                    emptied(("bcT", k))
                    src = (Bs, Cs)[k // 2][:, 8 * (k % 2):8 * (k % 2) + 8, :].rearrange("p i g -> p (i g)")
                    pe.matmul(b[:, :], const("swap"), src, start=True, stop=True).then_inc(pe_done, 1)

            def s5_chunk(f):
                pe.wait_ge(injects_made, f + 1)
                for k in range(2):
                    b = begin(("wT", f, k))
                    for g in range(4):
                        last = pe.transpose(b[:, g * P:(g + 1) * P],
                                            inject[:, 4 * k + g, :, :].rearrange("p j i -> p (j i)"), ident)
                    last.then_inc(pe_done, 1)
                pe.wait_ge(pads_filled, f + 1)
                pe.wait_ge(readouts_made, f + 1)
                b = begin(("taps", f))
                for g in range(8):
                    last = pe.matmul(b[:, 0:P], pads[:, g * P:(g + 1) * P],
                                     readout[:, g, 0:L, :].rearrange("p k o -> p (k o)"),
                                     start=(g == 0), stop=(g == 7))
                last.then_inc(pe_done, 1)

            mlp(0, x_has("w_o"))

            b = begin("gain_gi")
            pe.wait_ge(gain_rows_ready, 1)
            pe.transpose(b[:, 0:G], gain_rows[:, 1, :], ident[0:G, 0:G]).then_inc(pe_done, 1)
            for n in range(4):
                pe.wait_ge(regrouped_a if n < 2 else regrouped_b, 1)
                b = begin(("ug", n))
                for g in range(16):
                    f = 16 * n + g
                    last = pe.transpose(b[:, g * NC:(g + 1) * NC], xg[:, f].rearrange("p j i -> p (j i)"),
                                        ident[0:NC, 0:NC])
                last.then_inc(pe_done, 1)
            turn("mix1", h)
            for n in range(4):
                b = begin(("inject", n))
                emptied(("ug", n))
                weights_here(("inject", n // 2))
                wi = weights(("inject", n // 2), 32, P)
                for g in range(16):
                    f = 16 * n + g
                    last = pe.matmul(b[:, g * NC:(g + 1) * NC], wi[:, f % 32, :], ug[:, f, :], start=True, stop=True)
                last.then_inc(pe_done, 1)
            for n in range(4):
                b = begin(("injectx", n))
                emptied(("inject", 3))
                pe.matmul(b[:, :], const("swap"),
                          states[:, 0, 1 + 8 * n:9 + 8 * n, :].rearrange("p c g -> p (c g)"),
                          start=True, stop=True).then_inc(pe_done, 1)
            for n in range(4):
                b = begin(("fir", n))
                emptied(("T", "mix1", n))
                weights_here(("taps", n // 2))
                wt = weights(("taps", n // 2), 32, P)
                for fl in range(2):
                    f = 2 * n + fl
                    src = uT[:, f, :].rearrange("p (c j) -> p c j", j=L)
                    dst = b[:, fl * S:(fl + 1) * S].rearrange("p (c j) -> p c j", j=L)
                    for k in range(L):
                        last = pe.matmul(dst[:, :, k:L], wt[:, (f % 4) * 8 + k, :], src[:, :, 0:L - k],
                                         start=(k == 0), stop=(k == L - 1), skip_group_check=True)
                last.then_inc(pe_done, 1)
            pe.wait_ge(states_ready, 1)
            for n in range(4):
                b = begin(("state_out", n))
                half, part = n // 2, n % 2
                weights_here(("readout", half))
                wr = weights(("readout", half), 32, P)
                for q in range(4):
                    for g in range(4):
                        f = 8 * q + 4 * part + g
                        last = pe.matmul(b[32 * q:32 * q + 32, g * P:(g + 1) * P], states[:, 0, 0:NC, 32 * half + f],
                                         wr[:, f, :], start=True, stop=True)
                last.then_inc(pe_done, 1)
            for n in range(4):
                b = begin(("state_outT", n))
                emptied(("state_out", 2 * (n // 2) + 1))
                for jj in range(4):
                    last = pe.transpose(b[:, jj * P:(jj + 1) * P], yc[:, n // 2, 4 * (n % 2) + jj, :], ident)
                last.then_inc(pe_done, 1)
            pe.wait_ge(gelu_ready, 4)
            for hh in range(2):
                for name in ("val", "gate"):
                    product((name, hh), 0, (name, hh))
            mlp(1, x_gated(8))

        @block.scalar
        def _(act):
            steps_done = [0]

            def link(ins):
                steps_done[0] += 1
                ins.then_inc(act_step, 1)
                act.wait_ge(act_step, steps_done[0])

            def filled(name):
                act.wait_ge(pe_done, done(name))
                return bank(name)

            def copy_out(name, dst, src=None, scale=1.0, func=ACT.Copy):
                b = filled(name)
                act.activation(dst, b[:, :] if src is None else src, func, scale=scale).then_inc(act_emptied, 1)

            def turned_out(stage, pairs, units=(1, 3), width=P):
                for k in units:
                    b = filled(("T", stage, k))
                    for n, (dst, name, one) in enumerate(pairs):
                        if name is None:
                            ins = act.activation(dst[0:width, 2 * k:2 * k + 2, :].rearrange("p c s -> p (c s)"),
                                                 b[0:width, :], ACT.Copy)
                            continue
                        for cc in range(2):
                            c = 2 * k + cc
                            ins = act.activation(dst[0:width, c, :], b[0:width, cc * S:cc * S + S], ACT.Copy,
                                                 scale=gain(name, 0 if one else c, width))
                    ins.then_inc(act_emptied, 1)

            def turned_high(stage, name):
                for k in range(4):
                    b = filled(("T", stage, k))
                    if name is None:
                        ins = act.activation(hT_hi[:, 2 * k:2 * k + 2, :].rearrange("p c s -> p (c s)"), b[:, :], ACT.Copy)
                    else:
                        for cc in range(2):
                            ins = act.activation(hT_hi[:, 2 * k + cc, :], b[:, cc * S:cc * S + S], ACT.Copy,
                                                 scale=gain(name, 2 * k + cc))
                    ins.then_inc(high_turned, 1)

            def fill(g):
                name, cols, at = half_of(g)
                act.wait_ge(block_landed[slot[name]], landed[name])
                if g >= PARTS:
                    before, second = split_names[(g - PARTS) // 2], (g - PARTS) % 2
                    if not second:
                        act.wait_ge(first_used, order[before] + 1)
                    elif reader_of[before][0] == "f2":
                        act.wait_ge(f2_done, reader_of[before][1] + 1)
                    else:
                        act.wait_ge(pe_done, done(reader_of[before]))
                act.activation(whi[at], ring[:, slot[name], cols], ACT.Copy).then_inc(high_made, 1)

            def refill(name, half):
                g = 2 * order[name] + half + PARTS
                if g < 2 * len(split_names):
                    fill(g)

            def squares_of_x(m):
                for t in range(NT):
                    act.wait_ge(ssq_ready, 2 * m + t)
                    act.activation(h[:, t, :], x[:, t, :], ACT.Square, accum_out=ssq[:, m, t:t + 1]).then_inc(ssq_ready, 1)

            def root(m):
                act.wait_ge(rstd_ready, m + 1)

            def tokens_out(stage, nb, dst, m=None, func=ACT.Copy, width=512):
                for t in range(NT):
                    copy_out((stage, nb, t), dst[:, t, nb * width:(nb + 1) * width], bank((stage, nb, t))[:, 0:width],
                             1.0 if m is None else rstd[:, m, t:t + 1], func)

            act.dma_start(x[:, :, :], w["x"].rearrange("b (t p) n -> p (b t) n", p=P)).then_inc(x_landed, 16)
            act.dma_start(cst[:, :], w["tables"]).then_inc(tables_landed, 16)
            act.dma_start(vrows[:, :], w["vecs"]).then_inc(vecs_landed, 16)
            for l in range(2):
                act.dma_start(p_tok[:, l], w["p"][l, 0].rearrange("(t p) n -> p t n", p=P)).then_inc(p_landed, 16)
            act.dma_start(aux[:, 2048:2048 + NPOOL], w["pools"]).then_inc(pools_landed, 16)
            act.wait_ge(x_landed, 16)
            squares_of_x(0)
            act.wait_ge(gains_ready, 3)
            for l in range(2):
                copy_out(("pT", l), pT[:, l, :, :].rearrange("p c s -> p (c s)"))
            turned_high("a", "a_norm")
            for g in range(PARTS):
                fill(g)
            root(0)
            for nb in range(2):
                refill(("u", nb), 0)
                tokens_out("u", nb, u_tok, 0)
                refill(("u", nb), 1)
            for nb in range(2):
                refill(("za", nb), 0)
                tokens_out("za", nb, z_tok, 0, ACT.Silu)
                if nb == 0:
                    refill(("za", 0), 1)
            for g in range(4):
                copy_out(("pool", g), pooledT[:, 2 * g:2 * g + 2, :].rearrange("p c s -> p (c s)"))
            turned_high("mixed", "a_scale")
            refill(("za", 1), 1)
            refill(("a_out", 0), 0)
            refill(("a_out", 0), 1)
            refill(("a_out", 1), 0)
            turned_high("x0", None)
            refill(("a_out", 1), 1)
            for nb in range(2):
                tokens_out("ple0", nb, pl_tok)

            sigs = [0]

            def gate(name):
                b = filled(name)
                n = sigs[0]
                sigs[0] += 1
                if n >= 2:
                    act.wait_ge(x_updated, n - 1)
                act.activation(sig[:, n % 2, :], b[:, :], ACT.Sigmoid).then_inc(act_emptied, 1)

            for nb in range(2):
                refill(("gate0", nb), 0)
                for t in range(NT):
                    gate(("gate0", nb, t))
                if nb == 0:
                    refill(("gate0", 0), 1)
            turned_high("kv", "kv_norm")
            refill(("gate0", 1), 1)
            act.wait_ge(x_updated, 4)
            squares_of_x(1)
            root(1)
            for nb in range(2):
                refill(("k", nb), 0)
                tokens_out("k", nb, k_tok, 1)
                refill(("k", nb), 1)
            for nb in range(2):
                refill(("v", nb), 0)
                tokens_out("v", nb, v_tok, 1)
                if nb == 0:
                    refill(("v", 0), 1)
            turned_high("qz", "b_norm")
            refill(("v", 1), 1)
            turned_out("k", [(kT, "k_norm", True)])
            for nb in range(2):
                refill(("q", nb), 0)
                tokens_out("q", nb, q_tok, 1)
                refill(("q", nb), 1)
            for nb in range(2):
                refill(("zb", nb), 0)
                tokens_out("zb", nb, z_tok, 1, ACT.Silu)
                if nb == 0:
                    turned_out("q", [(qT, "q_norm", True)])
                    refill(("zb", 0), 1)
            for i in range(NH + 3):
                if i < NH:
                    b = filled(("logits", i))
                    if i >= 3:
                        act.wait_ge(sp_ready, i - 2)
                    link(act.activation(logs[:, i % 3, :], b[:, 0:384], ACT.Abs))
                    link(act.activation(logs[:, i % 3, :], logs[:, i % 3, :], ACT.Exp, scale=-1.0))
                    act.activation(logs[:, i % 3, :], logs[:, i % 3, :], ACT.Ln, bias=1.0).then_inc(logs_ready, 1)
                if 2 <= i < NH + 2:
                    n = i - 2
                    b = filled(("loga", n))
                    act.activation(sticks[:, n % 3, :], b[:, 0:384], ACT.Exp).then_inc(act_emptied, 1)
            turned_high("o1", None)
            refill(("zb", 1), 1)
            refill(("b_out", 0), 0)
            refill(("b_out", 0), 1)
            refill(("b_out", 1), 0)
            turned_high("x1", None)
            refill(("b_out", 1), 1)
            for nb in range(2):
                tokens_out("ple1", nb, pl_tok)
            for nb in range(2):
                refill(("gate1", nb), 0)
                for t in range(NT):
                    gate(("gate1", nb, t))
                if nb == 0:
                    refill(("gate1", 0), 1)
            turned_high("mix0", "mix0")
            refill(("gate1", 1), 1)
            act.wait_ge(x_updated, 8)
            squares_of_x(2)
            root(2)
            refill("wc", 0)
            tokens_out("wc", 0, cbuf, 2, width=416)
            refill("wc", 1)
            for name, dst in (("wq", qb), ("wk", kb), ("wv", vb)):
                refill(name, 0)
                tokens_out(name, 0, dst, 2)
                if name != "wv":
                    refill(name, 1)
            tq, tk = turned_qk["moba"]
            turned_out("qmoba", [(tq, "qn_moba", True)], units=(1,))
            turned_out("kmoba", [(tk, "kn_moba", True)], units=(1,))
            act.wait_ge(lowr_ready, 1)
            for nb in range(2):
                for t in range(NT):
                    copy_out(("uq", nb, t), qm[:, t, nb * 384:(nb + 1) * 384], bank(("uq", nb, t))[:, 0:384],
                             lowr[:, t:t + 1])
            for nb in range(2):
                for t in range(NT):
                    b = filled(("ukv", nb, t))
                    v = b[:, :].rearrange("p (h n) -> p h n", h=4)
                    kv = km[:, t, :].rearrange("p (h n) -> p h n", h=MH)
                    act.activation(kv[:, 4 * nb:4 * nb + 4, 0:MNOPE], v[:, :, 0:MNOPE], ACT.Copy, scale=lowr[:, 2 + t:3 + t])
                    act.activation(vm[:, t, 256 * nb:256 * nb + 256].rearrange("p (h n) -> p h n", h=4), v[:, :, MNOPE:P],
                                   ACT.Copy, scale=lowr[:, 2 + t:3 + t]).then_inc(act_emptied, 1)
            for n, kind in enumerate(("moba", "mla")):
                moba = kind == "moba"
                tq, tk = turned_qk[kind]
                if not moba:
                    turned_out("qmla", [(tq, "qn_mla", True)], width=MQK)
                    turned_out("kmla", [(tk, "kn_mla", True)], width=MQK)
                for i in range(MH):
                    b = filled(("scores", kind, i))
                    act.wait_ge(max_ready, MH * n + i + 1)
                    if i >= 3:
                        act.wait_ge(pe_done, done(("probsT", kind, i - 3)))
                    act.activation(probs[:, i % 3, 0:P], b[:, 0:P], ACT.Exp, bias=nmax[:, n, i, 0:1],
                                   accum_out=den[:, n, i, 0:1])
                    act.activation(probs[:, i % 3, P:384], b[:, P:384], ACT.Exp, bias=nmax[:, n, i, 1:2],
                                   accum_out=den[:, n, i, 1:2]).then_inc(act_emptied, 1)
            turned_high("o2", None)
            refill("wv", 1)
            refill(("w_o", 0), 0)
            refill(("w_o", 0), 1)
            refill(("w_o", 1), 0)

            def mlp(layer, m):
                turned_high(("ffn", layer), f"ffn{layer}")
                refill(("gate", 1) if layer else ("w_o", 1), 1)
                squares_of_x(m)
                for i in range(FB + 1):
                    if i:
                        for k in range(2):
                            b = filled(("fT", layer, i - 1, k))
                            act.activation(hidT_hi[:, 2 * k:2 * k + 2, :].rearrange("p c s -> p (c s)"), b[:, :],
                                           ACT.Copy).then_inc(high_turned, 1)
                    late = layer == 0 and i == 2
                    if i < FB:
                        if not late:
                            refill(("f1", layer, i), 0)
                        for t in range(NT):
                            b = filled((("f1", layer, i), 0, t))
                            act.activation(hid[:, t, :], b[:, :], ACT.Relu).then_inc(relu_ready, 1)
                    if layer == 0 and i == 0:
                        act.wait_ge(lam_landed, 48)
                        act.activation(log_dt[:, 1:2], log_dt[:, 0:1], ACT.Exp).then_inc(dt_ready, 1)
                        act.wait_ge(zr_ready, 1)
                        act.activation(lam[:, 5, :], lam[:, 3, :], ACT.Exp).then_inc(exp_ready, 1)
                        act.wait_ge(angle_ready, 1)
                        act.activation(lam[:, 8:10, :], lam[:, 6:8, :], ACT.Sin).then_inc(sin_ready, 1)
                    if layer == 0 and i == 2:
                        for k in range(3):
                            q = min(8, 20 - 8 * k)
                            copy_out(("powT", k), powT[:, 8 * k:8 * k + q, :].rearrange("p q g -> p (q g)"),
                                     bank(("powT", k))[:, 0:q * G])
                    if late:
                        refill(("f2", 0, 0), 1)
                        refill(("f1", 0, 2), 0)
                    if i < FB:
                        refill(("f1", layer, i), 1)
                    if layer == 0 and i >= 3:
                        injects_out(i - 3)
                    if i and (layer or i < FB):
                        refill(("f2", layer, i - 1), 0)
                    if i and (layer or 1 < i < FB - 1):
                        refill(("f2", layer, i - 1), 1)

            def injects_out(f):
                if f:
                    act.wait_ge(w_stored, 16 * f)
                for k in range(2):
                    copy_out(("wT", f, k), inject_T[:, 512 * k:512 * k + 512])

            mlp(0, 3)
            injects_out(FB - 2)
            act.wait_ge(dve_emptied, u.emptied(("acc", 0, 3)))
            squares_of_x(4)
            injects_out(FB - 1)
            act.wait_ge(h_normed, 2)
            act.wait_ge(pe_done, done(("taps", FB - 1)))
            act.wait_ge(v_stored, 16 * 8)
            for half in range(2):
                if half:
                    act.wait_ge(w_stored, 16 * 8)
                    act.wait_ge(t_stored, 16 * 8)
                for t in range(NT):
                    act.dma_start(xc[half][16 * t:16 * t + 16, :, :],
                                  h[:, t, 512 * half:512 * half + 512]).then_inc(chunked[half], 16)
            act.wait_ge(chunked[1], 32)
            act.activation(xg[:, 32:64].rearrange("p g j i -> p j g i"),
                           xc[1].rearrange("p j (g i) -> p j g i", i=GI), ACT.Copy).then_inc(regrouped_b, 1)
            turned_out("mix1", [(uT, "mix1", False)])
            for n in range(4):
                b = filled(("inject", n))
                act.activation(states[:, 0, 1:NC + 1, 16 * n:16 * n + 16], b[:, :].rearrange("p (g c) -> p c g", g=16),
                               ACT.Copy).then_inc(act_emptied, 1)
            for n in range(4):
                copy_out(("injectx", n), states[:, 1, 1 + 8 * n:9 + 8 * n, :].rearrange("p c g -> p (c g)"))
            refill(("f2", 0, FB - 2), 1)
            refill(("f2", 0, FB - 1), 0)
            for n in range(4):
                b = filled(("state_out", n))
                dst = yc[:, n // 2, :, 64 * (n % 2):64 * (n % 2) + 64].rearrange("p j (g o) -> p j g o", g=4)
                act.activation(dst, b[:, :].rearrange("p (g j o) -> p j g o", g=4, j=L), ACT.Copy).then_inc(act_emptied, 1)
            for n in range(4):
                act.wait_ge(dve_emptied, u.emptied(("state_outT", 2 * (n // 2) + 1)))
                yv = ybuf[:, 2 * n:2 * n + 2, :]
                link(act.activation(yv, yv, ACT.Gelu_apprx_tanh))
                act.activation(hT_hi[:, 2 * n:2 * n + 2, :], yv, ACT.Copy).then_inc(gelu_high, 1)
            refill(("f2", 0, FB - 1), 1)
            for hh in range(2):
                refill(("val", hh), 0)
                refill(("val", hh), 1)
                refill(("gate", hh), 0)
                for t in range(NT):
                    gate((("gate", hh), 0, t))
                if hh == 0:
                    refill(("gate", 0), 1)
            mlp(1, 5)

        @block.vector
        def _(dve):
            steps_done = [0]

            def link(ins):
                steps_done[0] += 1
                ins.then_inc(dve_step, 1)
                dve.wait_ge(dve_step, steps_done[0])

            def filled(name):
                dve.wait_ge(pe_done, done(name))
                return bank(name)

            def emptied(name):
                dve.wait_ge(act_emptied, u.emptied(name))

            def turned_out(stage, pairs, units=(0, 2), width=P, chunks=8):
                for k in units:
                    b = filled(("T", stage, k))
                    for n, (dst, name, one) in enumerate(pairs):
                        if name is None:
                            ins = dve.tensor_copy(dst[0:width, 2 * k:2 * k + 2, :].rearrange("p c s -> p (c s)"),
                                                  b[0:width, :])
                            continue
                        for cc in range(min(2, chunks - 2 * k)):
                            c = 2 * k + cc
                            ins = dve.tensor_scalar(dst[0:width, c, :], b[0:width, cc * S:cc * S + S],
                                                    gain(name, 0 if one else c, width), None, ALU.mult)
                    ins.then_inc(dve_emptied, 1)

            def turned_low(stage, name):
                for k in range(4):
                    b = bank(("T", stage, k))
                    dve.wait_ge(high_turned, u.high[("T", stage, k)])
                    for cc in range(2):
                        c = 2 * k + cc
                        ins = dve.scalar_tensor_tensor(out=hT_lo[:, c, :], in0=b[:, cc * S:cc * S + S],
                                                       scalar=1.0 if name is None else gain(name, c), in1=hT_hi[:, c, :],
                                                       op0=ALU.mult, op1=ALU.subtract)
                    ins.then_inc(dve_emptied, 1)

            def fill(g):
                name, cols, at = half_of(g)
                dve.wait_ge(high_made, g + 1)
                dve.tensor_tensor(wlo[at], ring[:, slot[name], cols], whi[at], ALU.subtract).then_inc(low_made, 1)

            def refill(name, half):
                g = 2 * order[name] + half + PARTS
                if g < 2 * len(split_names):
                    fill(g)

            def refills(*names):
                for name in names:
                    refill(name, 0)
                    refill(name, 1)

            def means(m):
                dve.wait_ge(ssq_ready, 2 * m + 2)
                dve.tensor_scalar(ms[:, m, :], ssq[:, m, :], 1.0 / D, EPS, ALU.mult, ALU.add).then_inc(ms_ready, 1)

            def add_to_x(stage, nb_at, nb, t):
                b = filled((stage, nb, t))
                xs = x[:, t, nb_at * 512:(nb_at + 1) * 512]
                dve.tensor_tensor(xs, xs, b[:, :], ALU.add).then_inc(dve_emptied, 1)

            dve.memset(allneg[:, :], -1.0).then_inc(masks_ready, 1)
            dve.wait_ge(tables_landed, 16)
            dve.tensor_copy(bf[:, 0, :], ident).then_inc(masks_ready, 1)
            dve.tensor_copy(bf[:, 1, :], const("mask_st")).then_inc(masks_ready, 1)
            dve.tensor_copy(bf[:, 2, :], const("mask_ts")).then_inc(masks_ready, 1)
            b = filled("vec")
            dve.tensor_copy(vcols[:, :], b[:, 0:NVEC]).then_inc(dve_emptied, 1)
            dve.wait_ge(dve_emptied, 1)
            for name, scale in (("q_norm", HD ** -0.5), ("qn_moba", HD ** -0.5), ("qn_mla", MQK ** -0.5)):
                dve.tensor_scalar(gain(name), gain(name), scale, None, ALU.mult).then_inc(gains_ready, 1)
            dve.wait_ge(gains_ready, 3)
            means(0)
            turned_low("a", "a_norm")
            for g in range(PARTS):
                fill(g)
            refills(("u", 0), ("u", 1), ("za", 0))
            refill(("za", 1), 0)
            for nb in range(2):
                for t in range(NT):
                    b = filled(("mixed", nb, t))
                    emptied(("za", nb, t))
                    dve.tensor_tensor(h[:, t, nb * 512:(nb + 1) * 512], b[:, :], z_tok[:, t, nb * 512:(nb + 1) * 512],
                                      ALU.mult).then_inc(dve_emptied, 1)
            turned_low("mixed", "a_scale")
            refill(("za", 1), 1)
            for nb in range(2):
                refill(("a_out", nb), 0)
                for t in range(NT):
                    add_to_x("a_out", nb, nb, t)
                if nb == 0:
                    refill(("a_out", 0), 1)

            gates = [0]

            def gate_in(name, t, nb, other, free):
                n = gates[0]
                gates[0] += 1
                emptied(name)
                s = sig[:, n % 2, :]
                ins = dve.tensor_tensor(s, s, other, ALU.mult)
                if free:
                    ins.then_inc(dve_emptied, 1)
                    dve.wait_ge(dve_emptied, u.emptied(free))
                else:
                    link(ins)
                xs = x[:, t, nb * 512:(nb + 1) * 512]
                dve.tensor_tensor(xs, xs, s, ALU.add).then_inc(x_updated, 1)

            turned_low("x0", None)
            refill(("a_out", 1), 1)
            for nb in range(2):
                refill(("gate0", nb), 0)
                for t in range(NT):
                    gate_in(("gate0", nb, t), t, nb, pl_tok[:, t, nb * 512:(nb + 1) * 512], None)
                if nb == 0:
                    refill(("gate0", 0), 1)
            turned_low("kv", "kv_norm")
            refill(("gate0", 1), 1)
            means(1)

            def norm_heads(buf, n, width):
                sq = squares[:, 0:n * width].rearrange("p (n c) -> p n c", n=n)
                k = headnorms[0] = headnorms[0] + 1
                link(dve.tensor_tensor(sq, buf, buf, ALU.mult))
                link(dve.tensor_reduce(ssh[:, 0:n], sq, AX_X, ALU.add))
                dve.tensor_scalar(msh[:, 0:n], ssh[:, 0:n], 1.0 / width, EPS, ALU.mult, ALU.add).then_inc(headms_ready, 1)
                dve.wait_ge(headr_ready, k)
                dve.tensor_tensor(buf, buf, rsh[:, 0:n].unsqueeze(2).broadcast_to([P, n, width]), ALU.mult)\
                    .then_inc(heads_normed, 1)

            headnorms = [0]
            refills(("k", 0), ("k", 1))
            emptied(("k", 1, 1))
            norm_heads(work[:, 2048:4096].rearrange("p (n c) -> p n c", c=HD), NT * NH, HD)
            refills(("v", 0))
            refill(("v", 1), 0)
            turned_low("qz", "b_norm")
            turned_out("k", [(kT, "k_norm", True)])
            refill(("v", 1), 1)
            refills(("q", 0), ("q", 1))
            emptied(("q", 1, 1))
            norm_heads(work[:, 0:2048].rearrange("p (n c) -> p n c", c=HD), NT * NH, HD)
            refill(("zb", 0), 0)
            turned_out("q", [(qT, "q_norm", True)])
            refill(("zb", 0), 1)
            refill(("zb", 1), 0)
            emptied(("zb", 1, 1))
            for i in range(NH + 3):
                if i < NH:
                    b = bank(("logits", i))
                    dve.wait_ge(logs_ready, i + 1)
                    dve.scalar_tensor_tensor(out=sps[:, i % 3, :], in0=b[:, 0:384], scalar=0.0, in1=logs[:, i % 3, :],
                                             op0=ALU.max, op1=ALU.add).then_inc(sp_ready, 1)
                if i >= 3 and (i - 3) % 4 == 3:
                    k = (i - 3) // 4
                    b = filled(("stick_out", k))
                    hv, zv = (a[:, :, 256 * k:256 * k + 256].rearrange("p t (n d) -> p n t d", d=HD) for a in (h, z_tok))
                    dve.tensor_tensor(hv, b[:, :].rearrange("p (n t d) -> p n t d", n=4, t=NT), zv, ALU.mult)\
                        .then_inc(dve_emptied, 1)
            turned_low("o1", None)
            refill(("zb", 1), 1)
            for nb in range(2):
                refill(("b_out", nb), 0)
                for t in range(NT):
                    add_to_x("b_out", nb, nb, t)
                if nb == 0:
                    refill(("b_out", 0), 1)
            turned_low("x1", None)
            refill(("b_out", 1), 1)
            for nb in range(2):
                refill(("gate1", nb), 0)
                for t in range(NT):
                    gate_in(("gate1", nb, t), t, nb, pl_tok[:, t, nb * 512:(nb + 1) * 512], None)
                if nb == 0:
                    refill(("gate1", 0), 1)

            turned_low("mix0", "mix0")
            refill(("gate1", 1), 1)
            means(2)
            refills("wc")
            emptied(("wc", 0, 1))
            sq = squares[:, 0:768].rearrange("p (t n) -> p t n", t=NT)
            link(dve.tensor_tensor(sq, cbuf[:, :, 0:384], cbuf[:, :, 0:384], ALU.mult))
            link(dve.tensor_reduce(lowss[:, 0:2], sq[:, :, 0:256], AX_X, ALU.add))
            link(dve.tensor_reduce(lowss[:, 2:4], sq[:, :, 256:384], AX_X, ALU.add))
            dve.tensor_scalar(lowms[:, 0:2], lowss[:, 0:2], 1.0 / 256, EPS, ALU.mult, ALU.add).then_inc(lowms_ready, 1)
            dve.tensor_scalar(lowms[:, 2:4], lowss[:, 2:4], 1.0 / 128, EPS, ALU.mult, ALU.add).then_inc(lowms_ready, 1)
            emptied(("wq", 0, 1))
            norm_heads(work[:, 4096:5120].rearrange("p (n c) -> p n c", c=HD), NT * MH, HD)
            refills("wq")
            emptied(("wk", 0, 1))
            norm_heads(work[:, 5120:6144].rearrange("p (n c) -> p n c", c=HD), NT * MH, HD)
            turned_out("c", [(cT, "g_cq", False)], units=(0, 1), chunks=3)
            refills("wk")
            refill("wv", 0)
            tq, tk = turned_qk["moba"]
            turned_out("qmoba", [(tq, "qn_moba", True)], units=(0,))
            turned_out("kmoba", [(tk, "kn_moba", True)], units=(0,))

            def rotate(a1, a2, out1, out2, n, spread):
                cs, sn = (const(name).rearrange("p (t c) -> p t c", t=NT) for name in ("cos", "sin"))
                part = [ropes[:, k, :, 0:n, :] for k in range(4)]
                if n > 1:
                    cs, sn = (a.unsqueeze(2).broadcast_to([P, NT, n, 16]) for a in (cs, sn))
                else:
                    part = [a[:, :, 0, :] for a in part]
                for o, a, c in zip(part, (a1, a2, a1, a2), (cs, sn, sn, cs)):
                    ins = dve.tensor_tensor(o, a, c, ALU.mult)
                link(ins)
                if spread:
                    part = [a.unsqueeze(2).broadcast_to([P, NT, MH, 16]) for a in part]
                dve.tensor_tensor(out1, part[0], part[1], ALU.subtract)
                link(dve.tensor_tensor(out2, part[2], part[3], ALU.add))

            def mla_rows(step):
                qh = qm.rearrange("p t (h c) -> p t h c", h=MH)
                kh = km.rearrange("p t (h c) -> p t h c", h=MH)
                if step == 1:
                    emptied(("uq", 1, 1))
                    rotate(qh[:, :, :, 64:80], qh[:, :, :, 80:96], qh[:, :, :, 64:80], qh[:, :, :, 80:96], MH, False)
                if step == 2:
                    norm_heads(work[:, 0:1536].rearrange("p (n c) -> p n c", c=MQK), NT * MH, MQK)
                if step == 3:
                    emptied(("ukv", 1, 1))
                    rotate(cbuf[:, :, 384:400], cbuf[:, :, 400:416], kh[:, :, :, 64:80], kh[:, :, :, 80:96], 1, True)
                if step == 4:
                    norm_heads(work[:, 1536:3072].rearrange("p (n c) -> p n c", c=MQK), NT * MH, MQK)

            for n, kind in enumerate(("moba", "mla")):
                moba = kind == "moba"
                tq, tk = turned_qk[kind]
                if not moba:
                    turned_out("qmla", [(tq, "qn_mla", True)], width=MQK)
                    turned_out("kmla", [(tk, "kn_mla", True)], width=MQK)
                for i in range(MH + 3):
                    if i < MH:
                        b = filled(("scores", kind, i))
                        dve.tensor_reduce(nmax[:, n, i, 0:1], b[:, 0:P], AX_X, ALU.max, negate=True)
                        dve.tensor_reduce(nmax[:, n, i, 1:2], b[:, P:384], AX_X, ALU.max, negate=True)\
                            .then_inc(max_ready, 1)
                    if 2 <= i < MH + 2:
                        b = filled(("probsT", kind, i - 2))
                        dve.tensor_copy(probsT[:, (i - 2) % 3, :], b[:, 0:384]).then_inc(dve_emptied, 1)
                    if moba:
                        mla_rows(i)
                    if i >= 3 and (i - 3) % 4 == 3:
                        k = (i - 3) // 4
                        b = filled(("soft_out", kind, k))
                        emptied(("scores", kind, 4 * k + 3))
                        link(dve.reciprocal(rden[:, n, 4 * k:4 * k + 4, :], den[:, n, 4 * k:4 * k + 4, :]))
                        at = (512 if moba else 0) + 256 * k
                        dve.tensor_tensor(h[:, :, at:at + 256].rearrange("p t (n d) -> p n t d", d=HD),
                                          b[:, :].rearrange("p (n t d) -> p n t d", n=4, t=NT),
                                          rden[:, n, 4 * k:4 * k + 4, :].unsqueeze(3).broadcast_to([P, 4, NT, HD]),
                                          ALU.mult).then_inc(dve_emptied, 1)
            turned_low("o2", None)
            refill("wv", 1)
            for nb in range(2):
                refill(("w_o", nb), 0)
                for t in range(NT):
                    add_to_x("w_o", nb, nb, t)
                if nb == 0:
                    refill(("w_o", 0), 1)

            def s5_powers():
                tau = 2 * np.pi
                c1 = 6.28125
                c2 = float(np.float32(np.round((tau - c1) * 2 ** 20) / 2 ** 20))
                c3 = float(np.float32(tau - c1 - c2))
                magic = 12582912.0
                lr, li = lam[:, 0, :], lam[:, 1, :]
                dve.wait_ge(dt_ready, 1)
                dve.wait_ge(lam_landed, 48)
                dt = log_dt[:, 1:2]
                dve.tensor_scalar(lam[:, 3, :], lr, dt, None, ALU.mult).then_inc(zr_ready, 1)
                link(dve.tensor_scalar(lam[:, 4, :], li, dt, 0.5, ALU.mult, ALU.mult))
                link(dve.tensor_scalar(lam[:, 10, :], lam[:, 4, :], 0.5 * np.pi, None, ALU.add))
                for a, o in ((lam[:, 4, :], lam[:, 6, :]), (lam[:, 10, :], lam[:, 7, :])):
                    turns = lam[:, 11, :]
                    link(dve.tensor_scalar(turns, a, 1 / tau, magic, ALU.mult, ALU.add))
                    link(dve.tensor_scalar(turns, turns, magic, None, ALU.subtract))
                    link(dve.scalar_tensor_tensor(out=o, in0=turns, scalar=-c1, in1=a, op0=ALU.mult, op1=ALU.add))
                    link(dve.scalar_tensor_tensor(out=o, in0=turns, scalar=-c2, in1=o, op0=ALU.mult, op1=ALU.add))
                    link(dve.scalar_tensor_tensor(out=o, in0=turns, scalar=-c3, in1=o, op0=ALU.mult, op1=ALU.add))
                    ins = dve.tensor_scalar(o, o, 3.1415925, -3.1415925, ALU.min, ALU.max)
                    link(ins)
                dve.tensor_copy(lam[:, 12, :], lam[:, 4, :]).then_inc(angle_ready, 1)
                dve.wait_ge(sin_ready, 1)
                dve.wait_ge(exp_ready, 1)
                e, sn, co = lam[:, 5, :], lam[:, 8, :], lam[:, 9, :]
                s2, es, es2, e1, cosv = (lam[:, n, :] for n in (12, 13, 14, 15, 16))
                link(dve.tensor_tensor(s2, sn, sn, ALU.mult))
                dve.tensor_tensor(es, e, sn, ALU.mult)
                dve.tensor_tensor(es2, e, s2, ALU.mult)
                dve.tensor_scalar(e1, e, -1.0, None, ALU.add)
                link(dve.tensor_scalar(cosv, s2, -2.0, 1.0, ALU.mult, ALU.add))
                re, im = powers[:, 0], powers[:, 1]
                dve.tensor_tensor(re[:, 0, :], e, cosv, ALU.mult)
                dve.scalar_tensor_tensor(out=im[:, 0, :], in0=es, scalar=2.0, in1=co, op0=ALU.mult, op1=ALU.mult)
                num = lam[:, 17, :]
                link(dve.scalar_tensor_tensor(out=num, in0=es2, scalar=-2.0, in1=e1, op0=ALU.mult, op1=ALU.add))
                a, b2, c, d, e2 = (lam[:, n, :] for n in (18, 19, 20, 21, 3))
                dve.tensor_tensor(a, lr, lr, ALU.mult)
                dve.tensor_tensor(b2, li, li, ALU.mult)
                dve.tensor_tensor(c, num, lr, ALU.mult)
                dve.tensor_tensor(d, im[:, 0, :], li, ALU.mult)
                link(dve.tensor_tensor(e2, im[:, 0, :], lr, ALU.mult))
                dve.tensor_tensor(lam[:, 4, :], num, li, ALU.mult)
                dve.tensor_tensor(a, a, b2, ALU.add)
                link(dve.tensor_tensor(c, c, d, ALU.add))
                link(dve.reciprocal(b2, a))
                link(dve.tensor_tensor(e2, e2, lam[:, 4, :], ALU.subtract))
                dve.tensor_tensor(pw[:, 18, 0, :], c, b2, ALU.mult)
                dve.tensor_tensor(pw[:, 18, 1, :], c, b2, ALU.mult)
                dve.tensor_tensor(pw[:, 19, 1, :], e2, b2, ALU.mult)
                for m in (1, 2, 4):
                    ar, ai = re[:, 0:m, :], im[:, 0:m, :]
                    br, bi = (v[:, m - 1:m, :].broadcast_to([G, m, GP]) for v in (re, im))
                    for n, (p1, p2) in enumerate(((ar, br), (ai, bi), (ar, bi), (ai, br))):
                        ins = dve.tensor_tensor(prods[:, n, 0:m, :], p1, p2, ALU.mult)
                    link(ins)
                    dve.tensor_tensor(re[:, m:2 * m, :], prods[:, 0, 0:m, :], prods[:, 1, 0:m, :], ALU.subtract)
                    link(dve.tensor_tensor(im[:, m:2 * m, :], prods[:, 2, 0:m, :], prods[:, 3, 0:m, :], ALU.add))
                dve.tensor_scalar(pw[:, 19, 0, :], pw[:, 19, 1, :], -1.0, None, ALU.mult)
                dve.memset(pw[:, 0, :, :], 1.0)
                dve.memset(pw[:, 9, :, :], 0.0)
                dve.tensor_copy(pw[:, 1:9, 0, :], re)
                dve.tensor_copy(pw[:, 1:9, 1, :], re)
                dve.tensor_scalar(pw[:, 10:18, 0, :], im, -1.0, None, ALU.mult)
                dve.tensor_copy(pw[:, 10:18, 1, :], im).then_inc(powers_ready, 1)

            def s5_inputs():
                sgn = const("sgn")[:, 0:1]
                for k in range(4):
                    b = filled(("bcT", k))
                    dst = (Bs, Cs)[k // 2][:, 8 * (k % 2):8 * (k % 2) + 8, :].rearrange("p i g -> p (i g)")
                    if k < 2:
                        dve.tensor_copy(dst, b[:, :]).then_inc(dve_emptied, 1)
                    else:
                        dve.tensor_scalar(dst, b[:, :], sgn, None, ALU.mult).then_inc(dve_emptied, 1)
                for k in range(4):
                    b = filled(("bcX", k))
                    dst = (Bx, Cx)[k // 2][:, 8 * (k % 2):8 * (k % 2) + 8, :].rearrange("p i g -> p (i g)")
                    dve.tensor_scalar(dst, b[:, :], 1.0 if k < 2 else -1.0, None, ALU.mult).then_inc(dve_emptied, 1)
                emptied(("powT", 2))
                dve.wait_ge(dve_emptied, u.emptied(("bcX", 3)))
                fr, fi = (powT[:, q, :].unsqueeze(1).broadcast_to([P, GI, G]) for q in (18, 19))
                m1, m2, m3 = (v[:, 0:1024].rearrange("p (i g) -> p i g", i=GI) for v in (t1, t2, work[:, 0:1024]))
                dve.tensor_tensor(m1, Bs, fr, ALU.mult)
                dve.tensor_tensor(m2, Bx, fi, ALU.mult)
                link(dve.tensor_tensor(m3, Bs, fi, ALU.mult))
                link(dve.tensor_tensor(Bs, m1, m2, ALU.add))
                link(dve.tensor_tensor(m1, Bx, fr, ALU.mult))
                dve.tensor_tensor(Bx, m1, m3, ALU.subtract).then_inc(inputs_scaled, 1)
                dve.wait_ge(inputs_scaled, 1)
                dve.tensor_copy(a8[:, 0, :], powT[:, 8, :])
                dve.tensor_copy(a8[:, 1, :], powT[:, 17, :])
                dve.tensor_scalar(a8[:, 2, :], powT[:, 17, :], -1.0, None, ALU.mult)

            def s5_inject(f):
                if f:
                    dve.wait_ge(pe_done, done(("taps", f - 1)))
                gs = slice(8 * f, 8 * f + 8)
                ar, ai = (powT[:, q:q + 8, gs][:, ::-1, :].rearrange("p q g -> p g q").unsqueeze(3)
                          .broadcast_to([P, 8, L, GI]) for q in (0, 9))
                bs, bx = (v[:, :, gs].rearrange("p i g -> p g i").unsqueeze(2).broadcast_to([P, 8, L, GI])
                          for v in (Bs, Bx))
                m1, m2 = (v[:, 0:1024].rearrange("p (g j i) -> p g j i", g=8, j=L) for v in (t1, t2))
                dve.tensor_tensor(m1, ar, bs, ALU.mult)
                link(dve.tensor_tensor(m2, ai, bx, ALU.mult))
                dve.tensor_tensor(inject, m1, m2, ALU.add).then_inc(injects_made, 1)
                dve.wait_ge(pads_zeroed, 1)
                diagonal = work[:, 9856:9856 + 8 * 144].rearrange("p (g n) -> p g n", n=144)[:, :, 0:GI]
                dve.tensor_copy(diagonal, Bs[:, :, gs].rearrange("p i g -> p g i")).then_inc(pads_filled, 1)

            def s5_taps(f):
                b = filled(("taps", f))
                if f:
                    dve.wait_ge(t_stored, 16 * f)
                dve.tensor_tensor(taps.rearrange("p (k g o) -> p k g o", k=L, g=8),
                                  b[:, 0:P].rearrange("p (k o) -> p k o", k=L).unsqueeze(2).broadcast_to([P, L, 8, GI]),
                                  const("bmask").rearrange("p (g o) -> p g o", g=8).unsqueeze(1)
                                  .broadcast_to([P, L, 8, GI]), ALU.mult).then_inc(dve_emptied, 1)

            def mlp(layer, m):
                turned_low(("ffn", layer), f"ffn{layer}")
                refill(("gate", 1) if layer else ("w_o", 1), 1)
                means(m)
                dve.wait_ge(ms_ready, m + 1)
                dve.reciprocal(inv[:, layer, :], ms[:, m, :]).then_inc(inv_ready, 1)
                for i in range(FB + 1):
                    if i:
                        for k in range(2):
                            b = bank(("fT", layer, i - 1, k))
                            dve.wait_ge(high_turned, u.high[("fT", layer, i - 1, k)])
                            lo, hi = (v[:, 2 * k:2 * k + 2, :].rearrange("p c s -> p (c s)") for v in (hidT_lo, hidT_hi))
                            dve.tensor_tensor(lo, b[:, :], hi, ALU.subtract).then_inc(dve_emptied, 1)
                    late = layer == 0 and i == 2
                    if i < FB:
                        if not late:
                            refill(("f1", layer, i), 0)
                        for t in range(NT):
                            b = bank((("f1", layer, i), 0, t))
                            dve.wait_ge(relu_ready, NT * (FB * layer + i) + t + 1)
                            dve.tensor_tensor(hid[:, t, :], b[:, :], hid[:, t, :], ALU.mult).then_inc(dve_emptied, 1)
                    if layer == 0 and i == 0:
                        s5_powers()
                    if layer == 0 and i == 2:
                        s5_inputs()
                    if late:
                        refill(("f2", 0, 0), 1)
                        refill(("f1", 0, 2), 0)
                    if i < FB:
                        refill(("f1", layer, i), 1)
                    if layer == 0 and i >= 3:
                        s5_taps(i - 3)
                    if layer == 0 and i >= 2:
                        s5_inject(i - 2)
                    if i and (layer or i < FB):
                        refill(("f2", layer, i - 1), 0)
                    if i and (layer or 1 < i < FB - 1):
                        refill(("f2", layer, i - 1), 1)
                dve.wait_ge(inv_ready, layer + 1)
                for t in range(NT):
                    for nb in range(2):
                        b = filled(("acc", layer, 2 * t + nb))
                        xs = x[:, t, nb * 512:(nb + 1) * 512]
                        dve.scalar_tensor_tensor(out=xs, in0=b[:, :], scalar=inv[:, layer, t:t + 1], in1=xs,
                                                 op0=ALU.mult, op1=ALU.add).then_inc(dve_emptied, 1)

            mlp(0, 3)
            s5_taps(FB - 2)

            means(4)
            s5_inject(FB - 1)
            dve.wait_ge(gain_landed, 16)
            dve.tensor_copy(gain_rows[:, 1, :].rearrange("p (j i) -> p j i", j=L),
                            gain_rows[:, 0, 0:GI].unsqueeze(1).broadcast_to([G, L, GI])).then_inc(gain_rows_ready, 1)
            dve.wait_ge(rstd_ready, 4)
            for t in range(NT):
                dve.tensor_scalar(h[:, t, :], x[:, t, :], rstd[:, 4, t:t + 1], None, ALU.mult).then_inc(h_normed, 1)
            s5_taps(FB - 1)
            dve.wait_ge(chunked[0], 32)
            dve.tensor_copy(xg[:, 0:32].rearrange("p g j i -> p j g i"),
                            xc[0].rearrange("p j (g i) -> p j g i", i=GI)).then_inc(regrouped_a, 1)
            b = filled("gain_gi")
            dve.tensor_copy(gain_gi[:, :], b[:, 0:G]).then_inc(dve_emptied, 1)
            dve.wait_ge(dve_emptied, u.emptied("gain_gi"))
            for n in range(4):
                b = filled(("ug", n))
                dve.tensor_tensor(ug[:, 16 * n:16 * n + 16, :], b[:, :].rearrange("p (g c) -> p g c", g=16),
                                  gain_gi[:, 16 * n:16 * n + 16].unsqueeze(2).broadcast_to([P, 16, NC]),
                                  ALU.mult).then_inc(dve_emptied, 1)
            dve.wait_ge(w_stored, 16 * 8)
            dve.wait_ge(t_stored, 16 * 8)
            turned_out("mix1", [(uT, "mix1", False)])
            link(dve.memset(states[:, :, 0, :], 0.0))
            emptied(("injectx", 3))
            ar = a8[:, 0:1, :].broadcast_to([P, 2, G])
            for c in range(2, NC):
                if c == NC // 2:
                    refill(("f2", 0, FB - 2), 1)
                    refill(("f2", 0, FB - 1), 0)
                before, now = states[:, :, c - 1, :], states[:, :, c, :]
                dve.tensor_tensor(steps[:, 0], ar, before, ALU.mult)
                link(dve.tensor_tensor(steps[:, 1], a8[:, 1:3, :], before[:, ::-1, :], ALU.mult))
                link(dve.tensor_tensor(steps[:, 0], steps[:, 0], steps[:, 1], ALU.add))
                ins = dve.tensor_tensor(now, now, steps[:, 0], ALU.add)
                if c < NC - 1:
                    link(ins)
            ins.then_inc(states_ready, 1)
            for n in range(4):
                b = filled(("fir", n))
                for fl in range(2):
                    f = 2 * n + fl
                    ins = dve.scalar_tensor_tensor(out=ybuf[:, f, :], in0=uT[:, f, :], scalar=gain("d_skip", f),
                                                   in1=b[:, fl * S:(fl + 1) * S], op0=ALU.mult, op1=ALU.add)
                ins.then_inc(dve_emptied, 1)
            for n in range(4):
                b = filled(("state_outT", n))
                dve.wait_ge(dve_emptied, u.emptied(("fir", 2 * (n // 2) + 1)))
                yv = ybuf[:, 4 * (n // 2):4 * (n // 2) + 4, :].rearrange("p c s -> p (c s)")\
                    .rearrange("p (n j) -> p n j", j=L)[:, :, 4 * (n % 2):4 * (n % 2) + 4]
                dve.tensor_tensor(yv, yv, b[:, :].rearrange("p (j n) -> p n j", j=4), ALU.add).then_inc(dve_emptied, 1)
            for n in range(4):
                dve.wait_ge(gelu_high, n + 1)
                dve.tensor_tensor(hT_lo[:, 2 * n:2 * n + 2, :], ybuf[:, 2 * n:2 * n + 2, :], hT_hi[:, 2 * n:2 * n + 2, :],
                                  ALU.subtract).then_inc(gelu_ready, 1)
            refill(("f2", 0, FB - 1), 1)
            for hh in range(2):
                refills(("val", hh))
                refill(("gate", hh), 0)
                for t in range(NT):
                    gate_in((("gate", hh), 0, t), t, hh, bank((("val", hh), 0, t))[:, :], (("val", hh), 0, t))
                if hh == 0:
                    refill(("gate", 0), 1)
            mlp(1, 5)

        @block.gpsimd
        def _(pool):
            pool.memset(half_neg[:, :], -0.5).then_inc(halves_ready, 1)
            pool.dma_start(gain_rows[:, 0, 0:GI], w["mix_norm_g_2"][1].rearrange("(g i) -> g i", i=GI))\
                .then_inc(gain_landed, 16)
            pool.wait_ge(halves_ready, 1)

            def root(m):
                pool.wait_ge(ms_ready, m + 1)
                pool.tensor_tensor(rstd[:, m, :], ms[:, m, :], half_neg[:, 0:NT], ALU.pow).then_inc(rstd_ready, 1)

            def head_root(k, n):
                pool.wait_ge(headms_ready, k)
                pool.tensor_tensor(rsh[:, 0:n], msh[:, 0:n], half_neg[:, 0:n], ALU.pow).then_inc(headr_ready, 1)

            root(0)
            root(1)
            head_root(1, NT * NH)
            head_root(2, NT * NH)
            root(2)
            pool.wait_ge(lowms_ready, 2)
            pool.tensor_tensor(lowr[:, :], lowms[:, :], half_neg[:, 0:4], ALU.pow).then_inc(lowr_ready, 1)
            for k in range(3, 7):
                head_root(k, NT * MH)
            pool.wait_ge(pe_done, done(("soft_out", "mla", 1)))
            pool.dma_start(lam[:, 0, :], w["lam_re_2"][0]).then_inc(lam_landed, 16)
            pool.dma_start(lam[:, 1, :], w["lam_im_2"][0]).then_inc(lam_landed, 16)
            pool.dma_start(log_dt[:, 0:1], w["log_dt_2"][0].rearrange("(g a) -> g a", a=1)).then_inc(lam_landed, 16)
            pool.memset(pads, 0.0).then_inc(pads_zeroed, 1)
            pool.wait_ge(inputs_scaled, 1)
            stored = 0
            for f in range(8):
                gs = slice(8 * f, 8 * f + 8)
                if f:
                    pool.wait_ge(pe_done, done(("taps", f - 1)))
                    pool.wait_ge(v_stored, 16 * f)
                ar, ai = (powT[:, q:q + 9, gs].rearrange("p q g -> p g q").unsqueeze(3)
                          .broadcast_to([P, 8, L + 1, GI]) for q in (0, 9))
                cs, cx = (v[:, :, gs].rearrange("p i g -> p g i").unsqueeze(2).broadcast_to([P, 8, L + 1, GI])
                          for v in (Cs, Cx))
                tmp = t3.rearrange("p (g k o) -> p g k o", g=8, k=L + 1)
                pool.tensor_tensor(readout, ar, cs, ALU.mult).then_inc(pool_step, 1)
                pool.tensor_tensor(tmp, ai, cx, ALU.mult).then_inc(pool_step, 1)
                pool.wait_ge(pool_step, 2 * f + 2)
                pool.tensor_tensor(readout, readout, tmp, ALU.add).then_inc(readouts_made, 1)
                pool.wait_ge(readouts_made, f + 1)
                if f == 7:
                    root(4)
                pool.dma_start(w["scratch_readout"][:, 1024 * f:1024 * f + 1024].rearrange("p (g n) -> p g n", g=8),
                               readout[:, :, 1:L + 1, :].rearrange("p g k o -> p g (k o)")).then_inc(v_stored, 16)
                pool.wait_ge(act_emptied, u.emptied(("wT", f, 1)))
                pool.dma_start(w["scratch_inject"][:, 1024 * f:1024 * f + 1024], inject_T).then_inc(w_stored, 16)
                pool.wait_ge(dve_emptied, u.emptied(("taps", f)))
                pool.dma_start(w["scratch_taps"][:, 1024 * f:1024 * f + 1024], taps).then_inc(t_stored, 16)


_INS = ["x", "p", "a_w_in", "a_w_group", "a_w_out", "w_kv", "b_w_in", "b_w_out", "ple_w", "ple_gate_w", "mix_norm_g_2",
        "w_in_2", "w_uq_2", "w_ukv_2", "w_o_2", "lam_re_2", "lam_im_2", "log_dt_2", "b_re_2", "b_im_2", "c_re_2",
        "c_im_2", "w_glu_2", "w_ff1_2", "w_ff2_2"]


def kernel(**inputs):
    import numpy as np
    import concourse.bacc as bacc
    from concourse.bass_utils import run_bass_kernel_spmd

    vecs = np.zeros((NVEC, P), np.float32)
    for name, v in (("a_norm", inputs["a_norm"][0]), ("a_scale", inputs["a_scale"][0]), ("kv_norm", inputs["kv_norm"]),
                    ("b_norm", inputs["b_norm"][0]), ("mix0", inputs["mix_norm_g_2"][0]),
                    ("mix1", inputs["mix_norm_g_2"][1]), ("ffn0", inputs["ffn_norm_g_2"][0]),
                    ("ffn1", inputs["ffn_norm_g_2"][1]), ("d_skip", inputs["d_skip_2"][0]),
                    ("g_cq", inputs["g_cq_2"][0]), ("g_ckv", inputs["g_ckv_2"][0]), ("k_norm", inputs["k_norm"]),
                    ("q_norm", inputs["b_q_norm"][0]), ("qn_mla", inputs["g_qn_mla_2"][0]),
                    ("kn_mla", inputs["g_kn_mla_2"][0]), ("qn_moba", inputs["g_qn_moba_2"][0]),
                    ("kn_moba", inputs["g_kn_moba_2"][0])):
        v = np.asarray(v)
        if v.size == HD:
            v = np.concatenate([v, v])
        if v.size % P:
            v = np.concatenate([v, np.zeros(-v.size % P, np.float32)])
        vecs[VEC_AT[name]:VEC_AT[name] + VEC_ROWS[name]] = v.reshape(-1, P)
    tables, pools = constants()

    nc = bacc.Bacc("TRN2", target_bir_lowering=False, num_devices=1)
    arrays, w = {}, {}
    given = {name: np.ascontiguousarray(inputs[name]) for name in _INS}
    for name, a in {**given, "vecs": vecs, "tables": tables, "pools": pools}.items():
        arrays[f"in_{name}"] = a
        w[name] = nc.dram_tensor(f"in_{name}", a.shape, mybir.dt.from_np(a.dtype), kind="ExternalInput").ap()
    for name in ("inject", "readout", "taps"):
        w["scratch_" + name] = nc.dram_tensor("scratch_" + name, (P, 2 * BLK), F32, kind="Internal").ap()
    out = nc.dram_tensor("out_0", (1, S, D), F32, kind="ExternalOutput").ap()
    program(nc, w, out)
    r = run_bass_kernel_spmd(nc, [arrays], core_ids=[0])
    return r.results[0]["out_0"]
```

```python
from contextlib import ExitStack

import concourse.bass as bass
from concourse import mybir

F32 = mybir.dt.float32
BF16 = mybir.dt.bfloat16
F32R = mybir.dt.float32r
ALU = mybir.AluOpType
ACT = mybir.ActivationFunctionType
AX_X = mybir.AxisListType.X

P = 128
S, D = 256, 1024
NT = S // P
KC = D // P
EPS = 1e-6
WINDOWS = (2, 4, 8, 16)
RING = 2
PARTS = 3
BLK = 4096
NH = 16
HD = 64
MH, MQK, MNOPE, MROPE = 8, 96, 64, 32
G, GI, GP = 64, 16, 64
L = 8
NC = S // L
FB = 8
BIG = -1.0e30
SPLIT = ("u", "za", "a_out", "gate0", "k", "v", "q", "zb", "b_out", "gate1", "wc", "wq", "wk", "wv", "w_o",
         "val", "gate", "f1", "f2")

VEC_ROWS = {"a_norm": 8, "a_scale": 8, "kv_norm": 8, "b_norm": 8, "mix0": 8, "ffn0": 8, "mix1": 8, "ffn1": 8,
            "d_skip": 8, "g_cq": 2, "g_ckv": 1, "k_norm": 1, "q_norm": 1, "qn_mla": 1, "kn_mla": 1,
            "qn_moba": 1, "kn_moba": 1}
VEC_AT = {}
for _n, _k in VEC_ROWS.items():
    VEC_AT[_n] = sum(VEC_ROWS[m] for m in VEC_AT)
NVEC = sum(VEC_ROWS.values())

CONST_COLS = {"ident": 128, "tneg": 128, "swap": 128, "bmask": 128, "mask_st": 128, "mask_ts": 128, "cos": 32,
              "sin": 32, "sgn": 2}
CONST_AT = {}
for _n, _k in CONST_COLS.items():
    CONST_AT[_n] = sum(CONST_COLS[m] for m in CONST_AT)
NCONST = sum(CONST_COLS.values())
NPOOL = 4 * 384


def constants():
    import numpy as np
    i = np.arange(P)
    c = np.zeros((P, NCONST), np.float32)

    def put(name, a):
        c[:, CONST_AT[name]:CONST_AT[name] + CONST_COLS[name]] = a

    put("ident", np.eye(P))
    put("tneg", -(i[:, None] >= i[None, :]).astype(np.float32))
    put("swap", np.roll(np.eye(P), 64, axis=1))
    put("bmask", (i[:, None] // GI == i[None, :] // GI))
    put("mask_st", np.where(i[:, None] >= i[None, :], BIG, 0))
    put("mask_ts", np.where(i[None, :] > i[:, None], BIG, 0))
    half = MROPE // 2
    inv = (np.float32(10000.0) ** (-np.arange(half, dtype=np.float32) / np.float32(half))).astype(np.float32)
    ang = (np.arange(S, dtype=np.float32)[:, None] * inv[None, :]).astype(np.float32)
    put("cos", np.cos(ang).reshape(NT, P, half).transpose(1, 0, 2).reshape(P, 32))
    put("sin", np.sin(ang).reshape(NT, P, half).transpose(1, 0, 2).reshape(P, 32))
    put("sgn", np.where(i[:, None] < 64, [[1.0, -1.0]], [[-1.0, 1.0]]))
    pool = np.zeros((P, 4, 384), np.float32)
    t = np.arange(S)
    for g, w in enumerate(WINDOWS):
        m = ((t[:, None] <= t[None, :]) & (t[:, None] > t[None, :] - w)) / np.minimum(t[None, :] + 1, w)
        m = m - np.eye(S)
        pool[:, g, 0:256] = m[0:P]
        pool[:, g, 256:384] = m[P:, P:]
    return c, pool.reshape(P, NPOOL)


class Units:

    def __init__(self):
        self.at, self.bank, self.before, self.by, self.count = {}, [], [], [], []
        self.last, self.turn, self.banks, self.high = {}, 0, list(range(8)), {}

    def add(self, name, freed_by, bank=None):
        if freed_by == "av":
            self.high[name] = len(self.high) + 1
            freed_by = "v"
        if bank is None:
            bank = self.banks[self.turn % len(self.banks)]
            self.turn += 1
        q = len(self.bank)
        assert name not in self.at, name
        self.at[name] = q
        self.bank.append(bank)
        self.before.append(self.last.get(bank))
        self.by.append(freed_by)
        self.count.append(self.by.count(freed_by))
        self.last[bank] = q

    def done(self, name):
        return self.at[name] + 1

    def emptied(self, name):
        return self.count[self.at[name]]


def gemm(u, stage, blocks, freed_by):
    for nb in range(blocks):
        for t in range(NT):
            u.add((stage, nb, t), freed_by)


def turned(u, stage, n=4):
    for k in range(n):
        u.add(("T", stage, k), "va"[k % 2])


def turned_in_two(u, stage, units=range(4)):
    for k in units:
        u.add(("T", stage, k), "av")


def plan():
    u = Units()
    u.add("vec", "v")
    turned_in_two(u, "a")
    gemm(u, "u", 2, "a")
    gemm(u, "za", 2, "a")
    for g in range(4):
        u.add(("pool", g), "a")
    gemm(u, "mixed", 2, "v")
    u.add(("pT", 0), "a")
    u.add(("pT", 1), "a")
    turned_in_two(u, "mixed")
    gemm(u, "a_out", 2, "v")
    turned_in_two(u, "x0", (0, 1))
    gemm(u, "ple0", 2, "a")
    turned_in_two(u, "x0", (2, 3))
    gemm(u, "gate0", 2, "a")
    turned_in_two(u, "kv")
    gemm(u, "k", 2, "a")
    gemm(u, "v", 2, "a")
    turned_in_two(u, "qz")
    turned(u, "k")
    gemm(u, "q", 2, "a")
    gemm(u, "zb", 2, "a")
    turned(u, "q")
    for j in range(NH // 2 + 2):
        for i in (2 * j, 2 * j + 1):
            if i < NH:
                u.add(("logits", i), "", bank=i % 6)
        for i in (2 * j - 2, 2 * j - 1):
            if 0 <= i < NH:
                u.add(("loga", i), "a", bank=i % 6)
        for i in (2 * j - 4, 2 * j - 3):
            if i >= 0 and i % 4 == 3:
                u.add(("stick_out", i // 4), "v", bank=6 + i // 4 % 2)
    turned_in_two(u, "o1")
    gemm(u, "b_out", 2, "v")
    turned_in_two(u, "x1", (0, 1))
    gemm(u, "ple1", 2, "a")
    turned_in_two(u, "x1", (2, 3))
    gemm(u, "gate1", 2, "a")
    turned_in_two(u, "mix0")
    gemm(u, "wc", 1, "a")
    gemm(u, "wq", 1, "a")
    gemm(u, "wk", 1, "a")
    u.add(("T", "c", 0), "v")
    u.add(("T", "c", 1), "v")
    gemm(u, "wv", 1, "a")
    turned(u, "qmoba", 2)
    turned(u, "kmoba", 2)
    gemm(u, "uq", 2, "a")
    gemm(u, "ukv", 2, "a")
    for kind in ("moba", "mla"):
        if kind == "mla":
            turned(u, "qmla")
            turned(u, "kmla")
        for i in range(MH + 3):
            if i < MH:
                u.add(("scores", kind, i), "a", bank=i % 4)
            if 2 <= i < MH + 2:
                u.add(("probsT", kind, i - 2), "v", bank=4 + i % 2)
            if i >= 3 and (i - 3) % 4 == 3:
                u.add(("soft_out", kind, (i - 3) // 4), "v", bank=6 + (i - 3) // 4)
    turned_in_two(u, "o2")
    gemm(u, "w_o", 2, "v")
    mlp_plan(u, 0)
    u.add("gain_gi", "v")
    for b in range(4):
        u.add(("ug", b), "v")
    for b in range(5):
        if b < 4:
            u.add(("added", b), "a")
        if b:
            u.add(("inject", b - 1), "a")
            u.add(("injectx", b - 1), "a")
    for b in range(4):
        u.add(("T", "mix1", b), "a")
    for b in range(4):
        u.add(("fir", b), "v")
    for b in range(4):
        u.add(("state_out", b), "a")
    for b in range(4):
        u.add(("state_outT", b), "v")
    for h in range(2):
        gemm(u, ("val", h), 1, "v")
        gemm(u, ("gate", h), 1, "a")
    mlp_plan(u, 1)
    return u


def mlp_plan(u, layer):
    turned_in_two(u, ("ffn", layer))
    u.banks, u.turn = [4, 5, 6, 7], 0

    def s5_chunk(f):
        u.add(("wT", f, 0), "a")
        u.add(("wT", f, 1), "a")
        u.add(("taps", f), "v")

    for i in range(FB + 1):
        if i:
            for k in range(2):
                u.add(("fT", layer, i - 1, k), "av")
        if i < FB:
            gemm(u, ("f1", layer, i), 1, "v")
        if layer == 0 and i == 2:
            for k in range(3):
                u.add(("powT", k), "a")
            for name in ("bcT", "bcX"):
                for k in range(4):
                    u.add((name, k), "v")
        if layer == 0:
            for f in chunks_before(i) + chunks_after(i):
                s5_chunk(f)
    for k in range(4):
        u.add(("acc", layer, k), "v", bank=k)
    u.banks, u.turn = list(range(8)), 4


def chunks_before(i):
    return [] if i < 3 else [i - 3] if i < FB - 1 else [FB - 3] if i == FB - 1 else [FB - 1]


def chunks_after(i):
    return [FB - 4] if i == FB - 2 else [FB - 2] if i == FB - 1 else []


def loads(w):
    def cols(a, c0, c1):
        return a[:, c0:c1].rearrange("(k p) n -> p k n", p=P)

    out = []
    a_in, a_out, w_kv, b_in, b_out = w["a_w_in"][0], w["a_w_out"][0], w["w_kv"], w["b_w_in"][0], w["b_w_out"][0]

    def add(name, parts, reader):
        out.append((name, parts, reader))

    def two(name, a, base, unit):
        for nb in range(2):
            add((name, nb), [(0, cols(a, base + 512 * nb, base + 512 * nb + 512))], (unit, nb, 1))

    two("u", a_in, 0, "u")
    two("za", a_in, D, "za")
    add("w_group", [(0, w["a_w_group"][0].rearrange("g (k p) n -> p (g k) n", p=P))], ("mixed", 1, 1))
    two("a_out", a_out, 0, "a_out")
    add("ple0", [(0, cols(w["ple_w"][0], 0, D))], ("ple0", 1, 1))
    two("gate0", w["ple_gate_w"][0], 0, "gate0")
    two("k", w_kv, 0, "k")
    two("v", w_kv, D, "v")
    two("q", b_in, 0, "q")
    two("zb", b_in, D, "zb")
    two("b_out", b_out, 0, "b_out")
    add("ple1", [(0, cols(w["ple_w"][1], 0, D))], ("ple1", 1, 1))
    two("gate1", w["ple_gate_w"][1], 0, "gate1")
    w_in = w["w_in_2"][0]
    add("wc", [(0, cols(w_in, 0, 416))], ("wc", 0, 1))
    add("wq", [(0, cols(w_in, 416, 928))], ("wq", 0, 1))
    add("wk", [(0, cols(w_in, 928, 1440))], ("wk", 0, 1))
    add("wv", [(0, cols(w_in, 1440, 1952))], ("wv", 0, 1))
    add("lowrank", [(0, cols(w["w_uq_2"][0], 0, 768)), (1536, cols(w["w_ukv_2"][0], 0, 1024))], ("ukv", 1, 1))
    two("w_o", w["w_o_2"][0], 0, "w_o")
    mlp_loads(w, add, cols, 0)
    def glu(name, h):
        base = 512 * h + (D if name == "gate" else 0)
        add((name, h), [(0, cols(w["w_glu_2"][0], base, base + 512))], ((name, h), 0, 1))

    for name, reader in (("inject", "added"), ("taps", "fir"), ("readout", "state_out")):
        if name == "readout":
            glu("val", 0)
        for half in range(2):
            add((name, half), [(0, w["scratch_" + name][:, half * BLK:half * BLK + BLK])], (reader, 2 * half + 1))
    for name, h in (("gate", 0), ("val", 1), ("gate", 1)):
        glu(name, h)
    mlp_loads(w, add, cols, 1)
    return out


def mlp_loads(w, add, cols, layer):
    w1, w2 = w["w_ff1_2"][layer], w["w_ff2_2"][layer]
    for i in range(FB + 1):
        if i < FB:
            add(("f1", layer, i), [(0, cols(w1, 512 * i, 512 * i + 512))], (("f1", layer, i), 0, 1))
        if i:
            add(("f2", layer, i - 1), [(0, w2[512 * (i - 1):512 * (i - 1) + 512, :].rearrange("(k p) n -> p k n", p=P))],
                ("f2", (FB - 1) * layer + i - 1) if i - 1 < FB - 1 else ("acc", layer, 3))


def program(nc, w, out):
    import numpy as np
    u = plan()
    blocks = loads(w)
    slot = {name: n % RING for n, (name, _, _) in enumerate(blocks)}
    landed = {}
    for n, (name, parts, _) in enumerate(blocks):
        before = landed[blocks[n - RING][0]] if n >= RING else 0
        landed[name] = before + 16 * len(parts)
    done = u.done
    split_names = [name for name, _, _ in blocks if name[0] in SPLIT or name in SPLIT]
    order = {name: n for n, name in enumerate(split_names)}
    reader_of = {name: reader for name, _, reader in blocks}
    size = {name: 8 * 416 if name == "wc" else BLK for name in split_names}

    with ExitStack() as ctx:
        def sb(name, shape, dt=F32):
            return ctx.enter_context(nc.sbuf_tensor(name, shape, dt))

        def sem(name):
            return ctx.enter_context(nc.semaphore(name))

        ps = [ctx.enter_context(nc.psum_tensor(f"bank{i}", [P, 512], F32)) for i in range(8)]

        x = sb("x", [P, NT, D])
        h = sb("h", [P, NT, D])
        hT_hi = sb("hT_hi", [P, KC, S], F32R)
        hT_lo = sb("hT_lo", [P, KC, S], F32R)
        hidT_hi = sb("hidT_hi", [P, 4, S], F32R)
        hidT_lo = sb("hidT_lo", [P, 4, S], F32R)
        work = sb("work", [P, 12288])
        aux = sb("aux", [P, 5504])
        ring = sb("ring", [P, RING, BLK])
        whi = sb("whi", [P, PARTS, BLK // 2], F32R)
        wlo = sb("wlo", [P, PARTS, BLK // 2], F32R)
        sig = sb("sig", [P, 2, 512])
        pT = sb("pT", [P, 2, 2, S])
        vrows = sb("vrows", [NVEC, P])
        vcols = sb("vcols", [P, NVEC])
        cst = sb("cst", [P, NCONST])
        bf = sb("bf", [P, 3, P], BF16)
        allneg = sb("allneg", [P, P])
        inv = sb("inv", [P, 2, NT])
        half_neg = sb("half_neg", [P, 32])
        ssq = sb("ssq", [P, 6, NT])
        ms = sb("ms", [P, 6, NT])
        rstd = sb("rstd", [P, 6, NT])
        ssh = sb("ssh", [P, 32])
        msh = sb("msh", [P, 32])
        rsh = sb("rsh", [P, 32])
        lowss = sb("lowss", [P, 4])
        lowms = sb("lowms", [P, 4])
        lowr = sb("lowr", [P, 4])
        nmax = sb("nmax", [P, 2, MH, NT])
        den = sb("den", [P, 2, MH, NT])
        rden = sb("rden", [P, 2, MH, NT])
        a8 = sb("a8", [P, 3, G])
        gain_rows = sb("gain_rows", [G, 2, P])
        gain_gi = sb("gain_gi", [P, G])
        log_dt = sb("log_dt", [G, 2])

        block_landed = [sem(f"block_landed{i}") for i in range(RING)]
        (pe_done, act_emptied, dve_emptied, x_landed, tables_landed, p_landed, pools_landed, vecs_landed,
         masks_ready, gains_ready, x_updated, ssq_ready, ms_ready, rstd_ready, headms_ready, headr_ready,
         heads_normed, logs_ready, sp_ready, lowms_ready, lowr_ready, max_ready, f2_done, halves_ready,
         dt_ready, zr_ready, exp_ready, angle_ready, sin_ready, lam_landed, powers_ready, pads_zeroed,
         inputs_scaled, injects_made, readouts_made, pads_filled, w_stored, v_stored, t_stored, h_normed,
         regrouped_a, regrouped_b, gain_rows_ready, gain_landed, states_ready, gelu_ready, act_step, dve_step, pool_step,
         out_stored) = (
            sem(n) for n in (
                "pe_done", "act_emptied", "dve_emptied", "x_landed", "tables_landed", "p_landed",
                "pools_landed", "vecs_landed", "masks_ready", "gains_ready", "x_updated",
                "ssq_ready", "ms_ready", "rstd_ready", "headms_ready", "headr_ready",
                "heads_normed", "logs_ready", "sp_ready", "lowms_ready", "lowr_ready", "max_ready",
                "f2_done", "halves_ready", "dt_ready", "zr_ready", "exp_ready", "angle_ready",
                "sin_ready", "lam_landed", "powers_ready", "pads_zeroed", "inputs_scaled",
                "injects_made", "readouts_made", "pads_filled", "w_stored", "v_stored", "t_stored",
                "h_normed", "regrouped_a", "regrouped_b", "gain_rows_ready", "gain_landed", "states_ready",
                "gelu_ready", "act_step", "dve_step", "pool_step", "out_stored"))

        chunked = [sem("chunked_a"), sem("chunked_b")]
        high_made, low_made, high_turned, inv_ready, gelu_high, relu_ready, first_used, exps_ready, bc_landed, first_landed = (
            sem(n) for n in ("high_made", "low_made", "high_turned", "inv_ready", "gelu_high", "relu_ready",
                             "first_used", "exps_ready", "bc_landed", "first_landed"))

        def half_of(g):
            name = split_names[g // 2]
            n = size[name] // 2
            return name, slice(n * (g % 2), n * (g % 2) + n), (slice(None), g % PARTS, slice(0, n))

        def const(name):
            return cst[:, CONST_AT[name]:CONST_AT[name] + CONST_COLS[name]]

        def gain(name, c=0, rows=P):
            return vcols[0:rows, VEC_AT[name] + c:VEC_AT[name] + c + 1]

        def weights(name, k, n, at=0):
            return ring[:, slot[name], at:at + k * n].rearrange("p (k n) -> p k n", k=k)

        def tok(at, n=D):
            return work[:, at:at + NT * n].rearrange("p (t n) -> p t n", t=NT)

        def bank(name):
            return ps[u.bank[u.at[name]]]

        ident, tneg = const("ident"), const("tneg")
        q_tok, k_tok, v_tok, z_tok = (tok(2048 * n) for n in range(4))
        u_tok = q_tok
        p_tok = work[:, 8192:9216].rearrange("p (l t n) -> p l t n", l=2, t=NT)
        pl_tok = aux[:, 0:2048].rearrange("p (t n) -> p t n", t=NT)
        pools = aux[:, 2048:2048 + NPOOL].rearrange("p (g n) -> p g n", g=4)
        qT = work[:, 8192:10240].rearrange("p (c s) -> p c s", c=KC)
        kT = work[:, 10240:12288].rearrange("p (c s) -> p c s", c=KC)
        squares = aux[:, 0:2048]
        logs, sps, sticks = (aux[:, 1536 * n:1536 * n + 1536].rearrange("p (b n) -> p b n", b=4) for n in range(3))
        qm, km = tok(0, MH * MQK), tok(1536, MH * MQK)
        vm, qb, kb, vb = (tok(3072 + 1024 * n, 512) for n in range(4))
        cbuf = tok(7168, 416)
        pooledT = work[:, 2048:4096].rearrange("p (c s) -> p c s", c=KC)
        cT = aux[:, 3200:3968].rearrange("p (c s) -> p c s", c=3)
        turned_qk = {"moba": (sig[:, :, :].rearrange("p b (c s) -> p (b c) s", s=S),
                              pT[:, :, :, :].rearrange("p l c s -> p (l c) s")), "mla": (qT, kT)}
        ropes = aux[:, 2048:3072].rearrange("p (n t h c) -> p n t h c", n=4, t=NT, h=MH)
        probs = aux[:, 3200:4352].rearrange("p (b n) -> p b n", b=3)
        probsT = aux[:, 4352:5504].rearrange("p (b n) -> p b n", b=3)
        hid = aux[:, 0:1024].rearrange("p (t n) -> p t n", t=NT)
        inject_T = aux[:, 2048:3072]
        taps = aux[:, 3072:4096]
        inject = work[:, 0:1024].rearrange("p (g j i) -> p g j i", g=8, j=L)
        readout = work[:, 1024:2176].rearrange("p (g k o) -> p g k o", g=8, k=L + 1)
        t1, t2 = work[:, 2176:3328], work[:, 3328:4480]
        Bs, Bx, Cs, Cx = (work[:, 4480 + 1024 * n:5504 + 1024 * n].rearrange("p (i g) -> p i g", i=GI)
                          for n in range(4))
        rawB = h[0:G, :, :].rearrange("p t n -> p (t n)").rearrange("p (rc i) -> p rc i", i=GI)
        rawC = [aux[0:G, at:at + 1024].rearrange("p (o rc) -> p o rc", o=8) for at in (1024, 4096)]
        powT = work[:, 8576:9856].rearrange("p (q g) -> p q g", q=20)
        pads = work[:, 9856:10880]
        t3 = work[:, 10880:12032]
        lam = work[0:G, 10880:12288].rearrange("p (n c) -> p n c", c=GP)
        pw = work[0:G, 0:2560].rearrange("p (q r c) -> p q r c", q=20, r=2)
        powers = work[0:G, 3328:4352].rearrange("p (r k c) -> p r k c", r=2, k=L)
        prods = work[0:G, 4480:5504].rearrange("p (n k c) -> p n k c", n=4, k=4)
        xc = [v.rearrange("p (j n) -> p j n", j=L) for v in (work[0:NC, 8192:12288], aux[0:NC, 0:4096])]
        xg = work[0:NC, 0:8192].rearrange("p (g j i) -> p g j i", g=G, j=L)
        uT = aux[:, 0:2048].rearrange("p (c s) -> p c s", c=KC)
        ug = work[:, 8192:10240].rearrange("p (g c) -> p g c", g=G)
        states = work[:, 0:33 * 128].rearrange("p (r c g) -> p r c g", r=2, c=NC + 1)
        steps = work[:, 4224:4480].rearrange("p (n r g) -> p n r g", n=2, r=2)
        yc = work[:, 4480:6528].rearrange("p (f j n) -> p f j n", f=2, j=L)
        added = work[:, 4480:6528].rearrange("p (n s rc) -> p n s rc", n=4, s=4)
        ybuf = work[:, 10240:12288].rearrange("p (c s) -> p c s", c=KC)

        block = ctx.enter_context(nc.Block())

        @block.sync
        def _(sp):
            stores = {"inject": w_stored, "readout": v_stored, "taps": t_stored}
            first = blocks[0][1][0][1]
            sp.dma_start(ring[:, 0, 0:BLK // 2].rearrange("p (k n) -> p k n", k=KC // 2), first[:, 0:KC // 2])\
                .then_inc(first_landed, 16)
            sp.wait_ge(x_landed, 16)
            sp.dma_start(ring[:, 0, BLK // 2:BLK].rearrange("p (k n) -> p k n", k=KC // 2), first[:, KC // 2:KC])\
                .then_inc(block_landed[0], 16)
            for n, (name, parts, _) in enumerate(blocks):
                if n == 0:
                    continue
                if n == 2:
                    sp.dma_start(aux[:, 2048:2048 + NPOOL], w["pools"]).then_inc(pools_landed, 16)
                    for l in range(2):
                        sp.dma_start(p_tok[:, l], w["p"][l, 0].rearrange("(t p) n -> p t n", p=P)).then_inc(p_landed, 16)
                if n >= RING:
                    before, _, reader = blocks[n - RING]
                    if before in order:
                        sp.wait_ge(low_made, 2 * order[before] + 2)
                    else:
                        sp.wait_ge(pe_done, done(reader))
                if name[0] in stores:
                    sp.wait_ge(stores[name[0]], 16 * 4 * (name[1] + 1))
                for at, src in parts:
                    rows, cols = src.shape[0], src.shape[1] * (src.shape[2] if len(src.shape) > 2 else 1)
                    dst = ring[0:rows, slot[name], at:at + cols]
                    if len(src.shape) > 2:
                        dst = dst.rearrange("p (k n) -> p k n", k=src.shape[1])
                    sp.dma_start(dst, src).then_inc(block_landed[slot[name]], 16)
            for t in range(NT):
                sp.wait_ge(dve_emptied, u.emptied(("acc", 1, 2 * t + 1)))
                sp.dma_start(out.rearrange("b (t p) n -> p (b t) n", p=P)[:, t], x[:, t, :]).then_inc(out_stored, 16)
            sp.wait_ge(out_stored, 16 * NT)

        @block.tensor
        def _(pe):

            def begin(name):
                before = u.before[u.at[name]]
                if before is not None and u.by[before] == "a":
                    pe.wait_ge(act_emptied, u.count[before])
                elif before is not None:
                    pe.wait_ge(dve_emptied, u.count[before])
                return bank(name)

            def emptied(name):
                if u.by[u.at[name]] == "a":
                    pe.wait_ge(act_emptied, u.emptied(name))
                else:
                    pe.wait_ge(dve_emptied, u.emptied(name))

            def weights_here(name):
                pe.wait_ge(block_landed[slot[name]], landed[name])

            def turn(stage, src, units=range(4), width=P, chunks=8, ready=None):
                for k in units:
                    b = begin(("T", stage, k))
                    if ready:
                        ready(k)
                    for cc in range(2):
                        c = 2 * k + cc
                        if c < chunks:
                            for t in range(NT):
                                last = pe.transpose(b[0:width, cc * S + t * P:cc * S + t * P + P],
                                                    src[:, t, c * width:(c + 1) * width], ident)
                    last.then_inc(pe_done, 1)

            def three(bank_cols, parts, at, w_high, w_low, first, last):
                high, low = parts
                pe.matmul(bank_cols, high[:, at[0], at[1]], w_high, start=first, stop=False)
                pe.matmul(bank_cols, high[:, at[0], at[1]], w_low, start=False, stop=False)
                return pe.matmul(bank_cols, low[:, at[0], at[1]], w_high, start=False, stop=last)

            def part_views(g, k, width):
                _, _, at = half_of(g)
                return (v[at].rearrange("p (k n) -> p k n", n=width) for v in (whi, wlo))

            def product(stage, nb, name, width=512, turned_by=None, gelus=False):
                banks = [begin((stage, nb, t)) for t in range(NT)]
                for half in range(2):
                    g = 2 * order[name] + half
                    w_high, w_low = part_views(g, 4, width)
                    pe.wait_ge(low_made, g + 1)
                    for t in range(NT):
                        for kk in range(4):
                            k = 4 * half + kk
                            if turned_by and nb == 0 and t == 0 and k % 2 == 0:
                                emptied(("T", turned_by, k // 2))
                            if gelus and t == 0 and k % 2 == 0:
                                pe.wait_ge(gelu_ready, k // 2 + 1)
                            last = three(banks[t][:, 0:width], (hT_hi, hT_lo), (k, slice(t * P, t * P + P)),
                                         w_high[:, kk, :], w_low[:, kk, :], k == 0, k == KC - 1)
                        if half:
                            last.then_inc(pe_done, 1)
                    if half == 0:
                        last.then_inc(first_used, 1)

            def x_has(stage):
                return lambda k: emptied((stage, k // 2, 1))

            def x_gated(before):
                return lambda k: pe.wait_ge(x_updated, before + (2 if k < 2 else 4))

            pe.wait_ge(tables_landed, 16)
            pe.wait_ge(vecs_landed, 16)
            b = begin("vec")
            pe.transpose(b[:, 0:NVEC], vrows[:, :], ident[0:NVEC, 0:NVEC]).then_inc(pe_done, 1)
            pe.wait_ge(x_landed, 16)
            turn("a", x)
            for stage in ("u", "za"):
                for nb in range(2):
                    product(stage, nb, (stage, nb), turned_by="a" if stage == "u" else None)
            pe.wait_ge(pools_landed, 16)
            for g in range(4):
                b = begin(("pool", g))
                emptied(("u", g // 2, 1))
                for cc in range(2):
                    c = 2 * g + cc
                    pe.matmul(b[:, cc * S:(cc + 1) * S], u_tok[:, 0, c * P:(c + 1) * P], pools[:, g, 0:S],
                              start=(cc == 0), stop=False, skip_group_check=True)
                    last = pe.matmul(b[:, cc * S + P:(cc + 1) * S], u_tok[:, 1, c * P:(c + 1) * P],
                                     pools[:, g, S:S + P], start=False, stop=True, skip_group_check=True)
                last.then_inc(pe_done, 1)
            weights_here("w_group")
            wg = ring[:, slot["w_group"], 0:2048].rearrange("p (g k n) -> p g k n", g=4, k=2)
            for nb in range(2):
                for t in range(NT):
                    b = begin(("mixed", nb, t))
                    for g in (2 * nb, 2 * nb + 1):
                        emptied(("pool", g))
                        for k in range(2):
                            last = pe.matmul(b[:, (g % 2) * S:(g % 2) * S + S], pooledT[:, 2 * g + k, t * P:(t + 1) * P],
                                             wg[:, g, k, :], start=(k == 0), stop=(k == 1))
                    last.then_inc(pe_done, 1)
            pe.wait_ge(p_landed, 32)
            for l in range(2):
                b = begin(("pT", l))
                for cc in range(2):
                    for t in range(NT):
                        last = pe.transpose(b[:, cc * S + t * P:cc * S + t * P + P],
                                            p_tok[:, l, t, cc * P:(cc + 1) * P], ident)
                last.then_inc(pe_done, 1)
            turn("mixed", h, ready=lambda k: emptied(("mixed", k // 2, 1)))
            for nb in range(2):
                product("a_out", nb, ("a_out", nb), turned_by="mixed")

            def ple(l, before):
                name = f"ple{l}"
                turn(f"x{l}", x, units=(0, 1), ready=x_has(before))
                weights_here(name)
                wp = weights(name, 2, D)
                emptied(("pT", l))
                for nb in range(2):
                    for t in range(NT):
                        b = begin((name, nb, t))
                        for k in range(2):
                            last = pe.matmul(b[:, :], pT[:, l, k, t * P:(t + 1) * P],
                                             wp[:, k, nb * 512:(nb + 1) * 512], start=(k == 0), stop=(k == 1))
                        last.then_inc(pe_done, 1)
                turn(f"x{l}", x, units=(2, 3), ready=x_has(before))
                for nb in range(2):
                    product(f"gate{l}", nb, (f"gate{l}", nb), turned_by=f"x{l}")

            ple(0, "a_out")

            turn("kv", x, ready=x_gated(0))
            for stage in ("k", "v"):
                for nb in range(2):
                    product(stage, nb, (stage, nb), turned_by="kv" if stage == "k" else None)
            turn("qz", x)
            turn("k", k_tok, ready=lambda k: pe.wait_ge(heads_normed, 1))
            for nb in range(2):
                product("q", nb, ("q", nb), turned_by="qz")
            for nb in range(2):
                product("zb", nb, ("zb", nb))
            turn("q", q_tok, ready=lambda k: pe.wait_ge(heads_normed, 2))
            pe.wait_ge(masks_ready, 4)
            def stick_logits(i):
                b = begin(("logits", i))
                c, p0 = i // 2, HD * (i % 2)
                if i % 2 == 0:
                    emptied(("T", "q", c // 2))
                    emptied(("T", "k", c // 2))
                pe.matmul(b[:, 0:S], kT[p0:p0 + HD, c, 0:P], qT[p0:p0 + HD, c, :], start=True, stop=False,
                          skip_group_check=True)
                pe.matmul(b[:, S:S + P], kT[p0:p0 + HD, c, P:S], qT[p0:p0 + HD, c, P:S], start=False,
                          stop=False, skip_group_check=True)
                pe.matmul(b[:, 0:P], bf[:, 0, :], bf[:, 1, :], start=False, stop=False, skip_group_check=True)
                pe.matmul(b[:, S:S + P], bf[:, 0, :], bf[:, 1, :], start=False, stop=False,
                          skip_group_check=True).then_inc(pe_done, 1)

            def stick_logs(n):
                b = bank(("loga", n))
                pe.wait_ge(sp_ready, n + 1)
                pe.matmul(b[:, 0:S], tneg, sps[:, n % 4, 0:S], start=False, stop=False, skip_group_check=True)
                pe.matmul(b[:, P:S], allneg[:, :], sps[:, n % 4, S:S + P], start=False, stop=False,
                          skip_group_check=True)
                pe.matmul(b[:, S:S + P], tneg, sps[:, n % 4, S:S + P], start=False, stop=True,
                          skip_group_check=True).then_inc(pe_done, 1)

            def stick_values(n):
                b = begin(("stick_out", n // 4)) if n % 4 == 0 else bank(("stick_out", n // 4))
                o = b[:, (n % 4) * P:(n % 4) * P + P]
                emptied(("loga", n))
                a = sticks[:, n % 4, :]
                vh = v_tok[:, :, n * HD:(n + 1) * HD]
                pe.matmul(o[:, 0:HD], a[:, 0:P], vh[:, 0, :], start=True, stop=True)
                pe.matmul(o[:, HD:P], a[:, P:S], vh[:, 0, :], start=True, stop=False)
                last = pe.matmul(o[:, HD:P], a[:, S:S + P], vh[:, 1, :], start=False, stop=True)
                if n % 4 == 3:
                    last.then_inc(pe_done, 1)

            for j in range(NH // 2 + 2):
                for i in (2 * j, 2 * j + 1):
                    if i < NH:
                        stick_logits(i)
                for i in (2 * j - 2, 2 * j - 1):
                    if 0 <= i < NH:
                        stick_logs(i)
                for i in (2 * j - 4, 2 * j - 3):
                    if i >= 0:
                        stick_values(i)
            turn("o1", h, ready=lambda k: emptied(("stick_out", k)))
            for nb in range(2):
                product("b_out", nb, ("b_out", nb), turned_by="o1")
            ple(1, "b_out")

            turn("mix0", x, ready=x_gated(4))
            product("wc", 0, "wc", width=416, turned_by="mix0")
            product("wq", 0, "wq")
            product("wk", 0, "wk")
            turn("c", cbuf, units=range(2), chunks=3, ready=lambda k: emptied(("wc", 0, 1)))
            product("wv", 0, "wv")
            turn("qmoba", qb, units=range(2), ready=lambda k: pe.wait_ge(heads_normed, 3))
            turn("kmoba", kb, units=range(2), ready=lambda k: pe.wait_ge(heads_normed, 4))
            weights_here("lowrank")
            wuq = weights("lowrank", 2, 768)
            for nb in range(2):
                for t in range(NT):
                    b = begin(("uq", nb, t))
                    for k in range(2):
                        emptied(("T", "c", 0))
                        last = pe.matmul(b[:, 0:384], cT[:, k, t * P:(t + 1) * P], wuq[:, k, nb * 384:(nb + 1) * 384],
                                         start=(k == 0), stop=(k == 1))
                    last.then_inc(pe_done, 1)
            for nb in range(2):
                weights_here("lowrank")
                wkv = ring[:, slot["lowrank"], 1536 + 512 * nb:2048 + 512 * nb]
                for t in range(NT):
                    b = begin(("ukv", nb, t))
                    emptied(("T", "c", 1))
                    pe.matmul(b[:, :], cT[:, 2, t * P:(t + 1) * P], wkv, start=True, stop=True).then_inc(pe_done, 1)
            for kind in ("moba", "mla"):
                moba = kind == "moba"
                tq, tk = turned_qk[kind]
                v_all = vb if moba else vm
                if not moba:
                    turn("qmla", qm, width=MQK, ready=lambda k: pe.wait_ge(heads_normed, 5))
                    turn("kmla", km, width=MQK, ready=lambda k: pe.wait_ge(heads_normed, 6))
                for i in range(MH + 3):
                    if i < MH:
                        b = begin(("scores", kind, i))
                        c, rows = (i // 2, slice(HD * (i % 2), HD * (i % 2) + HD)) if moba else (i, slice(0, MQK))
                        emptied(("T", "q" + kind, c // 2))
                        emptied(("T", "k" + kind, c // 2))
                        pe.matmul(b[:, 0:P], tq[rows, c, 0:P], tk[rows, c, 0:P], start=True, stop=False,
                                  skip_group_check=True)
                        pe.matmul(b[:, P:P + S], tq[rows, c, P:S], tk[rows, c, :], start=False, stop=False,
                                  skip_group_check=True)
                        pe.matmul(b[:, 0:P], bf[:, 0, :], bf[:, 2, :], start=False, stop=False,
                                  skip_group_check=True)
                        pe.matmul(b[:, S:S + P], bf[:, 0, :], bf[:, 2, :], start=False, stop=True,
                                  skip_group_check=True).then_inc(pe_done, 1)
                    if 2 <= i < MH + 2:
                        n = i - 2
                        b = begin(("probsT", kind, n))
                        emptied(("scores", kind, n))
                        for k in range(3):
                            last = pe.transpose(b[:, k * P:(k + 1) * P], probs[:, n % 3, k * P:(k + 1) * P], ident)
                        last.then_inc(pe_done, 1)
                    if i >= 3:
                        n = i - 3
                        name = ("soft_out", kind, n // 4)
                        b = begin(name) if n % 4 == 0 else bank(name)
                        o = b[:, (n % 4) * P:(n % 4) * P + P]
                        emptied(("probsT", kind, n))
                        a = probsT[:, n % 3, :]
                        vh = v_all[:, :, n * HD:(n + 1) * HD]
                        pe.matmul(o[:, 0:HD], a[:, 0:P], vh[:, 0, :], start=True, stop=True)
                        pe.matmul(o[:, HD:P], a[:, P:S], vh[:, 0, :], start=True, stop=False)
                        last = pe.matmul(o[:, HD:P], a[:, S:S + P], vh[:, 1, :], start=False, stop=True)
                        if n % 4 == 3:
                            last.then_inc(pe_done, 1)
            turn("o2", h, ready=lambda k: emptied(("soft_out", "mla" if k < 2 else "moba", k % 2)))
            for nb in range(2):
                product("w_o", nb, ("w_o", nb), turned_by="o2")

            def mlp(layer, ready):
                turn(("ffn", layer), x, ready=ready)
                acc = [ps[k] for k in range(4)]
                for i in range(FB + 1):
                    n = i - 1
                    if i:
                        for k in range(2):
                            b = begin(("fT", layer, n, k))
                            emptied((("f1", layer, n), 0, 1))
                            for cc in range(2):
                                for t in range(NT):
                                    c = 2 * k + cc
                                    last = pe.transpose(b[:, cc * S + t * P:cc * S + t * P + P],
                                                        hid[:, t, c * P:(c + 1) * P], ident)
                            last.then_inc(pe_done, 1)
                    if i < FB:
                        product(("f1", layer, i), 0, ("f1", layer, i), turned_by=("ffn", layer) if i == 0 else None)
                    if layer == 0 and i == 2:
                        s5_coefficients()
                    if layer == 0:
                        for f in chunks_before(i):
                            s5_chunk(f)
                    if i:
                        for half in range(2):
                            g = 2 * order[("f2", layer, n)] + half
                            w_high, w_low = part_views(g, 2, D)
                            pe.wait_ge(low_made, g + 1)
                            emptied(("fT", layer, n, half))
                            for t in range(NT):
                                for nb in range(2):
                                    if n == 0 and half == 0:
                                        begin(("acc", layer, 2 * t + nb))
                                    for kk in range(2):
                                        cols = slice(nb * 512, nb * 512 + 512)
                                        last = three(acc[2 * t + nb][:, :], (hidT_hi, hidT_lo),
                                                     (2 * half + kk, slice(t * P, t * P + P)), w_high[:, kk, cols],
                                                     w_low[:, kk, cols], n == 0 and half == 0 and kk == 0,
                                                     n == FB - 1 and half == 1 and kk == 1)
                                    if n == FB - 1 and half == 1:
                                        last.then_inc(pe_done, 1)
                            if half == 0:
                                last.then_inc(first_used, 1)
                            elif n < FB - 1:
                                last.then_inc(f2_done, 1)
                    if layer == 0:
                        for f in chunks_after(i):
                            s5_chunk(f)
            def s5_coefficients():
                pe.wait_ge(powers_ready, 1)
                for k in range(3):
                    b = begin(("powT", k))
                    for q in range(8 * k, min(8 * k + 8, 20)):
                        last = pe.transpose(b[:, (q % 8) * G:(q % 8) * G + G],
                                            pw[:, q, :, :].rearrange("p r c -> p (r c)"), ident[0:G, 0:G])
                    last.then_inc(pe_done, 1)
                pe.wait_ge(bc_landed, 16 * 6)
                for k in range(4):
                    b = begin(("bcT", k))
                    for i in range(8):
                        v = rawB[:, :, 8 * k + i] if k < 2 else rawC[k - 2][:, i, :]
                        last = pe.transpose(b[:, i * G:(i + 1) * G], v, ident[0:G, 0:G])
                    last.then_inc(pe_done, 1)
                for k in range(4):
                    b = begin(("bcX", k))
                    emptied(("bcT", k))
                    src = (Bs, Cs)[k // 2][:, 8 * (k % 2):8 * (k % 2) + 8, :].rearrange("p i g -> p (i g)")
                    pe.matmul(b[:, :], const("swap"), src, start=True, stop=True).then_inc(pe_done, 1)

            def s5_chunk(f):
                pe.wait_ge(injects_made, f + 1)
                for k in range(2):
                    b = begin(("wT", f, k))
                    for g in range(4):
                        last = pe.transpose(b[:, g * P:(g + 1) * P],
                                            inject[:, 4 * k + g, :, :].rearrange("p j i -> p (j i)"), ident)
                    last.then_inc(pe_done, 1)
                pe.wait_ge(pads_filled, f + 1)
                pe.wait_ge(readouts_made, f + 1)
                b = begin(("taps", f))
                for g in range(8):
                    last = pe.matmul(b[:, 0:P], pads[:, g * P:(g + 1) * P],
                                     readout[:, g, 0:L, :].rearrange("p k o -> p (k o)"),
                                     start=(g == 0), stop=(g == 7))
                last.then_inc(pe_done, 1)

            mlp(0, x_has("w_o"))

            b = begin("gain_gi")
            pe.wait_ge(gain_rows_ready, 1)
            pe.transpose(b[:, 0:G], gain_rows[:, 1, :], ident[0:G, 0:G]).then_inc(pe_done, 1)
            for n in range(4):
                pe.wait_ge(regrouped_a if n < 2 else regrouped_b, n % 2 + 1)
                b = begin(("ug", n))
                for g in range(16):
                    f = 16 * n + g
                    last = pe.transpose(b[:, g * NC:(g + 1) * NC], xg[:, f].rearrange("p j i -> p (j i)"),
                                        ident[0:NC, 0:NC])
                last.then_inc(pe_done, 1)
            def states_turned(n):
                b = begin(("inject", n))
                emptied(("added", n))
                for k in range(4):
                    last = pe.transpose(b[:, k * P:(k + 1) * P], added[:, n, k, :], ident)
                last.then_inc(pe_done, 1)
                b = begin(("injectx", n))
                for k in range(4):
                    for half in range(2):
                        last = pe.matmul(b[GP * half:GP * half + GP, k * P:(k + 1) * P],
                                         added[:, n, k, GP * (1 - half):GP * (1 - half) + GP], ident,
                                         start=True, stop=True)
                last.then_inc(pe_done, 1)

            for n in range(4):
                b = begin(("added", n))
                emptied(("ug", n))
                weights_here(("inject", n // 2))
                wi = weights(("inject", n // 2), 32, P)
                for g in range(16):
                    f = 16 * n + g
                    q = g % 4
                    last = pe.matmul(b[32 * q:32 * q + 32, (g // 4) * P:(g // 4) * P + P], ug[:, f, :], wi[:, f % 32, :],
                                     start=True, stop=True)
                last.then_inc(pe_done, 1)
                if n:
                    states_turned(n - 1)
            states_turned(3)
            turn("mix1", h)
            for n in range(4):
                b = begin(("fir", n))
                emptied(("T", "mix1", n))
                weights_here(("taps", n // 2))
                wt = weights(("taps", n // 2), 32, P)
                for fl in range(2):
                    f = 2 * n + fl
                    src = uT[:, f, :].rearrange("p (c j) -> p c j", j=L)
                    dst = b[:, fl * S:(fl + 1) * S].rearrange("p (c j) -> p c j", j=L)
                    for k in range(L):
                        last = pe.matmul(dst[:, :, k:L], wt[:, (f % 4) * 8 + k, :], src[:, :, 0:L - k],
                                         start=(k == 0), stop=(k == L - 1), skip_group_check=True)
                last.then_inc(pe_done, 1)
            pe.wait_ge(states_ready, 1)
            for n in range(4):
                b = begin(("state_out", n))
                half, part = n // 2, n % 2
                weights_here(("readout", half))
                wr = weights(("readout", half), 32, P)
                for q in range(4):
                    for g in range(4):
                        f = 8 * q + 4 * part + g
                        last = pe.matmul(b[32 * q:32 * q + 32, g * P:(g + 1) * P], states[:, 0, 0:NC, 32 * half + f],
                                         wr[:, f, :], start=True, stop=True)
                last.then_inc(pe_done, 1)
            for n in range(4):
                b = begin(("state_outT", n))
                emptied(("state_out", 2 * (n // 2) + 1))
                for jj in range(4):
                    last = pe.transpose(b[:, jj * P:(jj + 1) * P], yc[:, n // 2, 4 * (n % 2) + jj, :], ident)
                last.then_inc(pe_done, 1)
            for hh in range(2):
                for name in ("val", "gate"):
                    product((name, hh), 0, (name, hh), gelus=(name, hh) == ("val", 0))
            mlp(1, x_gated(8))

        @block.scalar
        def _(act):
            steps_done = [0]

            def link(ins):
                steps_done[0] += 1
                ins.then_inc(act_step, 1)
                act.wait_ge(act_step, steps_done[0])

            def filled(name):
                act.wait_ge(pe_done, done(name))
                return bank(name)

            def copy_out(name, dst, src=None, scale=1.0, func=ACT.Copy):
                b = filled(name)
                act.activation(dst, b[:, :] if src is None else src, func, scale=scale).then_inc(act_emptied, 1)

            def turned_out(stage, pairs, units=(1, 3), width=P):
                for k in units:
                    b = filled(("T", stage, k))
                    for n, (dst, name, one) in enumerate(pairs):
                        if name is None:
                            ins = act.activation(dst[0:width, 2 * k:2 * k + 2, :].rearrange("p c s -> p (c s)"),
                                                 b[0:width, :], ACT.Copy)
                            continue
                        for cc in range(2):
                            c = 2 * k + cc
                            ins = act.activation(dst[0:width, c, :], b[0:width, cc * S:cc * S + S], ACT.Copy,
                                                 scale=gain(name, 0 if one else c, width))
                    ins.then_inc(act_emptied, 1)

            def turned_high(stage, name, units=range(4)):
                for k in units:
                    b = filled(("T", stage, k))
                    if name is None:
                        ins = act.activation(hT_hi[:, 2 * k:2 * k + 2, :].rearrange("p c s -> p (c s)"), b[:, :], ACT.Copy)
                    else:
                        for cc in range(2):
                            ins = act.activation(hT_hi[:, 2 * k + cc, :], b[:, cc * S:cc * S + S], ACT.Copy,
                                                 scale=gain(name, 2 * k + cc))
                    ins.then_inc(high_turned, 1)

            def fill(g):
                name, cols, at = half_of(g)
                if g:
                    act.wait_ge(block_landed[slot[name]], landed[name])
                else:
                    act.wait_ge(first_landed, 16)
                if g >= PARTS:
                    before, second = split_names[(g - PARTS) // 2], (g - PARTS) % 2
                    if not second:
                        act.wait_ge(first_used, order[before] + 1)
                    elif reader_of[before][0] == "f2":
                        act.wait_ge(f2_done, reader_of[before][1] + 1)
                    else:
                        act.wait_ge(pe_done, done(reader_of[before]))
                act.activation(whi[at], ring[:, slot[name], cols], ACT.Copy).then_inc(high_made, 1)

            def refill(name, half):
                g = 2 * order[name] + half + PARTS
                if g < 2 * len(split_names):
                    fill(g)

            def squares_of_x(m):
                for t in range(NT):
                    act.wait_ge(ssq_ready, 2 * m + t)
                    act.activation(h[:, t, :], x[:, t, :], ACT.Square, accum_out=ssq[:, m, t:t + 1]).then_inc(ssq_ready, 1)

            def root(m):
                act.wait_ge(rstd_ready, m + 1)

            def tokens_out(stage, nb, dst, m=None, func=ACT.Copy, width=512):
                for t in range(NT):
                    copy_out((stage, nb, t), dst[:, t, nb * width:(nb + 1) * width], bank((stage, nb, t))[:, 0:width],
                             1.0 if m is None else rstd[:, m, t:t + 1], func)

            act.dma_start(x[:, :, :], w["x"].rearrange("b (t p) n -> p (b t) n", p=P)).then_inc(x_landed, 16)
            act.dma_start(cst[:, :], w["tables"]).then_inc(tables_landed, 16)
            act.dma_start(vrows[:, :], w["vecs"]).then_inc(vecs_landed, 16)
            act.wait_ge(x_landed, 16)
            squares_of_x(0)
            act.wait_ge(gains_ready, 3)
            fill(0)
            turned_high("a", "a_norm")
            for g in range(1, PARTS):
                fill(g)
            root(0)
            for nb in range(2):
                refill(("u", nb), 0)
                tokens_out("u", nb, u_tok, 0)
                refill(("u", nb), 1)
            for nb in range(2):
                refill(("za", nb), 0)
                tokens_out("za", nb, z_tok, 0, ACT.Silu)
                if nb == 0:
                    refill(("za", 0), 1)
            for g in range(4):
                copy_out(("pool", g), pooledT[:, 2 * g:2 * g + 2, :].rearrange("p c s -> p (c s)"))
            for l in range(2):
                copy_out(("pT", l), pT[:, l, :, :].rearrange("p c s -> p (c s)"))
            turned_high("mixed", "a_scale")
            refill(("za", 1), 1)
            refill(("a_out", 0), 0)
            refill(("a_out", 0), 1)
            turned_high("x0", None, (0, 1))
            refill(("a_out", 1), 0)
            for nb in range(2):
                tokens_out("ple0", nb, pl_tok)
            turned_high("x0", None, (2, 3))
            refill(("a_out", 1), 1)

            sigs = [0]

            def gate(name):
                b = filled(name)
                n = sigs[0]
                sigs[0] += 1
                if n >= 2:
                    act.wait_ge(x_updated, n - 1)
                act.activation(sig[:, n % 2, :], b[:, :], ACT.Sigmoid).then_inc(act_emptied, 1)

            for nb in range(2):
                refill(("gate0", nb), 0)
                for t in range(NT):
                    gate(("gate0", nb, t))
                if nb == 0:
                    refill(("gate0", 0), 1)
            turned_high("kv", "kv_norm")
            refill(("gate0", 1), 1)
            act.wait_ge(x_updated, 4)
            squares_of_x(1)
            root(1)
            for nb in range(2):
                refill(("k", nb), 0)
                tokens_out("k", nb, k_tok, 1)
                refill(("k", nb), 1)
            for nb in range(2):
                refill(("v", nb), 0)
                if nb:
                    turned_high("qz", "b_norm")
                tokens_out("v", nb, v_tok, 1)
                if nb == 0:
                    refill(("v", 0), 1)
            refill(("v", 1), 1)
            turned_out("k", [(kT, "k_norm", True)])
            for nb in range(2):
                refill(("q", nb), 0)
                tokens_out("q", nb, q_tok, 1)
                refill(("q", nb), 1)
            for nb in range(2):
                refill(("zb", nb), 0)
                tokens_out("zb", nb, z_tok, 1, ACT.Silu)
                if nb == 0:
                    refill(("zb", 0), 1)
            turned_out("q", [(qT, "q_norm", True)])
            for j in range(NH // 2 + 1):
                for i in (2 * j, 2 * j + 1):
                    if i < NH:
                        b = filled(("logits", i))
                        if i >= 4:
                            act.wait_ge(sp_ready, i - 3)
                        link(act.activation(logs[:, i % 4, :], b[:, 0:384], ACT.Abs))
                        act.activation(logs[:, i % 4, :], logs[:, i % 4, :], ACT.Exp, scale=-1.0).then_inc(exps_ready, 1)
                for i in (2 * j - 2, 2 * j - 1):
                    if i >= 0:
                        b = filled(("loga", i))
                        act.activation(sticks[:, i % 4, :], b[:, 0:384], ACT.Exp).then_inc(act_emptied, 1)
                for i in (2 * j, 2 * j + 1):
                    if i < NH:
                        act.wait_ge(exps_ready, i + 1)
                        act.activation(logs[:, i % 4, :], logs[:, i % 4, :], ACT.Ln, bias=1.0).then_inc(logs_ready, 1)
            turned_high("o1", None)
            refill(("zb", 1), 1)
            refill(("b_out", 0), 0)
            refill(("b_out", 0), 1)
            turned_high("x1", None, (0, 1))
            refill(("b_out", 1), 0)
            for nb in range(2):
                tokens_out("ple1", nb, pl_tok)
            turned_high("x1", None, (2, 3))
            refill(("b_out", 1), 1)
            for nb in range(2):
                refill(("gate1", nb), 0)
                for t in range(NT):
                    gate(("gate1", nb, t))
                if nb == 0:
                    refill(("gate1", 0), 1)
            turned_high("mix0", "mix0")
            refill(("gate1", 1), 1)
            act.wait_ge(x_updated, 8)
            squares_of_x(2)
            root(2)
            refill("wc", 0)
            tokens_out("wc", 0, cbuf, 2, width=416)
            refill("wc", 1)
            for name, dst in (("wq", qb), ("wk", kb), ("wv", vb)):
                refill(name, 0)
                tokens_out(name, 0, dst, 2)
                if name != "wv":
                    refill(name, 1)
            tq, tk = turned_qk["moba"]
            turned_out("qmoba", [(tq, "qn_moba", True)], units=(1,))
            turned_out("kmoba", [(tk, "kn_moba", True)], units=(1,))
            act.wait_ge(lowr_ready, 1)
            for nb in range(2):
                for t in range(NT):
                    copy_out(("uq", nb, t), qm[:, t, nb * 384:(nb + 1) * 384], bank(("uq", nb, t))[:, 0:384],
                             lowr[:, t:t + 1])
            for nb in range(2):
                for t in range(NT):
                    b = filled(("ukv", nb, t))
                    v = b[:, :].rearrange("p (h n) -> p h n", h=4)
                    kv = km[:, t, :].rearrange("p (h n) -> p h n", h=MH)
                    act.activation(kv[:, 4 * nb:4 * nb + 4, 0:MNOPE], v[:, :, 0:MNOPE], ACT.Copy, scale=lowr[:, 2 + t:3 + t])
                    act.activation(vm[:, t, 256 * nb:256 * nb + 256].rearrange("p (h n) -> p h n", h=4), v[:, :, MNOPE:P],
                                   ACT.Copy, scale=lowr[:, 2 + t:3 + t]).then_inc(act_emptied, 1)
            for n, kind in enumerate(("moba", "mla")):
                moba = kind == "moba"
                tq, tk = turned_qk[kind]
                if not moba:
                    turned_out("qmla", [(tq, "qn_mla", True)], width=MQK)
                    turned_out("kmla", [(tk, "kn_mla", True)], width=MQK)
                for i in range(MH):
                    b = filled(("scores", kind, i))
                    act.wait_ge(max_ready, MH * n + i + 1)
                    if i >= 3:
                        act.wait_ge(pe_done, done(("probsT", kind, i - 3)))
                    act.activation(probs[:, i % 3, 0:P], b[:, 0:P], ACT.Exp, bias=nmax[:, n, i, 0:1],
                                   accum_out=den[:, n, i, 0:1])
                    act.activation(probs[:, i % 3, P:384], b[:, P:384], ACT.Exp, bias=nmax[:, n, i, 1:2],
                                   accum_out=den[:, n, i, 1:2]).then_inc(act_emptied, 1)
            turned_high("o2", None)
            refill("wv", 1)
            refill(("w_o", 0), 0)
            refill(("w_o", 0), 1)
            refill(("w_o", 1), 0)

            def mlp(layer, m):
                turned_high(("ffn", layer), f"ffn{layer}")
                refill(("gate", 1) if layer else ("w_o", 1), 1)
                squares_of_x(m)
                for i in range(FB + 1):
                    if i:
                        for k in range(2):
                            b = filled(("fT", layer, i - 1, k))
                            act.activation(hidT_hi[:, 2 * k:2 * k + 2, :].rearrange("p c s -> p (c s)"), b[:, :],
                                           ACT.Copy).then_inc(high_turned, 1)
                    if i < FB:
                        refill(("f1", layer, i), 0)
                        for t in range(NT):
                            b = filled((("f1", layer, i), 0, t))
                            act.activation(hid[:, t, :], b[:, :], ACT.Relu).then_inc(relu_ready, 1)
                    if layer == 0 and i == 2:
                        for k in range(3):
                            q = min(8, 20 - 8 * k)
                            copy_out(("powT", k), powT[:, 8 * k:8 * k + q, :].rearrange("p q g -> p (q g)"),
                                     bank(("powT", k))[:, 0:q * G])
                    if i < FB:
                        refill(("f1", layer, i), 1)
                    if layer == 0 and i == 0:
                        act.wait_ge(lam_landed, 48)
                        act.activation(log_dt[:, 1:2], log_dt[:, 0:1], ACT.Exp).then_inc(dt_ready, 1)
                        act.wait_ge(zr_ready, 1)
                        act.activation(lam[:, 5, :], lam[:, 3, :], ACT.Exp).then_inc(exp_ready, 1)
                        act.wait_ge(angle_ready, 1)
                        act.activation(lam[:, 8:10, :], lam[:, 6:8, :], ACT.Sin).then_inc(sin_ready, 1)
                    if layer == 0:
                        for f in chunks_before(i):
                            injects_out(f)
                    if i and (layer or i < FB):
                        refill(("f2", layer, i - 1), 0)
                    if i and (layer or i < FB - 1):
                        refill(("f2", layer, i - 1), 1)
                    if layer == 0:
                        for f in chunks_after(i):
                            injects_out(f)

            def injects_out(f):
                if f:
                    act.wait_ge(w_stored, 16 * f)
                for k in range(2):
                    copy_out(("wT", f, k), inject_T[:, 512 * k:512 * k + 512])

            mlp(0, 3)
            act.wait_ge(dve_emptied, u.emptied(("acc", 0, 3)))
            squares_of_x(4)
            act.wait_ge(h_normed, 2)
            act.wait_ge(pe_done, done(("taps", FB - 1)))
            act.wait_ge(v_stored, 16 * 8)
            for half in range(2):
                if half:
                    act.wait_ge(w_stored, 16 * 8)
                    act.wait_ge(t_stored, 16 * 8)
                for t in range(NT):
                    act.dma_start(xc[half][16 * t:16 * t + 16, :, :],
                                  h[:, t, 512 * half:512 * half + 512]).then_inc(chunked[half], 16)
            act.wait_ge(chunked[1], 32)
            for n in range(2):
                act.activation(xg[:, 32 + 16 * n:48 + 16 * n].rearrange("p g j i -> p j g i"),
                               xc[1].rearrange("p j (g i) -> p j g i", i=GI)[:, :, 16 * n:16 * n + 16], ACT.Copy)\
                    .then_inc(regrouped_b, 1)
            for n in range(5):
                if n < 4:
                    copy_out(("added", n), added[:, n, :, :].rearrange("p s rc -> p (s rc)"))
                if n:
                    for half, name in enumerate(("inject", "injectx")):
                        b = filled((name, n - 1))
                        act.activation(states[:, half, 1:NC + 1, 16 * n - 16:16 * n],
                                       b[:, :].rearrange("p (g c) -> p c g", g=16), ACT.Copy).then_inc(act_emptied, 1)
            act.wait_ge(w_stored, 16 * 8)
            act.wait_ge(t_stored, 16 * 8)
            turned_out("mix1", [(uT, "mix1", False)], units=range(4))
            refill(("f2", 0, FB - 2), 1)
            refill(("f2", 0, FB - 1), 0)
            for n in range(4):
                b = filled(("state_out", n))
                dst = yc[:, n // 2, :, 64 * (n % 2):64 * (n % 2) + 64].rearrange("p j (g o) -> p j g o", g=4)
                act.activation(dst, b[:, :].rearrange("p (g j o) -> p j g o", g=4, j=L), ACT.Copy).then_inc(act_emptied, 1)
            for n in range(4):
                act.wait_ge(dve_emptied, u.emptied(("state_outT", 2 * (n // 2) + 1)))
                yv = ybuf[:, 2 * n:2 * n + 2, :]
                link(act.activation(yv, yv, ACT.Gelu_apprx_tanh))
                act.activation(hT_hi[:, 2 * n:2 * n + 2, :], yv, ACT.Copy).then_inc(gelu_high, 1)
            refill(("f2", 0, FB - 1), 1)
            for hh in range(2):
                refill(("val", hh), 0)
                refill(("val", hh), 1)
                refill(("gate", hh), 0)
                for t in range(NT):
                    gate((("gate", hh), 0, t))
                if hh == 0:
                    refill(("gate", 0), 1)
            mlp(1, 5)

        @block.vector
        def _(dve):
            steps_done = [0]

            def link(ins):
                steps_done[0] += 1
                ins.then_inc(dve_step, 1)
                dve.wait_ge(dve_step, steps_done[0])

            def filled(name):
                dve.wait_ge(pe_done, done(name))
                return bank(name)

            def emptied(name):
                dve.wait_ge(act_emptied, u.emptied(name))

            def turned_out(stage, pairs, units=(0, 2), width=P, chunks=8):
                for k in units:
                    b = filled(("T", stage, k))
                    for n, (dst, name, one) in enumerate(pairs):
                        if name is None:
                            ins = dve.tensor_copy(dst[0:width, 2 * k:2 * k + 2, :].rearrange("p c s -> p (c s)"),
                                                  b[0:width, :])
                            continue
                        for cc in range(min(2, chunks - 2 * k)):
                            c = 2 * k + cc
                            ins = dve.tensor_scalar(dst[0:width, c, :], b[0:width, cc * S:cc * S + S],
                                                    gain(name, 0 if one else c, width), None, ALU.mult)
                    ins.then_inc(dve_emptied, 1)

            def turned_low(stage, name, units=range(4)):
                for k in units:
                    b = bank(("T", stage, k))
                    dve.wait_ge(high_turned, u.high[("T", stage, k)])
                    for cc in range(2):
                        c = 2 * k + cc
                        ins = dve.scalar_tensor_tensor(out=hT_lo[:, c, :], in0=b[:, cc * S:cc * S + S],
                                                       scalar=1.0 if name is None else gain(name, c), in1=hT_hi[:, c, :],
                                                       op0=ALU.mult, op1=ALU.subtract)
                    ins.then_inc(dve_emptied, 1)

            def fill(g):
                name, cols, at = half_of(g)
                dve.wait_ge(high_made, g + 1)
                dve.tensor_tensor(wlo[at], ring[:, slot[name], cols], whi[at], ALU.subtract).then_inc(low_made, 1)

            def refill(name, half):
                g = 2 * order[name] + half + PARTS
                if g < 2 * len(split_names):
                    fill(g)

            def refills(*names):
                for name in names:
                    refill(name, 0)
                    refill(name, 1)

            def means(m):
                dve.wait_ge(ssq_ready, 2 * m + 2)
                dve.tensor_scalar(ms[:, m, :], ssq[:, m, :], 1.0 / D, EPS, ALU.mult, ALU.add).then_inc(ms_ready, 1)

            def add_to_x(stage, nb_at, nb, t):
                b = filled((stage, nb, t))
                xs = x[:, t, nb_at * 512:(nb_at + 1) * 512]
                dve.tensor_tensor(xs, xs, b[:, :], ALU.add).then_inc(dve_emptied, 1)

            dve.memset(allneg[:, :], -1.0).then_inc(masks_ready, 1)
            dve.wait_ge(tables_landed, 16)
            dve.tensor_copy(bf[:, 0, :], ident).then_inc(masks_ready, 1)
            dve.tensor_copy(bf[:, 1, :], const("mask_st")).then_inc(masks_ready, 1)
            dve.tensor_copy(bf[:, 2, :], const("mask_ts")).then_inc(masks_ready, 1)
            b = filled("vec")
            dve.tensor_copy(vcols[:, :], b[:, 0:NVEC]).then_inc(dve_emptied, 1)
            dve.wait_ge(dve_emptied, 1)
            for name, scale in (("q_norm", HD ** -0.5), ("qn_moba", HD ** -0.5), ("qn_mla", MQK ** -0.5)):
                dve.tensor_scalar(gain(name), gain(name), scale, None, ALU.mult).then_inc(gains_ready, 1)
            dve.wait_ge(gains_ready, 3)
            means(0)
            fill(0)
            turned_low("a", "a_norm")
            for g in range(1, PARTS):
                fill(g)
            refills(("u", 0), ("u", 1), ("za", 0))
            refill(("za", 1), 0)
            for nb in range(2):
                for t in range(NT):
                    b = filled(("mixed", nb, t))
                    emptied(("za", nb, t))
                    dve.tensor_tensor(h[:, t, nb * 512:(nb + 1) * 512], b[:, :], z_tok[:, t, nb * 512:(nb + 1) * 512],
                                      ALU.mult).then_inc(dve_emptied, 1)
            turned_low("mixed", "a_scale")
            refill(("za", 1), 1)
            refill(("a_out", 0), 0)
            for nb in range(2):
                for t in range(NT):
                    add_to_x("a_out", nb, nb, t)
                if nb == 0:
                    refill(("a_out", 0), 1)

            gates = [0]

            def gate_in(name, t, nb, other, free):
                n = gates[0]
                gates[0] += 1
                emptied(name)
                s = sig[:, n % 2, :]
                ins = dve.tensor_tensor(s, s, other, ALU.mult)
                if free:
                    ins.then_inc(dve_emptied, 1)
                    dve.wait_ge(dve_emptied, u.emptied(free))
                else:
                    link(ins)
                xs = x[:, t, nb * 512:(nb + 1) * 512]
                dve.tensor_tensor(xs, xs, s, ALU.add).then_inc(x_updated, 1)

            turned_low("x0", None, (0, 1))
            refill(("a_out", 1), 0)
            turned_low("x0", None, (2, 3))
            refill(("a_out", 1), 1)
            for nb in range(2):
                refill(("gate0", nb), 0)
                for t in range(NT):
                    gate_in(("gate0", nb, t), t, nb, pl_tok[:, t, nb * 512:(nb + 1) * 512], None)
                if nb == 0:
                    refill(("gate0", 0), 1)
            turned_low("kv", "kv_norm")
            refill(("gate0", 1), 1)
            means(1)

            def head_squares(buf, n, width):
                sq = squares[:, 0:n * width].rearrange("p (n c) -> p n c", n=n)
                link(dve.tensor_tensor(sq, buf, buf, ALU.mult))

            def head_means(n, width):
                headnorms[0] += 1
                sq = squares[:, 0:n * width].rearrange("p (n c) -> p n c", n=n)
                link(dve.tensor_reduce(ssh[:, 0:n], sq, AX_X, ALU.add))
                dve.tensor_scalar(msh[:, 0:n], ssh[:, 0:n], 1.0 / width, EPS, ALU.mult, ALU.add).then_inc(headms_ready, 1)

            def head_scale(buf, n, width):
                dve.wait_ge(headr_ready, headnorms[0])
                dve.tensor_tensor(buf, buf, rsh[:, 0:n].unsqueeze(2).broadcast_to([P, n, width]), ALU.mult)\
                    .then_inc(heads_normed, 1)

            def norm_heads(buf, n, width):
                head_squares(buf, n, width)
                head_means(n, width)
                head_scale(buf, n, width)

            headnorms = [0]
            refills(("k", 0), ("k", 1))
            refill(("v", 0), 0)
            emptied(("k", 1, 1))
            norm_heads(work[:, 2048:4096].rearrange("p (n c) -> p n c", c=HD), NT * NH, HD)
            refill(("v", 0), 1)
            refill(("v", 1), 0)
            turned_low("qz", "b_norm")
            turned_out("k", [(kT, "k_norm", True)])
            refill(("v", 1), 1)
            refills(("q", 0), ("q", 1))
            refill(("zb", 0), 0)
            emptied(("q", 1, 1))
            norm_heads(work[:, 0:2048].rearrange("p (n c) -> p n c", c=HD), NT * NH, HD)
            refill(("zb", 0), 1)
            refill(("zb", 1), 0)
            turned_out("q", [(qT, "q_norm", True)])
            emptied(("zb", 1, 1))
            for j in range(NH // 2 + 2):
                for i in (2 * j, 2 * j + 1):
                    if i < NH:
                        b = bank(("logits", i))
                        dve.wait_ge(logs_ready, i + 1)
                        dve.scalar_tensor_tensor(out=sps[:, i % 4, :], in0=b[:, 0:384], scalar=0.0, in1=logs[:, i % 4, :],
                                                 op0=ALU.max, op1=ALU.add).then_inc(sp_ready, 1)
                if j >= 3 and j % 2 == 1:
                    k = (j - 3) // 2
                    b = filled(("stick_out", k))
                    hv, zv = (a[:, :, 256 * k:256 * k + 256].rearrange("p t (n d) -> p n t d", d=HD) for a in (h, z_tok))
                    dve.tensor_tensor(hv, b[:, :].rearrange("p (n t d) -> p n t d", n=4, t=NT), zv, ALU.mult)\
                        .then_inc(dve_emptied, 1)
            turned_low("o1", None)
            refill(("zb", 1), 1)
            refill(("b_out", 0), 0)
            for nb in range(2):
                for t in range(NT):
                    add_to_x("b_out", nb, nb, t)
                if nb == 0:
                    refill(("b_out", 0), 1)
            turned_low("x1", None, (0, 1))
            refill(("b_out", 1), 0)
            turned_low("x1", None, (2, 3))
            refill(("b_out", 1), 1)
            for nb in range(2):
                refill(("gate1", nb), 0)
                for t in range(NT):
                    gate_in(("gate1", nb, t), t, nb, pl_tok[:, t, nb * 512:(nb + 1) * 512], None)
                if nb == 0:
                    refill(("gate1", 0), 1)

            turned_low("mix0", "mix0")
            refill(("gate1", 1), 1)
            means(2)
            refills("wc")
            emptied(("wc", 0, 1))
            sq = squares[:, 0:768].rearrange("p (t n) -> p t n", t=NT)
            link(dve.tensor_tensor(sq, cbuf[:, :, 0:384], cbuf[:, :, 0:384], ALU.mult))
            link(dve.tensor_reduce(lowss[:, 0:2], sq[:, :, 0:256], AX_X, ALU.add))
            link(dve.tensor_reduce(lowss[:, 2:4], sq[:, :, 256:384], AX_X, ALU.add))
            dve.tensor_scalar(lowms[:, 0:2], lowss[:, 0:2], 1.0 / 256, EPS, ALU.mult, ALU.add).then_inc(lowms_ready, 1)
            dve.tensor_scalar(lowms[:, 2:4], lowss[:, 2:4], 1.0 / 128, EPS, ALU.mult, ALU.add).then_inc(lowms_ready, 1)
            refill("wq", 0)
            emptied(("wq", 0, 1))
            norm_heads(work[:, 4096:5120].rearrange("p (n c) -> p n c", c=HD), NT * MH, HD)
            refill("wq", 1)
            refill("wk", 0)
            turned_out("c", [(cT, "g_cq", False)], units=(0, 1), chunks=3)
            emptied(("wk", 0, 1))
            norm_heads(work[:, 5120:6144].rearrange("p (n c) -> p n c", c=HD), NT * MH, HD)
            refill("wk", 1)
            refill("wv", 0)
            tq, tk = turned_qk["moba"]
            turned_out("qmoba", [(tq, "qn_moba", True)], units=(0,))
            turned_out("kmoba", [(tk, "kn_moba", True)], units=(0,))

            def rotate(a1, a2, out1, out2, n, spread):
                cs, sn = (const(name).rearrange("p (t c) -> p t c", t=NT) for name in ("cos", "sin"))
                part = [ropes[:, k, :, 0:n, :] for k in range(4)]
                if n > 1:
                    cs, sn = (a.unsqueeze(2).broadcast_to([P, NT, n, 16]) for a in (cs, sn))
                else:
                    part = [a[:, :, 0, :] for a in part]
                for o, a, c in zip(part, (a1, a2, a1, a2), (cs, sn, sn, cs)):
                    ins = dve.tensor_tensor(o, a, c, ALU.mult)
                link(ins)
                if spread:
                    part = [a.unsqueeze(2).broadcast_to([P, NT, MH, 16]) for a in part]
                dve.tensor_tensor(out1, part[0], part[1], ALU.subtract)
                link(dve.tensor_tensor(out2, part[2], part[3], ALU.add))

            def mla_rows(step):
                qh = qm.rearrange("p t (h c) -> p t h c", h=MH)
                kh = km.rearrange("p t (h c) -> p t h c", h=MH)
                rows = [work[:, at:at + 1536].rearrange("p (n c) -> p n c", c=MQK) for at in (0, 1536)]
                if step == 1:
                    emptied(("uq", 1, 1))
                    rotate(qh[:, :, :, 64:80], qh[:, :, :, 80:96], qh[:, :, :, 64:80], qh[:, :, :, 80:96], MH, False)
                if step == 3:
                    emptied(("ukv", 1, 1))
                    rotate(cbuf[:, :, 384:400], cbuf[:, :, 400:416], kh[:, :, :, 64:80], kh[:, :, :, 80:96], 1, True)
                if step in (2, 5):
                    head_squares(rows[step == 5], NT * MH, MQK)
                if step in (3, 6):
                    head_means(NT * MH, MQK)
                if step in (4, 7):
                    head_scale(rows[step == 7], NT * MH, MQK)

            for n, kind in enumerate(("moba", "mla")):
                moba = kind == "moba"
                tq, tk = turned_qk[kind]
                if not moba:
                    turned_out("qmla", [(tq, "qn_mla", True)], width=MQK)
                    turned_out("kmla", [(tk, "kn_mla", True)], width=MQK)
                for i in range(MH + 3):
                    if i < MH:
                        b = filled(("scores", kind, i))
                        dve.tensor_reduce(nmax[:, n, i, 0:1], b[:, 0:P], AX_X, ALU.max, negate=True)
                        dve.tensor_reduce(nmax[:, n, i, 1:2], b[:, P:384], AX_X, ALU.max, negate=True)\
                            .then_inc(max_ready, 1)
                    if 2 <= i < MH + 2:
                        b = filled(("probsT", kind, i - 2))
                        dve.tensor_copy(probsT[:, (i - 2) % 3, :], b[:, 0:384]).then_inc(dve_emptied, 1)
                    if moba:
                        mla_rows(i)
                    if i >= 3 and (i - 3) % 4 == 3:
                        k = (i - 3) // 4
                        b = filled(("soft_out", kind, k))
                        emptied(("scores", kind, 4 * k + 3))
                        link(dve.reciprocal(rden[:, n, 4 * k:4 * k + 4, :], den[:, n, 4 * k:4 * k + 4, :]))
                        at = (512 if moba else 0) + 256 * k
                        dve.tensor_tensor(h[:, :, at:at + 256].rearrange("p t (n d) -> p n t d", d=HD),
                                          b[:, :].rearrange("p (n t d) -> p n t d", n=4, t=NT),
                                          rden[:, n, 4 * k:4 * k + 4, :].unsqueeze(3).broadcast_to([P, 4, NT, HD]),
                                          ALU.mult).then_inc(dve_emptied, 1)
            turned_low("o2", None)
            refill("wv", 1)
            for nb in range(2):
                refill(("w_o", nb), 0)
                for t in range(NT):
                    add_to_x("w_o", nb, nb, t)
                if nb == 0:
                    refill(("w_o", 0), 1)

            def s5_angles():
                tau = 2 * np.pi
                c1 = 6.28125
                c2 = float(np.float32(np.round((tau - c1) * 2 ** 20) / 2 ** 20))
                c3 = float(np.float32(tau - c1 - c2))
                magic = 12582912.0
                lr, li = lam[:, 0, :], lam[:, 1, :]
                dve.wait_ge(dt_ready, 1)
                dve.wait_ge(lam_landed, 48)
                dt = log_dt[:, 1:2]
                dve.tensor_scalar(lam[:, 3, :], lr, dt, None, ALU.mult).then_inc(zr_ready, 1)
                link(dve.tensor_scalar(lam[:, 4, :], li, dt, 0.5, ALU.mult, ALU.mult))
                link(dve.tensor_scalar(lam[:, 10, :], lam[:, 4, :], 0.5 * np.pi, None, ALU.add))
                for a, o in ((lam[:, 4, :], lam[:, 6, :]), (lam[:, 10, :], lam[:, 7, :])):
                    turns = lam[:, 11, :]
                    link(dve.tensor_scalar(turns, a, 1 / tau, magic, ALU.mult, ALU.add))
                    link(dve.tensor_scalar(turns, turns, magic, None, ALU.subtract))
                    link(dve.scalar_tensor_tensor(out=o, in0=turns, scalar=-c1, in1=a, op0=ALU.mult, op1=ALU.add))
                    link(dve.scalar_tensor_tensor(out=o, in0=turns, scalar=-c2, in1=o, op0=ALU.mult, op1=ALU.add))
                    link(dve.scalar_tensor_tensor(out=o, in0=turns, scalar=-c3, in1=o, op0=ALU.mult, op1=ALU.add))
                    ins = dve.tensor_scalar(o, o, 3.1415925, -3.1415925, ALU.min, ALU.max)
                    link(ins)
                dve.tensor_copy(lam[:, 12, :], lam[:, 4, :]).then_inc(angle_ready, 1)

            def s5_powers():
                lr, li = lam[:, 0, :], lam[:, 1, :]
                dve.wait_ge(sin_ready, 1)
                dve.wait_ge(exp_ready, 1)
                e, sn, co = lam[:, 5, :], lam[:, 8, :], lam[:, 9, :]
                s2, es, es2, e1, cosv = (lam[:, n, :] for n in (12, 13, 14, 15, 16))
                link(dve.tensor_tensor(s2, sn, sn, ALU.mult))
                dve.tensor_tensor(es, e, sn, ALU.mult)
                dve.tensor_tensor(es2, e, s2, ALU.mult)
                dve.tensor_scalar(e1, e, -1.0, None, ALU.add)
                link(dve.tensor_scalar(cosv, s2, -2.0, 1.0, ALU.mult, ALU.add))
                re, im = powers[:, 0], powers[:, 1]
                dve.tensor_tensor(re[:, 0, :], e, cosv, ALU.mult)
                dve.scalar_tensor_tensor(out=im[:, 0, :], in0=es, scalar=2.0, in1=co, op0=ALU.mult, op1=ALU.mult)
                num = lam[:, 17, :]
                link(dve.scalar_tensor_tensor(out=num, in0=es2, scalar=-2.0, in1=e1, op0=ALU.mult, op1=ALU.add))
                a, b2, c, d, e2 = (lam[:, n, :] for n in (18, 19, 20, 21, 3))
                dve.tensor_tensor(a, lr, lr, ALU.mult)
                dve.tensor_tensor(b2, li, li, ALU.mult)
                dve.tensor_tensor(c, num, lr, ALU.mult)
                dve.tensor_tensor(d, im[:, 0, :], li, ALU.mult)
                link(dve.tensor_tensor(e2, im[:, 0, :], lr, ALU.mult))
                dve.tensor_tensor(lam[:, 4, :], num, li, ALU.mult)
                dve.tensor_tensor(a, a, b2, ALU.add)
                link(dve.tensor_tensor(c, c, d, ALU.add))
                link(dve.reciprocal(b2, a))
                link(dve.tensor_tensor(e2, e2, lam[:, 4, :], ALU.subtract))
                dve.tensor_tensor(pw[:, 18, 0, :], c, b2, ALU.mult)
                dve.tensor_tensor(pw[:, 18, 1, :], c, b2, ALU.mult)
                dve.tensor_tensor(pw[:, 19, 1, :], e2, b2, ALU.mult)
                for m in (1, 2, 4):
                    ar, ai = re[:, 0:m, :], im[:, 0:m, :]
                    br, bi = (v[:, m - 1:m, :].broadcast_to([G, m, GP]) for v in (re, im))
                    for n, (p1, p2) in enumerate(((ar, br), (ai, bi), (ar, bi), (ai, br))):
                        ins = dve.tensor_tensor(prods[:, n, 0:m, :], p1, p2, ALU.mult)
                    link(ins)
                    dve.tensor_tensor(re[:, m:2 * m, :], prods[:, 0, 0:m, :], prods[:, 1, 0:m, :], ALU.subtract)
                    link(dve.tensor_tensor(im[:, m:2 * m, :], prods[:, 2, 0:m, :], prods[:, 3, 0:m, :], ALU.add))
                dve.tensor_scalar(pw[:, 19, 0, :], pw[:, 19, 1, :], -1.0, None, ALU.mult)
                dve.memset(pw[:, 0, :, :], 1.0)
                dve.memset(pw[:, 9, :, :], 0.0)
                dve.tensor_copy(pw[:, 1:9, 0, :], re)
                dve.tensor_copy(pw[:, 1:9, 1, :], re)
                dve.tensor_scalar(pw[:, 10:18, 0, :], im, -1.0, None, ALU.mult)
                dve.tensor_copy(pw[:, 10:18, 1, :], im).then_inc(powers_ready, 1)

            def s5_inputs():
                sgn = const("sgn")[:, 0:1]
                for k in range(4):
                    b = filled(("bcT", k))
                    dst = (Bs, Cs)[k // 2][:, 8 * (k % 2):8 * (k % 2) + 8, :].rearrange("p i g -> p (i g)")
                    if k < 2:
                        dve.tensor_copy(dst, b[:, :]).then_inc(dve_emptied, 1)
                    else:
                        dve.tensor_scalar(dst, b[:, :], sgn, None, ALU.mult).then_inc(dve_emptied, 1)
                for k in range(4):
                    b = filled(("bcX", k))
                    dst = (Bx, Cx)[k // 2][:, 8 * (k % 2):8 * (k % 2) + 8, :].rearrange("p i g -> p (i g)")
                    dve.tensor_scalar(dst, b[:, :], 1.0 if k < 2 else -1.0, None, ALU.mult).then_inc(dve_emptied, 1)
                emptied(("powT", 2))
                dve.wait_ge(dve_emptied, u.emptied(("bcX", 3)))
                fr, fi = (powT[:, q, :].unsqueeze(1).broadcast_to([P, GI, G]) for q in (18, 19))
                m1, m2, m3 = (v[:, 0:1024].rearrange("p (i g) -> p i g", i=GI) for v in (t1, t2, work[:, 0:1024]))
                dve.tensor_tensor(m1, Bs, fr, ALU.mult)
                dve.tensor_tensor(m2, Bx, fi, ALU.mult)
                link(dve.tensor_tensor(m3, Bs, fi, ALU.mult))
                link(dve.tensor_tensor(Bs, m1, m2, ALU.add))
                link(dve.tensor_tensor(m1, Bx, fr, ALU.mult))
                dve.tensor_tensor(Bx, m1, m3, ALU.subtract).then_inc(inputs_scaled, 1)
                dve.wait_ge(inputs_scaled, 1)
                dve.tensor_copy(a8[:, 0, :], powT[:, 8, :])
                dve.tensor_copy(a8[:, 1, :], powT[:, 17, :])
                dve.tensor_scalar(a8[:, 2, :], powT[:, 17, :], -1.0, None, ALU.mult)

            def s5_inject(f):
                gs = slice(8 * f, 8 * f + 8)
                ar, ai = (powT[:, q:q + 8, gs][:, ::-1, :].rearrange("p q g -> p g q").unsqueeze(3)
                          .broadcast_to([P, 8, L, GI]) for q in (0, 9))
                bs, bx = (v[:, :, gs].rearrange("p i g -> p g i").unsqueeze(2).broadcast_to([P, 8, L, GI])
                          for v in (Bs, Bx))
                m1, m2 = (v[:, 0:1024].rearrange("p (g j i) -> p g j i", g=8, j=L) for v in (t1, t2))
                dve.tensor_tensor(m1, ar, bs, ALU.mult)
                link(dve.tensor_tensor(m2, ai, bx, ALU.mult))
                if f:
                    dve.wait_ge(pe_done, done(("wT", f - 1, 1)))
                dve.tensor_tensor(inject, m1, m2, ALU.add).then_inc(injects_made, 1)
                if f:
                    dve.wait_ge(pe_done, done(("taps", f - 1)))
                dve.wait_ge(pads_zeroed, 1)
                diagonal = work[:, 9856:9856 + 8 * 144].rearrange("p (g n) -> p g n", n=144)[:, :, 0:GI]
                dve.tensor_copy(diagonal, Bs[:, :, gs].rearrange("p i g -> p g i")).then_inc(pads_filled, 1)

            def s5_taps(f):
                b = filled(("taps", f))
                if f:
                    dve.wait_ge(t_stored, 16 * f)
                dve.tensor_tensor(taps.rearrange("p (k g o) -> p k g o", k=L, g=8),
                                  b[:, 0:P].rearrange("p (k o) -> p k o", k=L).unsqueeze(2).broadcast_to([P, L, 8, GI]),
                                  const("bmask").rearrange("p (g o) -> p g o", g=8).unsqueeze(1)
                                  .broadcast_to([P, L, 8, GI]), ALU.mult).then_inc(dve_emptied, 1)

            def mlp(layer, m):
                turned_low(("ffn", layer), f"ffn{layer}")
                refill(("gate", 1) if layer else ("w_o", 1), 1)
                means(m)
                dve.wait_ge(ms_ready, m + 1)
                dve.reciprocal(inv[:, layer, :], ms[:, m, :]).then_inc(inv_ready, 1)
                for i in range(FB + 1):
                    if i:
                        for k in range(2):
                            b = bank(("fT", layer, i - 1, k))
                            dve.wait_ge(high_turned, u.high[("fT", layer, i - 1, k)])
                            lo, hi = (v[:, 2 * k:2 * k + 2, :].rearrange("p c s -> p (c s)") for v in (hidT_lo, hidT_hi))
                            dve.tensor_tensor(lo, b[:, :], hi, ALU.subtract).then_inc(dve_emptied, 1)
                    if i < FB:
                        refill(("f1", layer, i), 0)
                        for t in range(NT):
                            b = bank((("f1", layer, i), 0, t))
                            dve.wait_ge(relu_ready, NT * (FB * layer + i) + t + 1)
                            dve.tensor_tensor(hid[:, t, :], b[:, :], hid[:, t, :], ALU.mult).then_inc(dve_emptied, 1)
                    if layer == 0 and i == 2:
                        s5_inputs()
                    if i < FB:
                        refill(("f1", layer, i), 1)
                    if layer == 0 and i == 0:
                        s5_angles()
                    if layer == 0 and i == 1:
                        s5_powers()
                    if layer == 0 and i == 2:
                        s5_inject(0)
                    if layer == 0:
                        for f in chunks_before(i):
                            s5_taps(f)
                            if f < FB - 1:
                                s5_inject(f + 1)
                    if i and (layer or i < FB):
                        refill(("f2", layer, i - 1), 0)
                    if i and (layer or i < FB - 1):
                        refill(("f2", layer, i - 1), 1)
                    if layer == 0:
                        for f in chunks_after(i):
                            s5_taps(f)
                            s5_inject(f + 1)
                dve.wait_ge(inv_ready, layer + 1)
                for t in range(NT):
                    for nb in range(2):
                        b = filled(("acc", layer, 2 * t + nb))
                        xs = x[:, t, nb * 512:(nb + 1) * 512]
                        dve.scalar_tensor_tensor(out=xs, in0=b[:, :], scalar=inv[:, layer, t:t + 1], in1=xs,
                                                 op0=ALU.mult, op1=ALU.add).then_inc(dve_emptied, 1)

            mlp(0, 3)

            means(4)
            dve.wait_ge(gain_landed, 16)
            dve.tensor_copy(gain_rows[:, 1, :].rearrange("p (j i) -> p j i", j=L),
                            gain_rows[:, 0, 0:GI].unsqueeze(1).broadcast_to([G, L, GI])).then_inc(gain_rows_ready, 1)
            dve.wait_ge(rstd_ready, 4)
            for t in range(NT):
                dve.tensor_scalar(h[:, t, :], x[:, t, :], rstd[:, 4, t:t + 1], None, ALU.mult).then_inc(h_normed, 1)
            dve.wait_ge(chunked[0], 32)
            for n in range(2):
                dve.tensor_copy(xg[:, 16 * n:16 * n + 16].rearrange("p g j i -> p j g i"),
                                xc[0].rearrange("p j (g i) -> p j g i", i=GI)[:, :, 16 * n:16 * n + 16])\
                    .then_inc(regrouped_a, 1)
            b = filled("gain_gi")
            dve.tensor_copy(gain_gi[:, :], b[:, 0:G]).then_inc(dve_emptied, 1)
            dve.wait_ge(dve_emptied, u.emptied("gain_gi"))
            for n in range(4):
                b = filled(("ug", n))
                dve.tensor_tensor(ug[:, 16 * n:16 * n + 16, :], b[:, :].rearrange("p (g c) -> p g c", g=16),
                                  gain_gi[:, 16 * n:16 * n + 16].unsqueeze(2).broadcast_to([P, 16, NC]),
                                  ALU.mult).then_inc(dve_emptied, 1)
            link(dve.memset(states[:, :, 0, :], 0.0))
            emptied(("injectx", 3))
            ar = a8[:, 0:1, :].broadcast_to([P, 2, G])
            for c in range(2, NC):
                before, now = states[:, :, c - 1, :], states[:, :, c, :]
                dve.tensor_tensor(steps[:, 0], ar, before, ALU.mult)
                link(dve.tensor_tensor(steps[:, 1], a8[:, 1:3, :], before[:, ::-1, :], ALU.mult))
                link(dve.tensor_tensor(steps[:, 0], steps[:, 0], steps[:, 1], ALU.add))
                ins = dve.tensor_tensor(now, now, steps[:, 0], ALU.add)
                if c < NC - 1:
                    link(ins)
            ins.then_inc(states_ready, 1)
            for n in range(4):
                b = filled(("fir", n))
                for fl in range(2):
                    f = 2 * n + fl
                    ins = dve.scalar_tensor_tensor(out=ybuf[:, f, :], in0=uT[:, f, :], scalar=gain("d_skip", f),
                                                   in1=b[:, fl * S:(fl + 1) * S], op0=ALU.mult, op1=ALU.add)
                ins.then_inc(dve_emptied, 1)
            for n in range(4):
                b = filled(("state_outT", n))
                dve.wait_ge(dve_emptied, u.emptied(("fir", 2 * (n // 2) + 1)))
                yv = ybuf[:, 4 * (n // 2):4 * (n // 2) + 4, :].rearrange("p c s -> p (c s)")\
                    .rearrange("p (n j) -> p n j", j=L)[:, :, 4 * (n % 2):4 * (n % 2) + 4]
                dve.tensor_tensor(yv, yv, b[:, :].rearrange("p (j n) -> p n j", j=4), ALU.add).then_inc(dve_emptied, 1)
            for n in range(4):
                dve.wait_ge(gelu_high, n + 1)
                dve.tensor_tensor(hT_lo[:, 2 * n:2 * n + 2, :], ybuf[:, 2 * n:2 * n + 2, :], hT_hi[:, 2 * n:2 * n + 2, :],
                                  ALU.subtract).then_inc(gelu_ready, 1)
            refill(("f2", 0, FB - 1), 1)
            for hh in range(2):
                refills(("val", hh))
                refill(("gate", hh), 0)
                for t in range(NT):
                    gate_in((("gate", hh), 0, t), t, hh, bank((("val", hh), 0, t))[:, :], (("val", hh), 0, t))
                if hh == 0:
                    refill(("gate", 0), 1)
            mlp(1, 5)

        @block.gpsimd
        def _(pool):
            pool.memset(half_neg[:, :], -0.5).then_inc(halves_ready, 1)
            pool.dma_start(gain_rows[:, 0, 0:GI], w["mix_norm_g_2"][1].rearrange("(g i) -> g i", i=GI))\
                .then_inc(gain_landed, 16)
            pool.wait_ge(halves_ready, 1)

            def root(m):
                pool.wait_ge(ms_ready, m + 1)
                pool.tensor_tensor(rstd[:, m, :], ms[:, m, :], half_neg[:, 0:NT], ALU.pow).then_inc(rstd_ready, 1)

            def head_root(k, n):
                pool.wait_ge(headms_ready, k)
                pool.tensor_tensor(rsh[:, 0:n], msh[:, 0:n], half_neg[:, 0:n], ALU.pow).then_inc(headr_ready, 1)

            root(0)
            root(1)
            head_root(1, NT * NH)
            head_root(2, NT * NH)
            root(2)
            pool.wait_ge(lowms_ready, 2)
            pool.tensor_tensor(lowr[:, :], lowms[:, :], half_neg[:, 0:4], ALU.pow).then_inc(lowr_ready, 1)
            for k in range(3, 7):
                head_root(k, NT * MH)
            pool.wait_ge(pe_done, done(("soft_out", "mla", 1)))
            pool.wait_ge(ssq_ready, 8)
            for n, (b, c) in enumerate((("b_re_2", "c_re_2"), ("b_im_2", "c_im_2"))):
                pool.dma_start(rawB[:, GP * n:GP * n + GP, :], w[b][0]).then_inc(bc_landed, 16)
                for half in range(2):
                    pool.dma_start(rawC[half][:, :, GP * n:GP * n + GP],
                                   w[c][0][:, 8 * half:8 * half + 8, :]).then_inc(bc_landed, 16)
            pool.dma_start(lam[:, 0, :], w["lam_re_2"][0]).then_inc(lam_landed, 16)
            pool.dma_start(lam[:, 1, :], w["lam_im_2"][0]).then_inc(lam_landed, 16)
            pool.dma_start(log_dt[:, 0:1], w["log_dt_2"][0].rearrange("(g a) -> g a", a=1)).then_inc(lam_landed, 16)
            pool.memset(pads, 0.0).then_inc(pads_zeroed, 1)
            pool.wait_ge(inputs_scaled, 1)
            stored = 0
            for f in range(8):
                gs = slice(8 * f, 8 * f + 8)
                if f:
                    pool.wait_ge(pe_done, done(("taps", f - 1)))
                    pool.wait_ge(v_stored, 16 * f)
                ar, ai = (powT[:, q:q + 9, gs].rearrange("p q g -> p g q").unsqueeze(3)
                          .broadcast_to([P, 8, L + 1, GI]) for q in (0, 9))
                cs, cx = (v[:, :, gs].rearrange("p i g -> p g i").unsqueeze(2).broadcast_to([P, 8, L + 1, GI])
                          for v in (Cs, Cx))
                tmp = t3.rearrange("p (g k o) -> p g k o", g=8, k=L + 1)
                pool.tensor_tensor(readout, ar, cs, ALU.mult).then_inc(pool_step, 1)
                pool.tensor_tensor(tmp, ai, cx, ALU.mult).then_inc(pool_step, 1)
                pool.wait_ge(pool_step, 2 * f + 2)
                pool.tensor_tensor(readout, readout, tmp, ALU.add).then_inc(readouts_made, 1)
                pool.wait_ge(readouts_made, f + 1)
                pool.dma_start(w["scratch_readout"][:, 1024 * f:1024 * f + 1024].rearrange("p (g n) -> p g n", g=8),
                               readout[:, :, 1:L + 1, :].rearrange("p g k o -> p g (k o)")).then_inc(v_stored, 16)
                pool.wait_ge(act_emptied, u.emptied(("wT", f, 1)))
                pool.dma_start(w["scratch_inject"][:, 1024 * f:1024 * f + 1024], inject_T).then_inc(w_stored, 16)
                pool.wait_ge(dve_emptied, u.emptied(("taps", f)))
                pool.dma_start(w["scratch_taps"][:, 1024 * f:1024 * f + 1024], taps).then_inc(t_stored, 16)
            root(4)
            for g in (2 * order[("val", 0)], 2 * order[("val", 0)] + 1):
                name, cols, at = half_of(g)
                pool.wait_ge(high_made, g + 1)
                pool.tensor_tensor(wlo[at], ring[:, slot[name], cols], whi[at], ALU.subtract).then_inc(low_made, 1)


_INS = ["x", "p", "a_w_in", "a_w_group", "a_w_out", "w_kv", "b_w_in", "b_w_out", "ple_w", "ple_gate_w", "mix_norm_g_2",
        "w_in_2", "w_uq_2", "w_ukv_2", "w_o_2", "lam_re_2", "lam_im_2", "log_dt_2", "b_re_2", "b_im_2", "c_re_2",
        "c_im_2", "w_glu_2", "w_ff1_2", "w_ff2_2"]


def kernel(**inputs):
    import numpy as np
    import concourse.bacc as bacc
    from concourse.bass_utils import run_bass_kernel_spmd

    vecs = np.zeros((NVEC, P), np.float32)
    for name, v in (("a_norm", inputs["a_norm"][0]), ("a_scale", inputs["a_scale"][0]), ("kv_norm", inputs["kv_norm"]),
                    ("b_norm", inputs["b_norm"][0]), ("mix0", inputs["mix_norm_g_2"][0]),
                    ("mix1", inputs["mix_norm_g_2"][1]), ("ffn0", inputs["ffn_norm_g_2"][0]),
                    ("ffn1", inputs["ffn_norm_g_2"][1]), ("d_skip", inputs["d_skip_2"][0]),
                    ("g_cq", inputs["g_cq_2"][0]), ("g_ckv", inputs["g_ckv_2"][0]), ("k_norm", inputs["k_norm"]),
                    ("q_norm", inputs["b_q_norm"][0]), ("qn_mla", inputs["g_qn_mla_2"][0]),
                    ("kn_mla", inputs["g_kn_mla_2"][0]), ("qn_moba", inputs["g_qn_moba_2"][0]),
                    ("kn_moba", inputs["g_kn_moba_2"][0])):
        v = np.asarray(v)
        if v.size == HD:
            v = np.concatenate([v, v])
        if v.size % P:
            v = np.concatenate([v, np.zeros(-v.size % P, np.float32)])
        vecs[VEC_AT[name]:VEC_AT[name] + VEC_ROWS[name]] = v.reshape(-1, P)
    tables, pools = constants()

    nc = bacc.Bacc("TRN2", target_bir_lowering=False, num_devices=1)
    arrays, w = {}, {}
    given = {name: np.ascontiguousarray(inputs[name]) for name in _INS}
    for name, a in {**given, "vecs": vecs, "tables": tables, "pools": pools}.items():
        arrays[f"in_{name}"] = a
        w[name] = nc.dram_tensor(f"in_{name}", a.shape, mybir.dt.from_np(a.dtype), kind="ExternalInput").ap()
    for name in ("inject", "readout", "taps"):
        w["scratch_" + name] = nc.dram_tensor("scratch_" + name, (P, 2 * BLK), F32, kind="Internal").ap()
    out = nc.dram_tensor("out_0", (1, S, D), F32, kind="ExternalOutput").ap()
    program(nc, w, out)
    r = run_bass_kernel_spmd(nc, [arrays], core_ids=[0])
    return r.results[0]["out_0"]
```
